# Optimizing a Trainium2 kernel written in Bass

```python
import math
import jax, jax.numpy as jnp
from jax import lax
import numpy as np

D_MODEL = 1024
BATCH = 1
SEQ = 256
DEPTH = 2

CTX_LEN = 256
GRID_W = 64
N_MIXERS = 4
Q_BLOCK = 128
ROPE_THETA = 10000.0
NORM_EPS = 1e-6
N_MOD = 9
D_FF = 2816
NEG_INF = -1e30

DA_QK_DIM = 64
DA_HEADS = D_MODEL // (2 * DA_QK_DIM)
DA_V_DIM = 2 * DA_QK_DIM
DA_QKV = 2 * DA_HEADS * 2 * DA_QK_DIM + DA_HEADS * DA_V_DIM
GA_HEAD_DIM = 128
GA_HEADS = D_MODEL // GA_HEAD_DIM
GA_KV_HEADS = 2
MLA_HEADS = 16
MLA_Q_RANK = 256
MLA_KV_RANK = 128
MLA_NOPE_DIM = 64
MLA_ROPE_DIM = 32
MLA_V_DIM = 64
SWA_HEAD_DIM = 64
SWA_HEADS = D_MODEL // SWA_HEAD_DIM
SWA_KV_HEADS = 2
WINDOW = 128
BAND = Q_BLOCK + 2 * WINDOW


def rmsnorm(x, g):
    xf = x.astype(jnp.float32)
    y = xf * lax.rsqrt(jnp.mean(xf * xf, axis=-1, keepdims=True) + NORM_EPS)
    return (y * g.astype(jnp.float32)).astype(x.dtype)

def axial_rope_tables(seq_len, rot_dim):
    rows = seq_len // GRID_W
    row = jnp.repeat(jnp.arange(rows, dtype=jnp.int32), GRID_W).astype(jnp.float32)
    col = jnp.tile(jnp.arange(GRID_W, dtype=jnp.int32), rows).astype(jnp.float32)
    n_axis = rot_dim // 4
    freqs = ROPE_THETA ** (-jnp.arange(n_axis, dtype=jnp.float32) / n_axis)
    ang = jnp.concatenate([row[:, None] * freqs, col[:, None] * freqs], axis=-1)
    return jnp.cos(ang), jnp.sin(ang)

def apply_rope(x, cos, sin):
    seq, half = cos.shape
    bshape = (seq,) + (1,) * (x.ndim - 3) + (half,)
    cs = cos.reshape(bshape).astype(x.dtype)
    sn = sin.reshape(bshape).astype(x.dtype)
    xp = x.reshape(x.shape[:-1] + (half, 2))
    x0, x1 = xp[..., 0], xp[..., 1]
    return jnp.stack([x0 * cs - x1 * sn, x0 * sn + x1 * cs], axis=-1).reshape(x.shape)

def sweep_query_blocks(fn, *qs):
    b, s = qs[0].shape[:2]
    nblk = s // Q_BLOCK
    blocks = tuple(jnp.moveaxis(q.reshape((b, nblk, Q_BLOCK) + q.shape[2:]), 1, 0) for q in qs)
    out = lax.map(lambda args: fn(*args), (jnp.arange(nblk),) + blocks)
    return jnp.moveaxis(out, 0, 1).reshape((b, s) + out.shape[3:])

def grouped_attend(q, k, v, scale):
    s = jnp.einsum('blhgd,bkhd->bhglk', q, k, preferred_element_type=jnp.float32) * scale
    p = jax.nn.softmax(s, axis=-1)
    o = jnp.einsum('bhglk,bkhd->blhgd', p.astype(v.dtype), v)
    return o.reshape(o.shape[:2] + (-1,))

def swiglu(h, w_in, w_out):
    gate, up = jnp.split(h @ w_in, 2, axis=-1)
    return (jax.nn.silu(gate) * up) @ w_out

def adaln(cond, w, b):
    m = jax.nn.silu(cond) @ w + b
    return m.reshape(m.shape[:-1] + (N_MOD, D_MODEL))

def modulated_norm(h, g, m, k):
    return rmsnorm(h, g) * (1.0 + m[..., k + 1, :]) + m[..., k, :]

def gated_residual(h, y, g, m, k, weight):
    return h + weight * m[..., k + 2, :] * rmsnorm(y, g)

def half_ffn(h, m, k, g_pre, g_post, w_in, w_out):
    y = swiglu(modulated_norm(h, g_pre, m, k), w_in, w_out)
    return gated_residual(h, y, g_post, m, k, 0.5)

def diff_attention_mixer(h, hc, w_in, lam, subln, w_out, lambda_init, ctx_out):
    b, s, _ = h.shape
    cos, sin = axial_rope_tables(s, DA_QK_DIM)

    def project(t):
        n = t.shape[1]
        q, k, v = jnp.split(t @ w_in, [DA_HEADS * 2 * DA_QK_DIM, 2 * DA_HEADS * 2 * DA_QK_DIM], axis=-1)
        return (q.reshape(b, n, DA_HEADS, 2, DA_QK_DIM), k.reshape(b, n, DA_HEADS, 2, DA_QK_DIM),
                v.reshape(b, n, DA_HEADS, DA_V_DIM))

    q, k, v = project(h)
    qc, kc, vc = project(hc)
    q, k = apply_rope(q, cos, sin), apply_rope(k, cos, sin)
    lf = lam.astype(jnp.float32)
    lam_full = jnp.exp(jnp.sum(lf[0] * lf[1])) - jnp.exp(jnp.sum(lf[2] * lf[3])) + lambda_init
    scale = DA_QK_DIM ** -0.5

    def attend(qb, kb, vb):
        sc = jnp.einsum('blhid,bkhid->bihlk', qb, kb, preferred_element_type=jnp.float32) * scale
        p = jax.nn.softmax(sc, axis=-1)
        p = p[:, 0] - lam_full * p[:, 1]
        o = jnp.einsum('bhlk,bkhd->blhd', p.astype(vb.dtype), vb)
        o = rmsnorm(o, subln) * (1.0 - lambda_init)
        return o.reshape(o.shape[0], o.shape[1], DA_HEADS * DA_V_DIM)

    k_all = jnp.concatenate([kc, k], axis=1)
    v_all = jnp.concatenate([vc, v], axis=1)
    y = sweep_query_blocks(lambda i, qb: attend(qb, k_all, v_all), q) @ w_out
    yc = attend(qc, kc, vc) @ w_out if ctx_out else None
    return y, yc

def gqa_axial_mixer(h, hc, w_in, q_norm, k_norm, w_out, ctx_out):
    b, s, _ = h.shape
    cos, sin = axial_rope_tables(s, GA_HEAD_DIM)
    grp = GA_HEADS // GA_KV_HEADS

    def project(t):
        n = t.shape[1]
        q, k, v = jnp.split(t @ w_in, [GA_HEADS * GA_HEAD_DIM, (GA_HEADS + GA_KV_HEADS) * GA_HEAD_DIM], axis=-1)
        q = rmsnorm(q.reshape(b, n, GA_KV_HEADS, grp, GA_HEAD_DIM), q_norm)
        k = rmsnorm(k.reshape(b, n, GA_KV_HEADS, GA_HEAD_DIM), k_norm)
        return q, k, v.reshape(b, n, GA_KV_HEADS, GA_HEAD_DIM)

    q, k, v = project(h)
    qc, kc, vc = project(hc)
    q, k = apply_rope(q, cos, sin), apply_rope(k, cos, sin)
    scale = GA_HEAD_DIM ** -0.5
    k_all = jnp.concatenate([kc, k], axis=1)
    v_all = jnp.concatenate([vc, v], axis=1)
    y = sweep_query_blocks(lambda i, qb: grouped_attend(qb, k_all, v_all, scale), q) @ w_out
    yc = grouped_attend(qc, kc, vc, scale) @ w_out if ctx_out else None
    return y, yc

def mla_mixer(h, hc, w_in, q_norm, kv_norm, w_uq, w_ukv, w_out, ctx_out):
    b, s, _ = h.shape
    cos, sin = axial_rope_tables(s, MLA_ROPE_DIM)

    def project(t):
        n = t.shape[1]
        cq, ckv, kr = jnp.split(t @ w_in, [MLA_Q_RANK, MLA_Q_RANK + MLA_KV_RANK], axis=-1)
        q = (rmsnorm(cq, q_norm) @ w_uq).reshape(b, n, MLA_HEADS, MLA_NOPE_DIM + MLA_ROPE_DIM)
        kv = (rmsnorm(ckv, kv_norm) @ w_ukv).reshape(b, n, MLA_HEADS, MLA_NOPE_DIM + MLA_V_DIM)
        qn, qr = jnp.split(q, [MLA_NOPE_DIM], axis=-1)
        kn, v = jnp.split(kv, [MLA_NOPE_DIM], axis=-1)
        return qn, qr, kn, kr, v

    qn, qr, kn, kr, v = project(h)
    qnc, qrc, knc, krc, vc = project(hc)
    qr, kr = apply_rope(qr, cos, sin), apply_rope(kr, cos, sin)
    scale = (MLA_NOPE_DIM + MLA_ROPE_DIM) ** -0.5

    def attend(qnb, qrb, knb, krb, vb):
        sc = (jnp.einsum('blhd,bkhd->bhlk', qnb, knb, preferred_element_type=jnp.float32)
              + jnp.einsum('blhd,bkd->bhlk', qrb, krb, preferred_element_type=jnp.float32)) * scale
        p = jax.nn.softmax(sc, axis=-1)
        o = jnp.einsum('bhlk,bkhd->blhd', p.astype(vb.dtype), vb)
        return o.reshape(o.shape[0], o.shape[1], MLA_HEADS * MLA_V_DIM)

    kn_all = jnp.concatenate([knc, kn], axis=1)
    kr_all = jnp.concatenate([krc, kr], axis=1)
    v_all = jnp.concatenate([vc, v], axis=1)
    y = sweep_query_blocks(lambda i, a, r: attend(a, r, kn_all, kr_all, v_all), qn, qr) @ w_out
    yc = attend(qnc, qrc, knc, krc, vc) @ w_out if ctx_out else None
    return y, yc

def window_sink_mixer(h, hc, w_in, sink, w_out, ctx_out):
    b, s, _ = h.shape
    cos, sin = axial_rope_tables(s, SWA_HEAD_DIM)
    grp = SWA_HEADS // SWA_KV_HEADS

    def project(t):
        n = t.shape[1]
        q, k, v = jnp.split(t @ w_in, [SWA_HEADS * SWA_HEAD_DIM, (SWA_HEADS + SWA_KV_HEADS) * SWA_HEAD_DIM], axis=-1)
        return (q.reshape(b, n, SWA_KV_HEADS, grp, SWA_HEAD_DIM), k.reshape(b, n, SWA_KV_HEADS, SWA_HEAD_DIM),
                v.reshape(b, n, SWA_KV_HEADS, SWA_HEAD_DIM))

    q, k, v = project(h)
    qc, kc, vc = project(hc)
    q, k = apply_rope(q, cos, sin), apply_rope(k, cos, sin)
    scale = SWA_HEAD_DIM ** -0.5
    sink_l = sink.astype(jnp.float32).reshape(SWA_KV_HEADS, grp)[None, :, :, None, None]

    def sink_softmax_mix(sc, vals):
        sc = jnp.concatenate([sc, jnp.broadcast_to(sink_l, sc.shape[:-1] + (1,))], axis=-1)
        p = jax.nn.softmax(sc, axis=-1)[..., :-1]
        o = jnp.einsum('bhglk,bkhd->blhgd', p.astype(vals.dtype), vals)
        return o.reshape(o.shape[:2] + (-1,))

    pad = ((0, 0), (WINDOW, WINDOW), (0, 0), (0, 0))
    k_pad, v_pad = jnp.pad(k, pad), jnp.pad(v, pad)

    def latent_block(i, qb):
        start = i * Q_BLOCK
        kb = lax.dynamic_slice_in_dim(k_pad, start, BAND, axis=1)
        vb = lax.dynamic_slice_in_dim(v_pad, start, BAND, axis=1)
        qpos = start + jnp.arange(Q_BLOCK)
        kpos = start - WINDOW + jnp.arange(BAND)
        allowed = (kpos[None, :] >= 0) & (kpos[None, :] < s) & (jnp.abs(qpos[:, None] - kpos[None, :]) <= WINDOW)
        s_band = jnp.einsum('blhgd,bkhd->bhglk', qb, kb, preferred_element_type=jnp.float32) * scale
        s_band = jnp.where(allowed, s_band, NEG_INF)
        s_ctx = jnp.einsum('blhgd,bkhd->bhglk', qb, kc, preferred_element_type=jnp.float32) * scale
        return sink_softmax_mix(jnp.concatenate([s_ctx, s_band], axis=-1), jnp.concatenate([vc, vb], axis=1))

    y = sweep_query_blocks(latent_block, q) @ w_out
    yc = None
    if ctx_out:
        s_cc = jnp.einsum('blhgd,bkhd->bhglk', qc, kc, preferred_element_type=jnp.float32) * scale
        yc = sink_softmax_mix(s_cc, vc) @ w_out
    return y, yc

def first_inputs(seed: int = 0) -> dict:
    key = jax.random.key(seed)
    ks = iter(jax.random.split(key, 32))
    f32 = jnp.float32

    def nrm(shape, scale=1.0):
        return jax.random.normal(next(ks), shape, f32) * scale

    def w(shape, fan_in):
        return nrm(shape, fan_in ** -0.5)

    def gain(shape):
        return 1.0 + nrm(shape, 0.02)

    n0, n1, n2, n3 = [len(range(k, DEPTH, N_MIXERS)) for k in range(N_MIXERS)]
    return {
        "x": nrm((BATCH, SEQ, D_MODEL)),
        "c": nrm((BATCH, D_MODEL)),
        "ctx": nrm((BATCH, CTX_LEN, D_MODEL)),
        "c_ctx": nrm((D_MODEL,)),
        "ada_w": w((DEPTH, D_MODEL, N_MOD * D_MODEL), D_MODEL),
        "ada_b": nrm((DEPTH, N_MOD * D_MODEL), 0.02),
        "norm_g": gain((DEPTH, 6, D_MODEL)),
        "ffn_w_in": w((DEPTH, 2, D_MODEL, 2 * D_FF), D_MODEL),
        "ffn_w_out": w((DEPTH, 2, D_FF, D_MODEL), D_FF),
        "da_w_in": w((n0, D_MODEL, DA_QKV), D_MODEL),
        "da_lambda": nrm((n0, 4, DA_QK_DIM), 0.1),
        "da_subln": gain((n0, DA_V_DIM)),
        "da_w_out": w((n0, DA_HEADS * DA_V_DIM, D_MODEL), DA_HEADS * DA_V_DIM),
        "ga_w_in": w((n1, D_MODEL, (GA_HEADS + 2 * GA_KV_HEADS) * GA_HEAD_DIM), D_MODEL),
        "ga_q_norm": gain((n1, GA_HEAD_DIM)),
        "ga_k_norm": gain((n1, GA_HEAD_DIM)),
        "ga_w_out": w((n1, GA_HEADS * GA_HEAD_DIM, D_MODEL), GA_HEADS * GA_HEAD_DIM),
        "mla_w_in": w((n2, D_MODEL, MLA_Q_RANK + MLA_KV_RANK + MLA_ROPE_DIM), D_MODEL),
        "mla_q_norm": gain((n2, MLA_Q_RANK)),
        "mla_kv_norm": gain((n2, MLA_KV_RANK)),
        "mla_w_uq": w((n2, MLA_Q_RANK, MLA_HEADS * (MLA_NOPE_DIM + MLA_ROPE_DIM)), MLA_Q_RANK),
        "mla_w_ukv": w((n2, MLA_KV_RANK, MLA_HEADS * (MLA_NOPE_DIM + MLA_V_DIM)), MLA_KV_RANK),
        "mla_w_out": w((n2, MLA_HEADS * MLA_V_DIM, D_MODEL), MLA_HEADS * MLA_V_DIM),
        "swa_w_in": w((n3, D_MODEL, (SWA_HEADS + 2 * SWA_KV_HEADS) * SWA_HEAD_DIM), D_MODEL),
        "swa_sink": nrm((n3, SWA_HEADS), 0.5),
        "swa_w_out": w((n3, SWA_HEADS * SWA_HEAD_DIM, D_MODEL), SWA_HEADS * SWA_HEAD_DIM),
    }

def first_block(x, c, ctx, c_ctx, ada_w, ada_b, norm_g, ffn_w_in, ffn_w_out,
              da_w_in, da_lambda, da_subln, da_w_out,
              ga_w_in, ga_q_norm, ga_k_norm, ga_w_out,
              mla_w_in, mla_q_norm, mla_kv_norm, mla_w_uq, mla_w_ukv, mla_w_out,
              swa_w_in, swa_sink, swa_w_out):
    h, hc = x, ctx
    for i in range(DEPTH):
        kind, occ = i % N_MIXERS, i // N_MIXERS
        ctx_out = i < DEPTH - 1
        m = adaln(c, ada_w[i], ada_b[i])[:, None]
        mc = adaln(c_ctx, ada_w[i], ada_b[i])[None]
        g = norm_g[i]
        h = half_ffn(h, m, 0, g[0], g[1], ffn_w_in[i, 0], ffn_w_out[i, 0])
        hc = half_ffn(hc, mc, 0, g[0], g[1], ffn_w_in[i, 0], ffn_w_out[i, 0])
        u = modulated_norm(h, g[2], m, 3)
        uc = modulated_norm(hc, g[2], mc, 3)
        if kind == 0:
            lambda_init = 0.8 - 0.6 * math.exp(-0.3 * i)
            y, yc = diff_attention_mixer(u, uc, da_w_in[occ], da_lambda[occ], da_subln[occ], da_w_out[occ],
                                         lambda_init, ctx_out)
        elif kind == 1:
            y, yc = gqa_axial_mixer(u, uc, ga_w_in[occ], ga_q_norm[occ], ga_k_norm[occ], ga_w_out[occ], ctx_out)
        elif kind == 2:
            y, yc = mla_mixer(u, uc, mla_w_in[occ], mla_q_norm[occ], mla_kv_norm[occ], mla_w_uq[occ],
                              mla_w_ukv[occ], mla_w_out[occ], ctx_out)
        else:
            y, yc = window_sink_mixer(u, uc, swa_w_in[occ], swa_sink[occ], swa_w_out[occ], ctx_out)
        h = gated_residual(h, y, g[3], m, 3, 1.0)
        h = half_ffn(h, m, 6, g[4], g[5], ffn_w_in[i, 1], ffn_w_out[i, 1])
        if ctx_out:
            hc = gated_residual(hc, yc, g[3], mc, 3, 1.0)
            hc = half_ffn(hc, mc, 6, g[4], g[5], ffn_w_in[i, 1], ffn_w_out[i, 1])
    return h


DEPTH_2 = 1

HEAD_DIM = 64
DSA_GROUPS = ((128, 1), (512, 4), (2048, 16))
DSA_HEADS_PER_GROUP = 4
DSA_HEADS = DSA_HEADS_PER_GROUP * len(DSA_GROUPS)
MOBA_HEADS = 8
MOBA_BLOCK = 256
MOBA_TOPK = 3
MOBA_Q_CHUNK = 64
D_FF_2 = ((8 * D_MODEL // 3 + 127) // 128) * 128
DSA_WIDTH = DSA_HEADS * HEAD_DIM
MOBA_WIDTH = MOBA_HEADS * HEAD_DIM
DSA_OUT = DSA_HEADS_PER_GROUP * HEAD_DIM
IN_WIDTH = 3 * DSA_WIDTH + 3 * MOBA_WIDTH + 2 * D_MODEL
EPS = 1e-6
NEG = -1e30


f32 = jnp.float32

def rmsnorm_2(x, g):
    xf = x.astype(f32)
    y = xf * lax.rsqrt(jnp.mean(xf * xf, axis=-1, keepdims=True) + EPS)
    return (y * g.astype(f32)).astype(x.dtype)

def swiglu_2(x, w_gate, w_up, w_down):
    return (jax.nn.silu(x @ w_gate) * (x @ w_up)) @ w_down

def alibi_slopes(n):
    return 2.0 ** (-8.0 * jnp.arange(1, n + 1, dtype=f32) / n)

def to_heads(a, n):
    b, s, _ = a.shape
    return a.reshape(b, s, n, HEAD_DIM).transpose(0, 2, 1, 3)

def dilated_window_attention(q, k, v, slopes, window, dilation):
    b, h, s, hd = q.shape
    blk = window // dilation
    L = s // dilation
    Lp = -(-L // blk) * blk
    nb = Lp // blk

    def to_residue(a):
        a = a.reshape(b, h, L, dilation, hd).transpose(0, 1, 3, 2, 4)
        return jnp.pad(a, ((0, 0), (0, 0), (0, 0), (0, Lp - L), (0, 0)))

    qr, kr, vr = to_residue(q), to_residue(k), to_residue(v)
    qb = qr.reshape(b, h, dilation, nb, blk, hd)

    def band(a):
        ap = jnp.pad(a, ((0, 0), (0, 0), (0, 0), (blk, 0), (0, 0)))
        prev = ap[:, :, :, :Lp].reshape(b, h, dilation, nb, blk, hd)
        cur = a.reshape(b, h, dilation, nb, blk, hd)
        return jnp.concatenate([prev, cur], axis=4)

    kb, vb = band(kr), band(vr)
    scores = jnp.einsum('bhrnqd,bhrnkd->bhrnqk', qb, kb).astype(f32)
    qi = jnp.arange(blk)[:, None]
    kj = jnp.arange(2 * blk)[None, :]
    delta = qi + blk - kj
    kpos = jnp.arange(nb)[:, None, None] * blk - blk + kj[None]
    valid = (delta >= 0)[None] & (delta <= blk)[None] & (kpos >= 0)
    bias = -slopes[:, None, None] * (delta * dilation).astype(f32)[None]
    scores = jnp.where(valid[None, None, None], scores + bias[None, :, None, None], NEG)
    lse = jax.nn.logsumexp(scores, axis=-1)
    p = jnp.exp(scores - lse[..., None]).astype(v.dtype)
    out = jnp.einsum('bhrnqk,bhrnkd->bhrnqd', p, vb)
    out = out.reshape(b, h, dilation, Lp, hd)[:, :, :, :L]
    out = out.transpose(0, 1, 3, 2, 4).reshape(b, h, s, hd)
    lse = lse.reshape(b, h, dilation, Lp)[..., :L].transpose(0, 1, 3, 2).reshape(b, h, s)
    return out, lse

def moba_attention(q, k, v, slopes):
    b, h, s, hd = q.shape
    nblk = -(-s // MOBA_BLOCK)
    sp = nblk * MOBA_BLOCK
    n_sel = min(MOBA_TOPK, nblk)
    padw = ((0, 0), (0, 0), (0, sp - s), (0, 0))
    q, k, v = jnp.pad(q, padw), jnp.pad(k, padw), jnp.pad(v, padw)
    bh = b * h
    kblk = k.reshape(bh, nblk, MOBA_BLOCK, hd)
    vblk = v.reshape(bh, nblk, MOBA_BLOCK, hd)
    qf = q.reshape(bh, sp, hd)
    kmean = jnp.mean(kblk.astype(f32), axis=2)
    gate = jnp.einsum('xtd,xnd->xtn', qf.astype(f32), kmean)
    own = jnp.arange(sp) // MOBA_BLOCK
    past = jnp.arange(nblk)[None, :] < own[:, None]
    gate = jnp.where(past[None], gate, NEG)
    _, sel = lax.top_k(gate, n_sel)
    slope_x = jnp.tile(slopes, b)
    nq = sp // MOBA_Q_CHUNK
    q_chunks = qf.reshape(bh, nq, MOBA_Q_CHUNK, hd).transpose(1, 0, 2, 3)
    sel_chunks = sel.reshape(bh, nq, MOBA_Q_CHUNK, n_sel).transpose(1, 0, 2, 3)
    take = jax.vmap(lambda blocks, ix: blocks[ix])
    blk_off = jnp.arange(MOBA_BLOCK)

    def chunk(args):
        qc, ix, c = args
        t = c * MOBA_Q_CHUNK + jnp.arange(MOBA_Q_CHUNK)
        own_blk = (c * MOBA_Q_CHUNK) // MOBA_BLOCK
        k_own = lax.dynamic_index_in_dim(kblk, own_blk, axis=1, keepdims=False)
        v_own = lax.dynamic_index_in_dim(vblk, own_blk, axis=1, keepdims=False)
        d_own = t[:, None] - (own_blk * MOBA_BLOCK + blk_off)[None, :]
        s_own = jnp.einsum('xqd,xkd->xqk', qc, k_own).astype(f32)
        s_own = jnp.where(d_own[None] >= 0,
                          s_own - slope_x[:, None, None] * d_own.astype(f32)[None], NEG)
        k_sel = take(kblk, ix)
        v_sel = take(vblk, ix)
        s_sel = jnp.einsum('xqd,xqjkd->xqjk', qc, k_sel).astype(f32)
        d_sel = t[None, :, None, None] - (ix[..., None] * MOBA_BLOCK + blk_off)
        ok = (ix < own_blk)[..., None]
        s_sel = jnp.where(ok, s_sel - slope_x[:, None, None, None] * d_sel.astype(f32), NEG)
        n_k = n_sel * MOBA_BLOCK
        scores = jnp.concatenate([s_sel.reshape(bh, MOBA_Q_CHUNK, n_k), s_own], axis=-1)
        p = jax.nn.softmax(scores, axis=-1).astype(v.dtype)
        p_sel = p[..., :n_k].reshape(bh, MOBA_Q_CHUNK, n_sel, MOBA_BLOCK)
        p_own = p[..., n_k:]
        return (jnp.einsum('xqjk,xqjkd->xqd', p_sel, v_sel)
                + jnp.einsum('xqk,xkd->xqd', p_own, v_own))

    out = lax.map(chunk, (q_chunks, sel_chunks, jnp.arange(nq)))
    return out.transpose(1, 0, 2, 3).reshape(b, h, sp, hd)[:, :, :s]

def hybrid_layer(x, norm_ffn1, ffn1_gate, ffn1_up, ffn1_down, norm_mix, w_in,
                 w_up_a, w_up_b, w_out, norm_ffn2, ffn2_gate, ffn2_up, ffn2_down):
    b, s, _ = x.shape
    x = x + 0.5 * swiglu_2(rmsnorm_2(x, norm_ffn1), ffn1_gate, ffn1_up, ffn1_down)
    h = rmsnorm_2(x, norm_mix)
    proj = h @ w_in
    o = 0
    parts = []
    for width in (DSA_WIDTH, DSA_WIDTH, DSA_WIDTH, MOBA_WIDTH, MOBA_WIDTH, MOBA_WIDTH,
                  D_MODEL, D_MODEL):
        parts.append(proj[..., o:o + width])
        o += width
    qa, ka, va, qb, kb, vb, g_a, g_b = parts
    scale = HEAD_DIM ** -0.5
    qa, ka, va = to_heads(qa, DSA_HEADS) * scale, to_heads(ka, DSA_HEADS), to_heads(va, DSA_HEADS)
    qb, kb, vb = to_heads(qb, MOBA_HEADS) * scale, to_heads(kb, MOBA_HEADS), to_heads(vb, MOBA_HEADS)

    slopes_a = alibi_slopes(DSA_HEADS)
    outs, lses = [], []
    for gi, (window, dilation) in enumerate(DSA_GROUPS):
        hs = slice(gi * DSA_HEADS_PER_GROUP, (gi + 1) * DSA_HEADS_PER_GROUP)
        og, lg = dilated_window_attention(qa[:, hs], ka[:, hs], va[:, hs], slopes_a[hs],
                                          window, dilation)
        outs.append(og)
        lses.append(lg)
    w_grp = jax.nn.softmax(jnp.stack(lses, 0), axis=0)
    y_a = jnp.sum(w_grp[..., None] * jnp.stack(outs, 0).astype(f32), axis=0).astype(x.dtype)
    y_a = y_a.transpose(0, 2, 1, 3).reshape(b, s, DSA_OUT)

    y_b = moba_attention(qb, kb, vb, alibi_slopes(MOBA_HEADS))
    y_b = y_b.transpose(0, 2, 1, 3).reshape(b, s, MOBA_WIDTH)

    merged = jax.nn.sigmoid(g_a) * (y_a @ w_up_a) + jax.nn.sigmoid(g_b) * (y_b @ w_up_b)
    x = x + merged @ w_out
    x = x + 0.5 * swiglu_2(rmsnorm_2(x, norm_ffn2), ffn2_gate, ffn2_up, ffn2_down)
    return x

def second_inputs(seed: int = 0) -> dict:
    key = jax.random.key(seed)
    ks = jax.random.split(key, 16)

    def dense(k, fan_in, fan_out):
        return jax.random.normal(k, (DEPTH_2, fan_in, fan_out), f32) * fan_in ** -0.5

    def gain(k):
        return 1.0 + 0.02 * jax.random.normal(k, (DEPTH_2, D_MODEL), f32)

    return {
        "x": jax.random.normal(ks[0], (BATCH, SEQ, D_MODEL), f32),
        "norm_ffn1": gain(ks[1]),
        "ffn1_gate": dense(ks[2], D_MODEL, D_FF_2),
        "ffn1_up": dense(ks[3], D_MODEL, D_FF_2),
        "ffn1_down": dense(ks[4], D_FF_2, D_MODEL),
        "norm_mix": gain(ks[5]),
        "w_in": dense(ks[6], D_MODEL, IN_WIDTH),
        "w_up_a": dense(ks[7], DSA_OUT, D_MODEL),
        "w_up_b": dense(ks[8], MOBA_WIDTH, D_MODEL),
        "w_out": dense(ks[9], D_MODEL, D_MODEL),
        "norm_ffn2": gain(ks[10]),
        "ffn2_gate": dense(ks[11], D_MODEL, D_FF_2),
        "ffn2_up": dense(ks[12], D_MODEL, D_FF_2),
        "ffn2_down": dense(ks[13], D_FF_2, D_MODEL),
        "norm_final": 1.0 + 0.02 * jax.random.normal(ks[14], (D_MODEL,), f32),
    }

def second_block(x, norm_ffn1, ffn1_gate, ffn1_up, ffn1_down, norm_mix, w_in, w_up_a,
              w_up_b, w_out, norm_ffn2, ffn2_gate, ffn2_up, ffn2_down, norm_final):
    for layer in range(DEPTH_2):
        x = hybrid_layer(x, norm_ffn1[layer], ffn1_gate[layer], ffn1_up[layer],
                         ffn1_down[layer], norm_mix[layer], w_in[layer], w_up_a[layer],
                         w_up_b[layer], w_out[layer], norm_ffn2[layer], ffn2_gate[layer],
                         ffn2_up[layer], ffn2_down[layer])
    return rmsnorm_2(x, norm_final)


def setup_inputs(seed=0):
    out = dict(first_inputs(seed))
    for name, value in second_inputs(seed + 1).items():
        if name != "x":
            out[name + "_2"] = value
    return out


def reference(
    x, c, ctx, c_ctx, ada_w, ada_b, norm_g, ffn_w_in, ffn_w_out, da_w_in, da_lambda, da_subln,
    da_w_out, ga_w_in, ga_q_norm, ga_k_norm, ga_w_out, mla_w_in, mla_q_norm, mla_kv_norm,
    mla_w_uq, mla_w_ukv, mla_w_out, swa_w_in, swa_sink, swa_w_out, norm_ffn1_2, ffn1_gate_2,
    ffn1_up_2, ffn1_down_2, norm_mix_2, w_in_2, w_up_a_2, w_up_b_2, w_out_2, norm_ffn2_2,
    ffn2_gate_2, ffn2_up_2, ffn2_down_2, norm_final_2,
):
    x = first_block(
        x, c, ctx, c_ctx, ada_w, ada_b, norm_g, ffn_w_in, ffn_w_out, da_w_in, da_lambda,
        da_subln, da_w_out, ga_w_in, ga_q_norm, ga_k_norm, ga_w_out, mla_w_in, mla_q_norm,
        mla_kv_norm, mla_w_uq, mla_w_ukv, mla_w_out, swa_w_in, swa_sink, swa_w_out,
    )
    return second_block(
        x, norm_ffn1_2, ffn1_gate_2, ffn1_up_2, ffn1_down_2, norm_mix_2, w_in_2, w_up_a_2,
        w_up_b_2, w_out_2, norm_ffn2_2, ffn2_gate_2, ffn2_up_2, ffn2_down_2, norm_final_2,
    )


_drawn_inputs = setup_inputs


def setup_inputs(seed=0):
    import zlib

    import numpy as np

    out = dict(_drawn_inputs(seed))
    spreads = {}
    factors = {'da_subln': 4.321,
     'ga_q_norm': 8.0,
     'ga_k_norm': 8.0,
     'norm_ffn1_2': 8.0,
     'norm_mix_2': 8.0,
     'norm_ffn2_2': 23.447,
     'norm_final_2': 8.123}
    for name, (base, spread) in spreads.items():
        noise = np.random.default_rng([zlib.crc32(name.encode()), seed]).standard_normal(out[name].shape)
        drawn = base * np.exp(spread * noise) if base else spread * noise
        out[name] = __import__('jax').numpy.asarray(drawn.astype(out[name].dtype))
    for name, factor in factors.items():
        out[name] = (out[name] * factor).astype(out[name].dtype)
    return out
```

```python
import numpy as np

import concourse.bass as bass
import concourse.mybir as mybir

D = 1024
CH = D // 128
CTX, SEQ = 256, 256
TOK = CTX + SEQ
FULL, LAT = slice(0, TOK), slice(CTX, TOK)
DFF = 2816
FCH = DFF // 128
EPS = 1e-6
MASKED = -1e30
GRID_W = 64
THETA = 10000.0
RING = 4
TW = 1024

DA_HEADS, DA_QK = 8, 64
GA_HEADS, GA_KV, GA_DIM = 8, 2, 128
DSA_GROUPS = ((128, 1), (512, 4), (2048, 16))
DSA_HPG = 4
MOBA_HEADS, HEAD64 = 8, 64
LAMBDA_INIT = 0.2

ADA_CHUNKS = 9 * D // 512
ADA_SLOTS = 6
ADA_TILE = 2048
MODS = 9 * CH

COL = {}
_at = 0
for _name, _n in (("norm_g", 2 * 6 * CH), ("norm2", 4 * CH), ("subln", 1), ("qnorm", 1), ("knorm", 1),
                  ("slopes", 20), ("lambda", 4 * DA_QK), ("cond", 2 * CH)):
    COL[_name] = _at
    _at += _n
NCOL = _at
TAB = {"ident": 0, "rot": 128, "da_cos": 256, "da_sin": 512, "ga_cos": 768, "ga_sin": 1024}
NTAB = 1280
DIST = {("dsa", 0): 0, ("dsa", 1): 384, ("moba", 0): 1152, ("moba", 1): 1280}
NDIST = 1536


def sub_blocks():
    spec = [("ffn", FULL, FULL, 0, 0), ("da", FULL, FULL, 0, 1), ("ffn", FULL, FULL, 0, 2),
            ("ffn", FULL, FULL, 1, 0), ("ga", FULL, LAT, 1, 1), ("ffn", LAT, LAT, 1, 2),
            ("ffn", LAT, LAT, None, 0), ("b2", LAT, LAT, None, 1), ("ffn", LAT, LAT, None, 2)]
    body_tiles = {"ffn": 2 * FCH, "da": 3 * DA_HEADS, "ga": 2 * GA_KV + GA_HEADS, "b2": 30 + 3 * CH}
    out, t, f = [], 0, 0
    for n, (kind, tok_in, tok_out, layer, part) in enumerate(spec):
        b = {"n": n, "kind": kind, "tok": tok_in, "tok_out": tok_out, "layer": layer, "part": part,
             "t_body": t, "t_out": t + body_tiles[kind], "f": f}
        b["out_tiles"] = 3 * CH if kind == "ffn" else CH
        t = b["t_out"] + b["out_tiles"]
        f += kind == "ffn"
        out.append(b)
    return out, t


def out_parts(kind):
    return [(0, 8), (8, 15), (15, 22)] if kind == "ffn" else [(0, 8)]


def mixer_plan(kind, t0):
    sets, t, idx, U = [], t0, 0, 0

    def item(what, s, g, tok, **more):
        nonlocal t, idx
        it = {"what": what, "s": s, "g": g, "tok": tok, "t": t, "idx": idx, "norm": False, "rope": False, **more}
        t, idx = t + 1, idx + 1
        return it

    if kind == "da":
        for h in range(DA_HEADS):
            items = [item("q", h, 0, FULL, rope=True, par=h % 2), item("k", h, 0, FULL, rope=True, par=h % 2),
                     item("v", h, 0, FULL, par=h % 2)]
            sets.append({"s": h, "items": items, "q": items[:1], "k": items[1:2], "v": items[2:],
                         "units": [{"qt": qt, "keys": keys, "ocol": qt * 128} for qt, keys in
                                   ((2, TOK), (3, TOK), (0, CTX), (1, CTX))]})
    elif kind == "ga":
        kv = None
        for h in range(GA_HEADS):
            g = h // (GA_HEADS // GA_KV)
            items = []
            if h % (GA_HEADS // GA_KV) == 0:
                kv = [item("k", h, 0, FULL, norm=True, rope=True, par=g % 2), item("v", h, 0, FULL, par=g % 2)]
                items += kv
            items.append(item("q", h, 0, LAT, norm=True, rope=True, par=h % 2))
            sets.append({"s": h, "items": items, "q": items[-1:], "k": kv[:1], "v": kv[1:],
                         "units": [{"qt": qt, "keys": TOK, "ocol": qt * 128} for qt in (2, 3)]})
    else:
        for s in range(6):
            ng = 3 if s < 2 else 1
            items = [item(w, s, g, LAT, par=s % 2) for g in range(ng) for w in "qkv"]
            sets.append({"s": s, "items": items, "q": items[0::3], "k": items[1::3], "v": items[2::3],
                         "units": [{"qt": qt, "j": j, "keys": 128 * (qt + 1), "ocol": (2 * j + qt) * 128}
                                   for qt in (1, 0) for j in (0, 1)]})
    for st in sets:
        st["first_unit"] = U
        for u in st["units"]:
            u.update(U=U, set=st, tiles=u["keys"] // 128)
            U += 1
        st["last_unit"] = U - 1

    order, turns, ropes, norms = [], 0, 0, 0

    def add(op, x):
        nonlocal turns, ropes, norms
        entry = [op, x, None]
        if op in ("ss", "rot", "vtr", "T", "oss"):
            entry[2] = turns
            turns += 1
        if op == "rot":
            ropes += 1
            x["rope_n"] = ropes
        if op == "ss":
            norms += 1
            x["norm_n"] = norms
        if op in ("ss", "vtr"):
            x["turn"] = entry[2]
        order.append(entry)

    def add_T(u):
        blocks = [(g, kt) for g in range(len(u["set"]["v"])) for kt in range(u["tiles"])]
        u["blocks"] = blocks
        for a in range(0, len(blocks), 4):
            add("T", (u, a, min(a + 4, len(blocks))))
        u["turn"] = turns - 1

    def preps(it):
        return [op for op, on in (("ss", it["norm"]), ("rot", it["rope"]), ("vtr", it["what"] == "v")) if on]

    for it in sets[0]["items"]:
        add("proj", it)
    for stage in range(2):
        for it in sets[0]["items"]:
            if len(preps(it)) > stage:
                add(preps(it)[stage], it)
    for s, st in enumerate(sets):
        nxt = sets[s + 1]["items"] if s + 1 < len(sets) else []
        nu = len(st["units"])
        late = []
        add("S", st["units"][0])
        for n, u in enumerate(st["units"]):
            mine = nxt[n * len(nxt) // nu:(n + 1) * len(nxt) // nu] if len(nxt) >= nu else nxt[n:n + 1]
            if kind == "ga" and len(nxt) == 3:
                mine = nxt[:2] if n == 0 else nxt[2:]
            for it in mine:
                add("proj", it)
            if n + 1 < nu:
                add("S", st["units"][n + 1])
            add_T(u)
            if n == 0 and s and kind == "da":
                add("oss", sets[s - 1])
            now, late = late, []
            for it in mine:
                p = preps(it)
                if p:
                    now.append((p[0], it))
                if len(p) > 1:
                    late.append((p[1], it))
            for op, it in now:
                add(op, it)
            add("PV", u)
        for op, it in late:
            add(op, it)
        add("O", st)
    if kind == "da":
        add("oss", sets[-1])
    return order, idx


def build(nc, A):
    F32, F32R = mybir.dt.float32, mybir.dt.float32r
    ACT, ALU, AX = mybir.ActivationFunctionType, mybir.AluOpType, mybir.AxisListType
    BLOCKS, N_TILES = sub_blocks()
    EXP_SET, SILU_SET, SIG_SET = "natural_log_exp_and_others", "silu_and_others", "sigmoid_and_others"

    base = (nc.sbuf_base + 63) // 64 * 64
    H0 = base
    U0 = H0 + CH * TOK * 4
    GU0 = U0 + 2 * CH * TOK * 4
    RING0 = GU0 + 2 * FCH * TOK * 4
    MISC0 = RING0 + 3 * RING * TW * 4

    def region(start):
        at = [start]

        def take(name, shape, dt=F32):
            t = nc.alloc_sbuf_tensor_at(name, [128, *shape], dt, offset=at[0])
            at[0] += (int(np.prod(shape)) * 4 + 31) // 32 * 32
            return t
        return take, at

    take, _ = region(H0)
    h = take("h", [CH, TOK])
    take, _ = region(U0)
    u_hi, u_lo = take("u_hi", [CH, TOK], F32R), take("u_lo", [CH, TOK], F32R)
    take, _ = region(U0)
    y = take("y", [CH, TOK])
    take, _ = region(U0)
    final = take("final", [CH, SEQ])
    take, _ = region(GU0)
    gu_hi, gu_lo = take("gu_hi", [FCH, TOK], F32R), take("gu_lo", [FCH, TOK], F32R)
    take, _ = region(GU0)
    ada_ring = take("ada_ring", [ADA_SLOTS, ADA_TILE])
    mrow = take("mrow", [9 * D])
    take, _ = region(GU0)
    v1 = take("v1", [2, TOK])
    ufull = take("ufull", [2, TOK])
    take, at = region(GU0)
    q_st, k_st = take("q_st", [2, 768]), take("k_st", [2, 768])
    vT = take("vT", [768])
    v_st = take("v_st", [2, 768])
    prob = take("prob", [2, 1024])
    pcomb = take("pcomb", [2, 768])
    probT = take("probT", [2, 768])
    rope_a, rope_b = take("rope_a", [SEQ]), take("rope_b", [SEQ])
    MIX0 = at[0]
    o_hi, o_lo = take("o_hi", [CH, TOK], F32R), take("o_lo", [CH, TOK], F32R)
    o_raw, o_sq, rs = take("o_raw", [TOK]), take("o_sq", [TOK]), take("rs", [TOK])
    n_sq = take("n_sq", [2, TOK])
    assert at[0] <= RING0
    take, at = region(MIX0)
    y_hi, y_lo = take("y_hi", [6, SEQ], F32R), take("y_lo", [6, SEQ], F32R)
    mg_hi, mg_lo = take("mg_hi", [CH, SEQ], F32R), take("mg_lo", [CH, SEQ], F32R)
    dist = take("dist", [NDIST])
    sbias = take("sbias", [2, 768])
    assert at[0] <= RING0
    take, _ = region(MIX0 - (2 * SEQ + 2 * 768 + 2 * 768 + 2048) * 4)
    sig_a, sig_b, mg = take("sig_a", [2, SEQ]), take("sig_b", [2, SEQ]), take("mg", [2, SEQ])
    take, _ = region(RING0)
    w_raw = take("w_raw", [RING, TW])
    w_hi, w_lo = take("w_hi", [RING, TW], F32R), take("w_lo", [RING, TW], F32R)
    take, at = region(MISC0)
    tab = take("tab", [NTAB])
    col = take("col", [NCOL])
    mcol = take("mcol", [4, MODS])
    a_col, g_col = take("a_col", [12, CH]), take("g_col", [12, CH])
    ones = take("ones", [128])
    rstd_y, rstd_h = take("rstd_y", [TOK]), take("rstd_h", [TOK])
    sq = take("sq", [2, TOK])
    sqsum = take("sqsum", [TOK])
    silu_at = at[0]
    s_up = take("s_up", [2, TOK])
    stat = take("stat", [4, 8])
    small = take("small", [16])
    silu_c = take("silu_c", [CH, 2])
    assert at[0] <= nc.sbuf_usable_end, at[0] - nc.sbuf_usable_end
    take, _ = region(silu_at)
    m_rows = take("m_rows", [4, 128])
    ada_bias = take("ada_bias", [2, 128])
    lam_t = take("lam_t", [2, DA_QK])
    psum = nc.alloc_psum_tensor("psum", [128, 8, 512], F32)
    SHARED, PVB, SSY, SSH = 3, 2, 6, 7

    ident, rot = tab[:, 0:128], tab[:, 128:256]
    eps = small[:, 0:1]
    neg_lam = small[:, 1:2]

    sem = nc.alloc_semaphore
    raw_landed = [sem(f"raw_landed{i}") for i in range(RING)]
    ada_landed = [sem(f"ada_landed{i}") for i in range(ADA_SLOTS)]
    hi_ready, lo_ready, tile_used = sem("hi_ready"), sem("lo_ready"), sem("tile_used")
    consts_in, h_in, dist_in, bias_in = sem("consts_in"), sem("h_in"), sem("dist_in"), sem("bias_in")
    set_up = sem("set_up")
    silu_c_ready, ada_used, m_evac = sem("silu_c_ready"), sem("ada_used"), sem("m_evac")
    m_gathered, m_biased, m_turned, m_cols, coefs = (sem("m_gathered"), sem("m_biased"), sem("m_turned"),
                                                     sem("m_cols"), sem("coefs"))
    lam_sum, lam_exp, lam_ready, lam_step = sem("lam_sum"), sem("lam_exp"), sem("lam_ready"), sem("lam_step")
    h_ready, hsq_ready, hsq_used = sem("h_ready"), sem("hsq_ready"), sem("hsq_used")
    ln_done, rstd_h_ready, rstd_y_ready = sem("ln_done"), sem("rstd_h_ready"), sem("rstd_y_ready")
    v1_ready, uhi_ready, u_ready = sem("v1_ready"), sem("uhi_ready"), sem("u_ready")
    silu_ready, g_ready, ghi_ready, gu_ready = sem("silu_ready"), sem("g_ready"), sem("ghi_ready"), sem("gu_ready")
    y_evac, ysq_ready, yacc_ready, yss_ready = sem("y_evac"), sem("ysq_ready"), sem("yacc_ready"), sem("yss_ready")
    sqsum_zero, ymul_ready = sem("sqsum_zero"), sem("ymul_ready")
    out_ready, out_done = sem("out_ready"), sem("out_done")
    MS = {}
    for kind in ("da", "ga", "b2"):
        MS[kind] = {name: sem(f"{kind}_{name}") for name in (
            "proj_evac", "turn_ready", "turn_free", "rs_ready", "normed", "qk_ready", "s_ready", "biased",
            "max_part", "max_ready", "exp_done", "recip", "comb_part", "pc_ready", "pv_ready", "osq_ready",
            "o_evac", "on_ready", "ohi_ready", "olo_ready")}
    sig_ready, gate_part, gate_sum, mhi_ready, merged_ready = (sem("sig_ready"), sem("gate_part"), sem("gate_sum"),
                                                               sem("mhi_ready"), sem("merged_ready"))

    LO0, USED0, PAIR0, ADA0, BANKS0 = RING, RING, 2, ADA_SLOTS, 3

    def conds(b):
        if b["layer"] is None:
            return [(b["tok"], None)]
        both = [(slice(0, CTX), 2 * b["layer"] + 1), (LAT, 2 * b["layer"])]
        return both if b["tok"] == FULL else both[1:]

    def width(tok):
        return tok.stop - tok.start

    plans = {b["kind"]: mixer_plan(b["kind"], b["t_body"]) for b in BLOCKS if b["kind"] != "ffn"}

    def item_stage(it):
        n = width(it["tok"])
        off = it["g"] * SEQ
        if it["what"] == "v":
            return vT[:, off:off + n]
        return (q_st if it["what"] == "q" else k_st)[:, it["par"], off:off + n]

    def latents(it):
        n = width(it["tok"])
        off = it["g"] * SEQ + n - SEQ
        return (q_st if it["what"] == "q" else k_st)[:, it["par"], off:off + SEQ]

    def v_tile(it, kt):
        off = it["g"] * SEQ + kt * 128
        return v_st[:, it["par"], off:off + 128]

    def scores_of(kind, u):
        b0 = 4 + 2 * (u["U"] % 2)
        if kind == "da":
            return psum[:, b0:b0 + 2, 0:u["keys"]]
        n = u["keys"] * len(u["set"]["v"])
        return psum[:, b0:b0 + 2, :].rearrange("p a b -> p (a b)")[:, 0:n]

    def slope_col(kind, u, g):
        s = u["set"]["s"]
        n = DSA_HPG * g + 2 * s + u["j"] if s < 2 else len(DSA_GROUPS) * DSA_HPG + 2 * (s - 2) + u["j"]
        c = COL["slopes"] + n
        return col[:, c:c + 1]

    def exps_through(kind, U):
        return (2 if kind == "da" else 1) * (U + 1)

    block_cm = nc.Block()
    block = block_cm.__enter__()

    @block.sync
    def _(sp):
        sp.dma_start(col[:, :], A["columns"]).then_inc(consts_in, 16)
        sp.dma_start(tab[:, :], A["tables"]).then_inc(consts_in, 16)
        with sp.Fori(0, 2 * ADA_CHUNKS * 2 // ADA_SLOTS) as i:
            for s in range(ADA_SLOTS):
                sp.wait_ge(ada_used, i * ADA_SLOTS + (s + 1))
                src = A["ada_w"][bass.ds(i * ADA_SLOTS + s, 1)].rearrange("o p c -> p (o c)")
                sp.dma_start(ada_ring[:, s, :], src).then_inc(ada_landed[s], 16)
        sp.dma_start(h[:, :, :], A["hT"]).then_inc(h_in, 16)

        def load(src, t, slot, cols):
            sp.wait_ge(lo_ready, t + 1)
            sp.dma_start(w_raw[:, slot, 0:cols], src).then_inc(raw_landed[slot], 16)

        def load_whole(dram, t0, count):
            loops = count // RING
            with sp.Fori(0, loops) as i:
                for j in range(RING):
                    src = dram[bass.ds(i * RING + j, 1)].rearrange("o p c -> p (o c)")
                    load(src, i * RING + (t0 + j), (t0 + j) % RING, TW)
            for n in range(loops * RING, count):
                load(dram[n], t0 + n, (t0 + n) % RING, TW)

        for b in BLOCKS:
            if b["kind"] == "ffn":
                load_whole(A[f"ffn_in{b['f']}"], b["t_body"], 2 * FCH)
                with sp.Fori(0, 2) as i:
                    for j in range(4):
                        row = A[f"ffn_out{b['f']}"][bass.ds(i * 4 + j, 1)].rearrange("o p c -> p (o c)")
                        for n, (k0, k1) in enumerate(out_parts("ffn")):
                            t = b["t_out"] + 3 * j + n
                            load(row[:, k0 * 128:k1 * 128], i * 12 + t, t % RING, (k1 - k0) * 128)
            elif b["kind"] == "b2":
                load_whole(A["b2_qkv"], b["t_body"], RING)
                sp.wait_ge(tile_used, b["t_body"] + USED0)
                sp.dma_start(dist[:, :], A["dist"]).then_inc(dist_in, 16)
                load_whole(A["b2_qkv"][RING:], b["t_body"] + RING, 30 - RING)
                t0 = b["t_body"] + 30
                with sp.Fori(0, 2) as i:
                    for j in range(4):
                        gates = A["b2_gate"][bass.ds(i * 4 + j, 1)].rearrange("o g p c -> p (o g) c")
                        up = A["b2_up"][bass.ds(i * 4 + j, 1)].rearrange("o p c -> p (o c)")
                        for n, (src, cols) in enumerate(((gates[:, 0, :], TW), (gates[:, 1, :], TW), (up, 6 * 128))):
                            load(src, i * 12 + (t0 + 3 * j + n), (t0 + 3 * j + n) % RING, cols)
                load_whole(A["b2_out"], b["t_out"], CH)
            else:
                load_whole(A[b["kind"] + "_in"], b["t_body"], b["t_out"] - b["t_body"])
                load_whole(A[b["kind"] + "_out"], b["t_out"], CH)
        for half in range(2):
            sp.wait_ge(out_ready, 4 * half + 4)
            c = slice(4 * half, 4 * half + 4)
            sp.dma_start(A["out"][:, c, :], final[:, c, :]).then_inc(out_done, 16)
        sp.wait_ge(out_done, 32)

    @block.gpsimd
    def _(pool):
        def rest(t, slot):
            pool.wait_ge(hi_ready, t + 1)
            pool.wait_ge(tile_used, t + 1)
            pool.tensor_tensor(w_lo[:, slot, :], w_raw[:, slot, :], w_hi[:, slot, :].bitcast(F32),
                               ALU.subtract).then_inc(lo_ready, 1)

        loops = N_TILES // RING
        with pool.Fori(0, loops) as i:
            for j in range(RING):
                rest(i * RING + j, j)
        for t in range(loops * RING, N_TILES):
            rest(t, t % RING)

    @block.scalar
    def _(act):
        logs = [0]
        scalar = nc.scalar

        def head(t, slot, cols=TW, i=0, per=0):
            act.wait_ge(raw_landed[slot], i * (per // RING * 16) + 16 * (t // RING + 1))
            scalar.activation(w_hi[:, slot, 0:cols], w_raw[:, slot, 0:cols], ACT.Copy).then_inc(hi_ready, 1)

        def tile_done(t, i=0, per=0):
            act.wait_ge(tile_used, i * per + (t + 1 + USED0))

        def refill(t, i=0, per=0, last=False):
            if not last:
                head(t + RING, (t + RING) % RING, TW, i, per)

        def rstd(out, ss, count, scale, ready, freed=None):
            ln = scalar.activation(out, ss, ACT.Ln, bias=eps, scale=scale)
            if freed is not None:
                ln.then_inc(freed, 1)
                act.wait_ge(freed, count)
            else:
                ln.then_inc(ln_done, 1)
                logs[0] += 1
                act.wait_ge(ln_done, logs[0])
            scalar.activation(out, out, ACT.Exp, scale=-0.5).then_inc(ready, 1)

        act.wait_ge(consts_in, 32)
        scalar.preload_act_table_set(SILU_SET)
        scalar.activation(silu_c[:, :, :], col[:, COL["cond"]:COL["cond"] + 2 * CH].rearrange("p (k c) -> p k c", c=2),
                          ACT.Silu).then_inc(silu_c_ready, 1)
        act.dma_start(ada_bias[0:MODS, :, :], A["ada_b"]).then_inc(bias_in, 16)
        scalar.preload_act_table_set(EXP_SET)
        act.wait_ge(lam_sum, 2)
        scalar.activation(small[:, 4:6], small[:, 2:4], ACT.Exp).then_inc(lam_exp, 1)
        for layer in range(2):
            act.wait_ge(m_evac, ADA_CHUNKS * (layer + 1) + BANKS0)
            for c in range(2):
                act.dma_start(m_rows[0:MODS, 2 * layer + c, :],
                              mrow[c:c + 1, :].rearrange("o (r x) -> o r x", x=128)).then_inc(m_gathered, 16)
        for t in range(RING):
            head(t, t)

        def pre_norm(b):
            n, tok = b["n"], b["tok"]
            if n == 0:
                act.wait_ge(h_in, 16)
                act.wait_ge(set_up, 2)
            for c in range(CH):
                if n:
                    act.wait_ge(h_ready, CH * (n - 1) + c + 1)
                if c >= 2:
                    act.wait_ge(hsq_used, CH * n + c - 1)
                scalar.activation(sq[:, c % 2, tok], h[:, c, tok], ACT.Square).then_inc(hsq_ready, 1)
            act.wait_ge(hsq_used, CH * n + CH)
            rstd(rstd_h[:, tok], psum[:, SSH, tok], None, 1.0 / D, rstd_h_ready)

        def modulate(b):
            n, tok = b["n"], b["tok"]
            for c in range(CH):
                act.wait_ge(v1_ready, CH * n + c + 1)
                if b["layer"] is None:
                    scalar.activation(u_hi[:, c, tok], v1[:, c % 2, tok], ACT.Copy).then_inc(uhi_ready, 1)
                    continue
                if c >= 2:
                    act.wait_ge(u_ready, CH * n + c - 1)
                for part, m in conds(b):
                    shift = mcol[:, m, 3 * b["part"] * CH + c:3 * b["part"] * CH + c + 1]
                    scalar.activation(ufull[:, c % 2, part], v1[:, c % 2, part], ACT.Identity, bias=shift)
                    last = scalar.activation(u_hi[:, c, part], v1[:, c % 2, part], ACT.Identity, bias=shift)
                last.then_inc(uhi_ready, 1)

        def ffn_body(b):
            tok, f, t0 = b["tok"], b["f"], b["t_body"]
            scalar.preload_act_table_set(SILU_SET)
            with act.Fori(0, FCH // 2) as i:
                for j in range(2):
                    gate, up = t0 + 2 * j, t0 + 2 * j + 1
                    tile_done(gate, i, 4)
                    act.wait_ge(gu_ready, i * 2 + (FCH * f + j + 1))
                    scalar.activation(s_up[:, j, tok], psum[:, 2 * j, tok], ACT.Silu).then_inc(silu_ready, 1)
                    refill(gate, i, 4)
                    tile_done(up, i, 4)
                    refill(up, i, 4)
            scalar.preload_act_table_set(EXP_SET)

        def output(b):
            n, tok = b["n"], b["tok_out"]
            gated = b["layer"] is not None
            parts = out_parts(b["kind"])
            per = 4 * len(parts)

            def chunks(i, end):
                for j in range(4):
                    for p in range(len(parts)):
                        t = b["t_out"] + len(parts) * j + p
                        tile_done(t, i, per)
                        if gated and p == len(parts) - 1:
                            act.wait_ge(yacc_ready, i * 4 + (CH * n + j + 1))
                            scalar.activation(sq[:, j % 2, tok], psum[:, 4 + j % 2, tok], ACT.Square)\
                                  .then_inc(ysq_ready, 1)
                        refill(t, i, per, last=end and t + per + RING >= N_TILES)

            if b["t_out"] + b["out_tiles"] == N_TILES:
                chunks(0, False)
                chunks(1, True)
            else:
                with act.Fori(0, 2) as i:
                    chunks(i, False)
            if gated:
                act.wait_ge(yss_ready, n + 1)
                rstd(rstd_y[:, tok], psum[:, SSY, tok], None, 1.0 / D, rstd_y_ready)

        def mixer(b):
            kind = b["kind"]
            S = MS[kind]
            order, _ = plans[kind]
            scale = {"da": DA_QK ** -0.5, "ga": GA_DIM ** -0.5, "b2": 1.0}[kind]
            normed = 0
            ss_turn = {}
            for op, x, turn in order:
                if op == "proj":
                    tile_done(x["t"])
                    src = psum[:, x["idx"] % 2, x["tok"]]
                    dst = item_stage(x)
                    if x["norm"]:
                        if x["idx"] - 2 in ss_turn:
                            act.wait_ge(S["turn_ready"], ss_turn[x["idx"] - 2] + 1)
                        ss_turn[x["idx"]] = x["turn"]
                        scalar.activation(dst, src, ACT.Copy)
                        scalar.activation(n_sq[:, x["idx"] % 2, x["tok"]], src, ACT.Square).then_inc(S["proj_evac"], 1)
                    else:
                        s = HEAD64 ** -0.5 if kind == "b2" and x["what"] == "q" else 1.0
                        scalar.activation(dst, src, ACT.Copy, scale=s).then_inc(S["proj_evac"], 1)
                    refill(x["t"])
                elif op == "ss":
                    act.wait_ge(S["turn_ready"], turn + 1)
                    if normed:
                        act.wait_ge(S["normed"], normed)
                    normed += 1
                    rstd(rs[:, x["tok"]], psum[:, SHARED, x["tok"]], turn + 1, 1.0 / GA_DIM, S["rs_ready"], S["turn_free"])
                elif op == "S":
                    U = x["U"]
                    act.wait_ge(S["max_ready"], U + 1)
                    if U >= 2:
                        act.wait_ge(S["pc_ready"], U - 1)
                    n = x["keys"] * (len(x["set"]["v"]) if kind == "b2" else 1)
                    for m in range(2 if kind == "da" else 1):
                        if kind == "da":
                            src = scores_of(kind, x)[:, m, :]
                        else:
                            src = scores_of(kind, x) if kind == "ga" else sbias[:, U % 2, 0:n]
                        scalar.activation(prob[:, U % 2, m * 512:m * 512 + n], src, ACT.Exp,
                                          bias=stat[:, U % 4, 2 + m:3 + m], scale=scale,
                                          accum_out=stat[:, U % 4, 4 + m:5 + m]).then_inc(S["exp_done"], 1)
                elif op == "T":
                    u, a, e = x
                    act.wait_ge(S["turn_ready"], turn + 1)
                    scalar.activation(probT[:, u["U"] % 2, a * 128:e * 128], psum[:, SHARED, 0:(e - a) * 128],
                                      ACT.Copy).then_inc(S["turn_free"], 1)
                elif op == "O":
                    act.wait_ge(S["pv_ready"], x["last_unit"] + 1)
                    s = x["s"]
                    if kind == "da":
                        scalar.activation(o_sq[:, :], psum[:, PVB, :], ACT.Square).then_inc(S["osq_ready"], 1)
                    elif kind == "ga":
                        scalar.activation(o_hi[:, s, LAT], psum[:, PVB, LAT], ACT.Copy).then_inc(S["ohi_ready"], 1)
                    else:
                        for j in range(2):
                            p = slice(64 * j, 64 * j + 64)
                            last = scalar.activation(y_hi[p, s, :], psum[p, PVB, 256 * j:256 * j + 256], ACT.Copy)
                        last.then_inc(S["ohi_ready"], 1)
                elif op == "oss":
                    act.wait_ge(S["turn_ready"], turn + 1)
                    rstd(rs[:, :], psum[:, SHARED, :], turn + 1, 1.0 / 128, S["rs_ready"], S["turn_free"])
                    act.wait_ge(S["on_ready"], x["s"] + 1)
                    scalar.activation(o_hi[:, x["s"], :], o_raw[:, :], ACT.Copy).then_inc(S["ohi_ready"], 1)

        def gates(b):
            scalar.preload_act_table_set(SIG_SET)
            t0 = b["t_body"] + 30
            with act.Fori(0, 2) as i:
                for j in range(4):
                    for n, sig in ((0, sig_a), (1, sig_b)):
                        tile_done(t0 + 3 * j + n, i, 12)
                        scalar.activation(sig[:, j % 2, :], psum[:, 4 * (j % 2) + n, 0:SEQ], ACT.Sigmoid)\
                              .then_inc(sig_ready, 1)
                        refill(t0 + 3 * j + n, i, 12)
                    tile_done(t0 + 3 * j + 2, i, 12)
                    refill(t0 + 3 * j + 2, i, 12)
            scalar.preload_act_table_set(EXP_SET)

        for b in BLOCKS:
            pre_norm(b)
            modulate(b)
            if b["kind"] == "ffn":
                ffn_body(b)
            else:
                mixer(b)
                if b["kind"] == "b2":
                    gates(b)
            output(b)
        pre_norm({"n": len(BLOCKS), "tok": LAT})

    @block.vector
    def _(dve):
        vec = nc.vector
        for s, n in ((ada_used, ADA0), (m_evac, BANKS0), (lo_ready, LO0), (tile_used, USED0), (g_ready, PAIR0),
                     (gu_ready, PAIR0), (y_evac, PAIR0), (ysq_ready, PAIR0), (yacc_ready, PAIR0), (merged_ready, PAIR0)):
            dve.sem_inc(s, n)
        vec.memset(ones[:, :], 1.0).then_inc(set_up, 1)
        vec.memset(eps, EPS).then_inc(set_up, 1)

        dve.wait_ge(consts_in, 32)
        for m in range(2):
            l0 = COL["lambda"] + 2 * m * DA_QK
            vec.tensor_tensor_reduce(out=lam_t[:, m, :], in0=col[:, l0:l0 + DA_QK], in1=col[:, l0 + DA_QK:l0 + 2 * DA_QK],
                                     scale=1.0, scalar=0.0, op0=ALU.mult, op1=ALU.add,
                                     accum_out=small[:, 2 + m:3 + m]).then_inc(lam_sum, 1)
        dve.wait_ge(lam_exp, 1)
        vec.tensor_tensor(small[:, 6:7], small[:, 5:6], small[:, 4:5], ALU.subtract).then_inc(lam_step, 1)
        dve.wait_ge(lam_step, 1)
        vec.tensor_scalar(neg_lam, small[:, 6:7], -LAMBDA_INIT, None, ALU.add).then_inc(lam_ready, 1)

        for layer in range(2):
            if layer:
                dve.wait_ge(m_gathered, 32)
            with dve.Fori(0, ADA_CHUNKS // 3) as i:
                for j in range(3):
                    dve.wait_ge(ada_used, i * 6 + (2 * (ADA_CHUNKS * layer + j) + 2 + ADA0))
                    vec.tensor_copy(mrow[0:2, bass.ds((i * 3 + j) * 512, 512)], psum[0:2, j, :]).then_inc(m_evac, 1)
        dve.wait_ge(bias_in, 16)
        dve.wait_ge(m_gathered, 64)
        for m in range(4):
            vec.tensor_tensor(m_rows[0:MODS, m, :], m_rows[0:MODS, m, :], ada_bias[0:MODS, m // 2, :], ALU.add)\
               .then_inc(m_biased, 1)
        dve.wait_ge(m_turned, 1)
        vec.tensor_copy(mcol[:, :, :], psum[:, SHARED, 0:4 * MODS].rearrange("p (m r) -> p m r", m=4)).then_inc(m_cols, 1)
        dve.wait_ge(m_cols, 1)
        for layer in range(2):
            for c in range(2):
                for part in range(3):
                    m, n = 2 * layer + c, 3 * (2 * layer + c) + part
                    pre = COL["norm_g"] + (6 * layer + 2 * part) * CH
                    post = pre + CH
                    scale = mcol[:, m, (3 * part + 1) * CH:(3 * part + 2) * CH]
                    gate = mcol[:, m, (3 * part + 2) * CH:(3 * part + 3) * CH]
                    vec.scalar_tensor_tensor(out=a_col[:, n, :], in0=scale, scalar=1.0, in1=col[:, pre:pre + CH],
                                             op0=ALU.add, op1=ALU.mult)
                    vec.scalar_tensor_tensor(out=g_col[:, n, :], in0=gate, scalar=1.0 if part == 1 else 0.5,
                                             in1=col[:, post:post + CH], op0=ALU.mult, op1=ALU.mult).then_inc(coefs, 1)
        dve.wait_ge(coefs, 12)

        def norm_gain(b, m, c):
            if m is None:
                g = COL["norm2"] + b["part"] * CH + c
                return col[:, g:g + 1]
            return a_col[:, 3 * m + b["part"], c:c + 1]

        def modulate(b):
            n, tok = b["n"], b["tok"]
            if n == 0:
                dve.wait_ge(h_in, 16)
            dve.wait_ge(rstd_h_ready, n + 1)

            def rest(c):
                dve.wait_ge(uhi_ready, CH * n + c + 1)
                full = v1 if b["layer"] is None else ufull
                vec.tensor_tensor(u_lo[:, c, tok], full[:, c % 2, tok], u_hi[:, c, tok].bitcast(F32), ALU.subtract)\
                   .then_inc(u_ready, 1)

            for c in range(CH):
                if c >= 2:
                    dve.wait_ge(u_ready, CH * n + c - 1)
                for part, m in conds(b):
                    last = vec.scalar_tensor_tensor(out=v1[:, c % 2, part], in0=h[:, c, part], scalar=norm_gain(b, m, c),
                                                    in1=rstd_h[:, part], op0=ALU.mult, op1=ALU.mult)
                last.then_inc(v1_ready, 1)
                if c:
                    rest(c - 1)
            rest(CH - 1)

        def ffn_body(b):
            tok, f, t0 = b["tok"], b["f"], b["t_body"]
            with dve.Fori(0, FCH // 2) as i:
                for j in range(2):
                    m0 = FCH * f + j
                    dve.wait_ge(silu_ready, i * 2 + (m0 + 1))
                    dve.wait_ge(tile_used, i * 4 + (t0 + 2 * j + 2 + USED0))
                    vec.tensor_tensor(s_up[:, j, tok], s_up[:, j, tok], psum[:, 2 * j + 1, tok], ALU.mult)\
                       .then_inc(g_ready, 1)
                    dve.wait_ge(g_ready, i * 2 + (m0 + 1 + PAIR0))
                    hi = gu_hi[:, bass.ds(i * 2 + j, 1), tok].rearrange("p o t -> p (o t)")
                    lo = gu_lo[:, bass.ds(i * 2 + j, 1), tok].rearrange("p o t -> p (o t)")
                    vec.tensor_copy(hi, s_up[:, j, tok]).then_inc(ghi_ready, 1)
                    dve.wait_ge(ghi_ready, i * 2 + (m0 + 1))
                    vec.tensor_tensor(lo, s_up[:, j, tok], hi.bitcast(F32), ALU.subtract).then_inc(gu_ready, 1)

        def output(b):
            n, tok = b["n"], b["tok_out"]
            parts = len(out_parts(b["kind"]))
            if b["layer"] is None:
                weight = 1.0 if b["part"] == 1 else 0.5
                with dve.Fori(0, 2) as i:
                    for j in range(4):
                        dve.wait_ge(tile_used, i * (4 * parts) + (b["t_out"] + parts * (j + 1) + USED0))
                        hc = h[:, bass.ds(i * 4 + j, 1), tok].rearrange("p o t -> p (o t)")
                        vec.scalar_tensor_tensor(out=hc, in0=psum[:, 4 + j % 2, tok], scalar=weight, in1=hc,
                                                 op0=ALU.mult, op1=ALU.add).then_inc(h_ready, 1)
                return
            vec.memset(sqsum[:, tok], 0.0).then_inc(sqsum_zero, 1)
            dve.wait_ge(sqsum_zero, n + 1)
            with dve.Fori(0, 2) as i:
                for j in range(4):
                    dve.wait_ge(tile_used, i * (4 * parts) + (b["t_out"] + parts * (j + 1) + USED0))
                    dve.wait_ge(ysq_ready, i * 4 + (CH * n + j + 1 + PAIR0))
                    for part, m in conds({**b, "tok": tok}):
                        gate = g_col[:, 3 * m + b["part"], bass.ds(i * 4 + j, 1)]
                        yc = y[:, bass.ds(i * 4 + j, 1), part].rearrange("p o t -> p (o t)")
                        last = vec.tensor_scalar(yc, psum[:, 4 + j % 2, part], gate, None, ALU.mult)
                    last.then_inc(y_evac, 1)
                    dve.wait_ge(yacc_ready, i * 4 + (CH * n + j + PAIR0))
                    vec.tensor_tensor(sqsum[:, tok], sqsum[:, tok], sq[:, j % 2, tok], ALU.add).then_inc(yacc_ready, 1)
            dve.wait_ge(rstd_y_ready, n + 1)

            def add(c):
                dve.wait_ge(ymul_ready, CH * n + c + 1)
                vec.tensor_tensor(h[:, c, tok], h[:, c, tok], y[:, c, tok], ALU.add).then_inc(h_ready, 1)

            dve.wait_ge(y_evac, CH * n + CH + PAIR0)
            for c in range(CH):
                vec.tensor_tensor(y[:, c, tok], y[:, c, tok], rstd_y[:, tok], ALU.mult).then_inc(ymul_ready, 1)
                if c:
                    add(c - 1)
            add(CH - 1)

        def mixer(b):
            kind = b["kind"]
            S = MS[kind]
            order, _ = plans[kind]
            scale = {"da": DA_QK ** -0.5, "ga": GA_DIM ** -0.5, "b2": 1.0}[kind]
            cos, sin = (tab[:, TAB[f"{kind}_{w}"]:TAB[f"{kind}_{w}"] + SEQ] if kind != "b2" else None for w in ("cos", "sin"))
            waiting = []
            t_turn = {}
            n_rs = 0
            biased = 0

            def combine(u):
                U = u["U"]
                n = u["keys"] * (len(u["set"]["v"]) if kind == "b2" else 1)
                maps = 2 if kind == "da" else 1
                dve.wait_ge(S["exp_done"], exps_through(kind, U))
                vec.reciprocal(stat[:, U % 4, 6:6 + maps], stat[:, U % 4, 4:4 + maps]).then_inc(S["recip"], 1)
                dve.wait_ge(S["recip"], U + 1)
                if U >= 2:
                    dve.wait_ge(S["turn_ready"], t_turn[U - 2] + 1)
                out = pcomb[:, U % 2, 0:n]
                if kind != "da":
                    vec.tensor_scalar(out, prob[:, U % 2, 0:n], stat[:, U % 4, 6:7], None, ALU.mult).then_inc(S["pc_ready"], 1)
                    return
                vec.tensor_tensor(stat[:, U % 4, 7:8], stat[:, U % 4, 7:8], neg_lam, ALU.mult)
                vec.tensor_scalar(prob[:, U % 2, 0:n], prob[:, U % 2, 0:n], stat[:, U % 4, 6:7], None, ALU.mult)\
                   .then_inc(S["comb_part"], 1)
                dve.wait_ge(S["comb_part"], U + 1)
                vec.scalar_tensor_tensor(out=out, in0=prob[:, U % 2, 512:512 + n], scalar=stat[:, U % 4, 7:8],
                                         in1=prob[:, U % 2, 0:n], op0=ALU.mult, op1=ALU.add).then_inc(S["pc_ready"], 1)

            if kind == "da":
                dve.wait_ge(lam_ready, 1)
            if kind == "b2":
                dve.wait_ge(dist_in, 16)
            for op, x, turn in order:
                if op == "ss":
                    n_rs += 1
                    dve.wait_ge(S["rs_ready"], n_rs)
                    gain = col[:, COL["qnorm" if x["what"] == "q" else "knorm"]:][:, 0:1]
                    vec.scalar_tensor_tensor(out=item_stage(x), in0=item_stage(x), scalar=gain, in1=rs[:, x["tok"]],
                                             op0=ALU.mult, op1=ALU.mult).then_inc(S["normed"], 1)
                elif op == "rot":
                    if x["norm"]:
                        dve.wait_ge(S["normed"], x["norm_n"])
                    dve.wait_ge(S["turn_ready"], turn + 1)
                    if x["rope_n"] > 1:
                        dve.wait_ge(S["qk_ready"], x["rope_n"] - 1)
                    vec.tensor_tensor(rope_a[:, :], latents(x), cos, ALU.mult)
                    vec.tensor_tensor(rope_b[:, :], psum[:, SHARED, 0:SEQ], sin, ALU.mult).then_inc(S["turn_free"], 1)
                    dve.wait_ge(S["turn_free"], turn + 1)
                    vec.tensor_tensor(latents(x), rope_a[:, :], rope_b[:, :], ALU.add).then_inc(S["qk_ready"], 1)
                elif op == "vtr":
                    dve.wait_ge(S["turn_ready"], turn + 1)
                    n = width(x["tok"])
                    vec.tensor_copy(v_st[:, x["par"], x["g"] * SEQ:x["g"] * SEQ + n], psum[:, SHARED, 0:n])\
                       .then_inc(S["turn_free"], 1)
                elif op == "S":
                    if waiting:
                        combine(waiting.pop())
                    waiting.append(x)
                    U = x["U"]
                    dve.wait_ge(S["s_ready"], U + 1)
                    maps = 2 if kind == "da" else 1
                    if kind == "b2":
                        if U >= 2:
                            dve.wait_ge(S["exp_done"], U - 1)
                        n, ng = x["keys"], len(x["set"]["v"])
                        d0 = DIST["dsa" if ng > 1 else "moba", x["qt"]]
                        for g in range(ng):
                            vec.scalar_tensor_tensor(out=sbias[:, U % 2, g * n:g * n + n], in0=dist[:, d0 + g * n:d0 + g * n + n],
                                                     scalar=slope_col(kind, x, g), in1=scores_of(kind, x)[:, g * n:g * n + n],
                                                     op0=ALU.mult, op1=ALU.add).then_inc(S["biased"], 1)
                        biased += ng
                        x["biased"] = biased
                        dve.wait_ge(S["biased"], biased)
                        src = sbias[:, U % 2, 0:ng * n]
                    else:
                        src = scores_of(kind, x)
                    vec.tensor_reduce(stat[:, U % 4, 0:maps], src, AX.X, ALU.max, negate=True).then_inc(S["max_part"], 1)
                    dve.wait_ge(S["max_part"], U + 1)
                    vec.tensor_scalar(stat[:, U % 4, 2:2 + maps], stat[:, U % 4, 0:maps], scale, None, ALU.mult)\
                       .then_inc(S["max_ready"], 1)
                elif op == "T":
                    u, a, e = x
                    if waiting and waiting[0] is u:
                        combine(waiting.pop())
                    t_turn[u["U"]] = u["turn"]
                elif op == "O":
                    dve.wait_ge(S["pv_ready"], x["last_unit"] + 1)
                    s = x["s"]
                    if kind == "da":
                        dve.wait_ge(S["osq_ready"], s + 1)
                        if s:
                            dve.wait_ge(S["olo_ready"], s)
                        vec.tensor_scalar(o_raw[:, :], psum[:, PVB, :], col[:, COL["subln"]:COL["subln"] + 1],
                                          1.0 - LAMBDA_INIT, ALU.mult, ALU.mult).then_inc(S["o_evac"], 1)
                        continue
                    dve.wait_ge(S["ohi_ready"], s + 1)
                    if kind == "ga":
                        vec.tensor_tensor(o_lo[:, s, LAT], psum[:, PVB, LAT], o_hi[:, s, LAT].bitcast(F32), ALU.subtract)\
                           .then_inc(S["olo_ready"], 1)
                    else:
                        for j in range(2):
                            p = slice(64 * j, 64 * j + 64)
                            last = vec.tensor_tensor(y_lo[p, s, :], psum[p, PVB, 256 * j:256 * j + 256],
                                                     y_hi[p, s, :].bitcast(F32), ALU.subtract)
                        last.then_inc(S["olo_ready"], 1)
                elif op == "oss":
                    s = x["s"]
                    dve.wait_ge(S["rs_ready"], s + 1)
                    dve.wait_ge(S["o_evac"], s + 1)
                    vec.tensor_tensor(o_raw[:, :], o_raw[:, :], rs[:, :], ALU.mult).then_inc(S["on_ready"], 1)
                    dve.wait_ge(S["ohi_ready"], s + 1)
                    vec.tensor_tensor(o_lo[:, s, :], o_raw[:, :], o_hi[:, s, :].bitcast(F32), ALU.subtract)\
                       .then_inc(S["olo_ready"], 1)

        def gates(b):
            t0 = b["t_body"] + 30
            with dve.Fori(0, 2) as i:
                for j in range(4):
                    bank = 4 * (j % 2)
                    dve.wait_ge(sig_ready, i * 8 + (2 * j + 2))
                    dve.wait_ge(tile_used, i * 12 + (t0 + 3 * j + 3 + USED0))
                    vec.tensor_tensor(sig_a[:, j % 2, :], sig_a[:, j % 2, :], psum[:, bank + 2, 0:SEQ], ALU.mult)
                    vec.tensor_tensor(sig_b[:, j % 2, :], sig_b[:, j % 2, :], psum[:, bank + 3, 0:SEQ], ALU.mult)\
                       .then_inc(gate_part, 1)
                    dve.wait_ge(gate_part, i * 4 + (j + 1))
                    vec.tensor_tensor(mg[:, j % 2, :], sig_a[:, j % 2, :], sig_b[:, j % 2, :], ALU.add).then_inc(gate_sum, 1)
                    dve.wait_ge(gate_sum, i * 4 + (j + 1))
                    hi = mg_hi[:, bass.ds(i * 4 + j, 1), :].rearrange("p o t -> p (o t)")
                    lo = mg_lo[:, bass.ds(i * 4 + j, 1), :].rearrange("p o t -> p (o t)")
                    vec.tensor_copy(hi, mg[:, j % 2, :]).then_inc(mhi_ready, 1)
                    dve.wait_ge(mhi_ready, i * 4 + (j + 1))
                    vec.tensor_tensor(lo, mg[:, j % 2, :], hi.bitcast(F32), ALU.subtract).then_inc(merged_ready, 1)

        for b in BLOCKS:
            modulate(b)
            if b["kind"] == "ffn":
                ffn_body(b)
            else:
                mixer(b)
                if b["kind"] == "b2":
                    gates(b)
            output(b)
        dve.wait_ge(rstd_h_ready, len(BLOCKS) + 1)
        for c in range(CH):
            g = COL["norm2"] + 3 * CH + c
            vec.scalar_tensor_tensor(out=final[:, c, :], in0=h[:, c, LAT], scalar=col[:, g:g + 1], in1=rstd_h[:, LAT],
                                     op0=ALU.mult, op1=ALU.mult).then_inc(out_ready, 1)

    @block.tensor
    def _(pe):
        mm = nc.tensor.matmul

        pe.wait_ge(silu_c_ready, 1)
        with pe.Fori(0, 2 * ADA_CHUNKS // 3) as i:
            for j in range(3):
                pe.wait_ge(m_evac, i * 3 + (j + 1))
                for half in range(2):
                    slot = 2 * j + half
                    pe.wait_ge(ada_landed[slot], i * 16 + 16)
                    for k4 in range(4):
                        k = 4 * half + k4
                        last = mm(psum[0:2, j, :], silu_c[:, k, :], ada_ring[:, slot, k4 * 512:(k4 + 1) * 512],
                                  start=(k == 0), stop=(k == CH - 1))
                    last.then_inc(ada_used, 1)
        pe.wait_ge(consts_in, 32)
        pe.wait_ge(m_biased, 4)
        for m in range(4):
            last = nc.tensor.transpose(psum[:, SHARED, m * MODS:(m + 1) * MODS], m_rows[0:MODS, m, :], tab[0:MODS, 0:MODS])
        last.then_inc(m_turned, 1)
        pe.wait_ge(set_up, 2)

        def blocks(slot, out, moving, ks, first=0, start=True, stop=True, ready=None):
            for n, k in enumerate(ks):
                if ready is not None:
                    pe.wait_ge(u_ready, ready + k + 1)
                w = slice((first + n) * 128, (first + n + 1) * 128)
                x_hi, x_lo = moving(k)
                mm(out, w_hi[:, slot, w], x_hi, start=start and n == 0, stop=False)
                mm(out, w_hi[:, slot, w], x_lo, start=False, stop=False)
                last = mm(out, w_lo[:, slot, w], x_hi, start=False, stop=stop and n == len(ks) - 1)
            return last

        def split(t, i=0, per=0):
            pe.wait_ge(lo_ready, i * per + (t + 1 + LO0))
            return t % RING

        def pre_norm(b):
            n, tok = b["n"], b["tok"]
            for c in range(CH):
                pe.wait_ge(hsq_ready, CH * n + c + 1)
                mm(psum[:, SSH, tok], ones[:, :], sq[:, c % 2, tok], start=c == 0, stop=c == CH - 1).then_inc(hsq_used, 1)

        def normed(tok):
            return lambda k: (u_hi[:, k, tok], u_lo[:, k, tok])

        def ffn_body(b):
            tok, t0 = b["tok"], b["t_body"]
            with pe.Fori(0, FCH // 2) as i:
                for j in range(2):
                    pe.wait_ge(g_ready, i * 2 + (FCH * b["f"] + j + 1))
                    for n in range(2):
                        t = t0 + 2 * j + n
                        blocks(split(t, i, 4), psum[:, 2 * j + n, tok], normed(tok), range(CH),
                               ready=CH * b["n"] if j + n == 0 else None).then_inc(tile_used, 1)

        def output(b):
            n, tok = b["n"], b["tok_out"]
            parts = out_parts(b["kind"])
            if b["kind"] == "ffn":
                pe.wait_ge(gu_ready, FCH * (b["f"] + 1) + PAIR0)
                moving = lambda k: (gu_hi[:, k, tok], gu_lo[:, k, tok])
            elif b["kind"] == "b2":
                pe.wait_ge(merged_ready, CH + PAIR0)
                moving = lambda k: (mg_hi[:, k, :], mg_lo[:, k, :])
            else:
                pe.wait_ge(MS[b["kind"]]["olo_ready"], 8)
                moving = lambda k: (o_hi[:, k, tok], o_lo[:, k, tok])
            with pe.Fori(0, 2) as i:
                for j in range(4):
                    if b["layer"] is None:
                        pe.wait_ge(h_ready, i * 4 + (CH * n + j - 1))
                    else:
                        pe.wait_ge(y_evac, i * 4 + (CH * n + j + 1))
                        pe.wait_ge(ysq_ready, i * 4 + (CH * n + j + 1))
                    for p, (k0, k1) in enumerate(parts):
                        t = b["t_out"] + len(parts) * j + p
                        blocks(split(t, i, 4 * len(parts)), psum[:, 4 + j % 2, tok], moving, range(k0, k1),
                               start=p == 0, stop=p == len(parts) - 1).then_inc(tile_used, 1)
            if b["layer"] is not None:
                pe.wait_ge(yacc_ready, CH * n + CH + PAIR0)
                mm(psum[:, SSY, tok], ones[:, :], sqsum[:, tok], start=True, stop=True).then_inc(yss_ready, 1)

        def mixer(b):
            kind = b["kind"]
            S = MS[kind]
            order, _ = plans[kind]
            n_o = 0
            biased = 0
            freed = {}

            def item_ready(it):
                if it["rope"]:
                    pe.wait_ge(S["qk_ready"], it["rope_n"])
                else:
                    pe.wait_ge(S["proj_evac"], it["idx"] + 1)

            def turn_wait(turn):
                if turn:
                    pe.wait_ge(S["turn_free"], turn)

            for op, x, turn in order:
                if op == "proj":
                    if x["idx"] >= 2:
                        pe.wait_ge(S["proj_evac"], x["idx"] - 1)
                    blocks(split(x["t"]), psum[:, x["idx"] % 2, x["tok"]], normed(x["tok"]), range(CH),
                           ready=CH * b["n"] if x["idx"] == 0 else None).then_inc(tile_used, 1)
                elif op == "ss":
                    pe.wait_ge(S["proj_evac"], x["idx"] + 1)
                    turn_wait(turn)
                    mm(psum[:, SHARED, x["tok"]], ones[:, :], n_sq[:, x["idx"] % 2, x["tok"]], start=True, stop=True)\
                        .then_inc(S["turn_ready"], 1)
                elif op == "rot":
                    if x["norm"]:
                        pe.wait_ge(S["normed"], x["norm_n"])
                    else:
                        pe.wait_ge(S["proj_evac"], x["idx"] + 1)
                    turn_wait(turn)
                    mm(psum[:, SHARED, 0:SEQ], rot, latents(x), start=True, stop=True).then_inc(S["turn_ready"], 1)
                elif op == "vtr":
                    pe.wait_ge(S["proj_evac"], x["idx"] + 1)
                    turn_wait(turn)
                    src = item_stage(x)
                    for kt in range(width(x["tok"]) // 128):
                        last = nc.tensor.transpose(psum[:, SHARED, kt * 128:(kt + 1) * 128],
                                                   src[:, kt * 128:(kt + 1) * 128], ident)
                    last.then_inc(S["turn_ready"], 1)
                elif op == "S":
                    U, st, n = x["U"], x["set"], x["keys"]
                    for it in st["q"] + st["k"]:
                        if U == st["first_unit"]:
                            item_ready(it)
                    if kind == "b2":
                        if U >= 2:
                            pe.wait_ge(S["biased"], freed[U - 2])
                        biased += len(st["v"])
                        freed[U] = biased
                    elif U >= 2:
                        pe.wait_ge(S["exp_done"], exps_through(kind, U - 2))
                    out = scores_of(kind, x)
                    if kind == "ga":
                        q = q_st[:, st["q"][0]["par"], x["qt"] * 128 - CTX:x["qt"] * 128 - CTX + 128]
                        last = mm(out, q, k_st[:, st["k"][0]["par"], 0:n], start=True, stop=True)
                    elif kind == "da":
                        for m in range(2):
                            rows = slice(64 * m, 64 * m + 64)
                            q = q_st[rows, st["q"][0]["par"], x["qt"] * 128:x["qt"] * 128 + 128]
                            last = mm(out[:, m, :], q, k_st[rows, st["k"][0]["par"], 0:n], start=True, stop=True)
                    else:
                        rows = slice(64 * x["j"], 64 * x["j"] + 64)
                        for g in range(len(st["v"])):
                            q0 = g * SEQ + x["qt"] * 128
                            last = mm(out[:, g * n:g * n + n], q_st[rows, st["q"][g]["par"], q0:q0 + 128],
                                      k_st[rows, st["k"][g]["par"], g * SEQ:g * SEQ + n], start=True, stop=True)
                    last.then_inc(S["s_ready"], 1)
                elif op == "T":
                    u, a, e = x
                    pe.wait_ge(S["pc_ready"], u["U"] + 1)
                    turn_wait(turn)
                    for n in range(a, e):
                        last = nc.tensor.transpose(psum[:, SHARED, (n - a) * 128:(n - a + 1) * 128],
                                                   pcomb[:, u["U"] % 2, n * 128:(n + 1) * 128], ident)
                    last.then_inc(S["turn_ready"], 1)
                elif op == "PV":
                    st, U = x["set"], x["U"]
                    pe.wait_ge(S["turn_free"], max([x["turn"]] + [it["turn"] for it in st["v"]]) + 1)
                    if U == st["first_unit"] and st["s"]:
                        if kind == "da":
                            pe.wait_ge(S["o_evac"], st["s"])
                            pe.wait_ge(S["osq_ready"], st["s"])
                        else:
                            pe.wait_ge(S["olo_ready"], st["s"])
                    for n, (g, kt) in enumerate(x["blocks"]):
                        last = mm(psum[:, PVB, x["ocol"]:x["ocol"] + 128], v_tile(st["v"][g], kt),
                                  probT[:, U % 2, n * 128:(n + 1) * 128], start=n == 0, stop=n == len(x["blocks"]) - 1)
                    last.then_inc(S["pv_ready"], 1)
                elif op == "oss":
                    pe.wait_ge(S["osq_ready"], x["s"] + 1)
                    turn_wait(turn)
                    mm(psum[:, SHARED, :], ones[:, :], o_sq[:, :], start=True, stop=True).then_inc(S["turn_ready"], 1)

        def gates(b):
            t0 = b["t_body"] + 30
            pe.wait_ge(MS["b2"]["olo_ready"], 6)
            branch = lambda k: (y_hi[:, k, :], y_lo[:, k, :])
            with pe.Fori(0, 2) as i:
                for j in range(4):
                    bank = 4 * (j % 2)
                    pe.wait_ge(merged_ready, i * 4 + (j + 1))
                    for n in range(2):
                        t = t0 + 3 * j + n
                        blocks(split(t, i, 12), psum[:, bank + n, 0:SEQ], normed(LAT), range(CH)).then_inc(tile_used, 1)
                    slot = split(t0 + 3 * j + 2, i, 12)
                    blocks(slot, psum[:, bank + 2, 0:SEQ], branch, range(0, 2))
                    blocks(slot, psum[:, bank + 3, 0:SEQ], branch, range(2, 6), first=2).then_inc(tile_used, 1)

        for b in BLOCKS:
            pre_norm(b)
            if b["kind"] == "ffn":
                ffn_body(b)
            else:
                mixer(b)
                if b["kind"] == "b2":
                    gates(b)
            output(b)
        pre_norm({"n": len(BLOCKS), "tok": LAT})

    block_cm.__exit__(None, None, None)


def _tiles(w):
    k, m = w.shape
    return np.ascontiguousarray(w.reshape(k // 128, 128, m // 128, 128).transpose(2, 1, 0, 3).reshape(m // 128, 128, k))


def _columns(v):
    return v.reshape(-1, CH, 128).transpose(2, 0, 1).reshape(128, -1)


def _tables():
    f32 = np.float32
    ident = np.eye(128, dtype=f32)
    rot = np.zeros((128, 128), f32)
    for j in range(64):
        rot[2 * j + 1, 2 * j] = -1.0
        rot[2 * j, 2 * j + 1] = 1.0

    def rope(dim):
        n = dim // 4
        pos = np.arange(SEQ)
        freqs = (f32(THETA) ** (-np.arange(n, dtype=f32) / f32(n))).astype(f32)
        ang = np.concatenate([(pos // GRID_W).astype(f32)[:, None] * freqs, (pos % GRID_W).astype(f32)[:, None] * freqs], 1)
        ang = np.repeat(ang, 2, axis=1)
        ang = np.tile(ang, (1, 128 // dim)).T
        return [np.cos(ang).astype(f32), np.sin(ang).astype(f32)]

    tables = np.concatenate([ident, rot, *rope(DA_QK), *rope(GA_DIM)], axis=1)
    qp, kp = np.arange(SEQ)[:, None], np.arange(SEQ)[None, :]
    delta = qp - kp

    def table(ok):
        return np.where(ok, -delta, f32(MASKED) * 1e3).astype(f32)

    dsa = [table((delta >= 0) & (delta <= w) & (delta % dil == 0)) for w, dil in DSA_GROUPS]
    moba = table(delta >= 0)
    parts = []
    for qt in range(2):
        parts += [d[qt * 128:qt * 128 + 128, 0:128 * (qt + 1)] for d in dsa]
    for qt in range(2):
        parts.append(moba[qt * 128:qt * 128 + 128, 0:128 * (qt + 1)])
    dist = np.concatenate(parts, axis=1)

    def slopes(n):
        return (f32(2.0) ** (f32(-8.0) * np.arange(1, n + 1, dtype=f32) / f32(n))).astype(f32)
    sl = np.concatenate([slopes(len(DSA_GROUPS) * DSA_HPG), slopes(MOBA_HEADS)])
    return np.ascontiguousarray(tables), np.ascontiguousarray(dist), np.broadcast_to(sl, (128, 20))


def kernel(**inputs):
    import concourse.bacc as bacc
    from concourse.bass_utils import run_bass_kernel_spmd

    I = {k: np.asarray(v) for k, v in inputs.items()}
    tables, dist, slopes = _tables()
    cond = np.stack([I["c"][0], I["c_ctx"]])
    col = np.concatenate([
        _columns(I["norm_g"]),
        _columns(np.stack([I["norm_ffn1_2"][0], I["norm_mix_2"][0], I["norm_ffn2_2"][0], I["norm_final_2"]])),
        I["da_subln"].reshape(128, 1), I["ga_q_norm"].reshape(128, 1), I["ga_k_norm"].reshape(128, 1), slopes,
        np.broadcast_to(I["da_lambda"].reshape(1, -1), (128, 4 * DA_QK)),
        cond.reshape(2, CH, 128).transpose(2, 1, 0).reshape(128, 2 * CH)], axis=1)
    X = {"columns": col, "tables": tables, "dist": dist}
    X["hT"] = np.concatenate([I["ctx"][0], I["x"][0]]).reshape(TOK, CH, 128).transpose(2, 1, 0)
    ada = I["ada_w"].reshape(2, 2, 4, 128, ADA_CHUNKS, 512).transpose(0, 4, 1, 3, 2, 5)
    X["ada_w"] = ada.reshape(2 * ADA_CHUNKS * 2, 128, ADA_TILE)
    X["ada_b"] = I["ada_b"].reshape(2, MODS, 128).transpose(1, 0, 2)
    win = [I["ffn_w_in"][l, p] for l in range(2) for p in range(2)]
    win += [np.concatenate([I[f"ffn{n}_gate_2"][0], I[f"ffn{n}_up_2"][0]], axis=1) for n in (1, 2)]
    wout = [I["ffn_w_out"][l, p] for l in range(2) for p in range(2)] + [I["ffn1_down_2"][0], I["ffn2_down_2"][0]]
    for f in range(6):
        X[f"ffn_in{f}"] = _tiles(win[f]).reshape(2, FCH, 128, TW).transpose(1, 0, 2, 3).reshape(2 * FCH, 128, TW)
        X[f"ffn_out{f}"] = _tiles(wout[f])
    X["da_in"] = _tiles(I["da_w_in"][0]).reshape(3, DA_HEADS, 128, TW).transpose(1, 0, 2, 3).reshape(3 * DA_HEADS, 128, TW)
    X["da_out"] = _tiles(I["da_w_out"][0])
    ga = _tiles(I["ga_w_in"][0])
    per = GA_HEADS // GA_KV
    X["ga_in"] = ga[[n for g in range(GA_KV) for n in (GA_HEADS + g, GA_HEADS + GA_KV + g, *range(per * g, per * g + per))]]
    X["ga_out"] = _tiles(I["ga_w_out"][0])
    w2 = _tiles(I["w_in_2"][0])
    X["b2_qkv"] = w2[[6 * w + 2 * g + s for s in range(2) for g in range(3) for w in range(3)]
                     + [18 + 4 * w + c for c in range(4) for w in range(3)]]
    X["b2_gate"] = w2[30:46].reshape(2, CH, 128, TW).transpose(1, 0, 2, 3)
    X["b2_up"] = np.concatenate([_tiles(I["w_up_a_2"][0]), _tiles(I["w_up_b_2"][0])], axis=2)
    X["b2_out"] = _tiles(I["w_out_2"][0])

    nc = bacc.Bacc("TRN2", target_bir_lowering=False, num_devices=1)
    arrays, A = {}, {}
    for name, a in X.items():
        arrays[f"in_{name}"] = np.ascontiguousarray(a)
        A[name] = nc.dram_tensor(f"in_{name}", list(a.shape), mybir.dt.float32, kind="ExternalInput").ap()
    A["out"] = nc.dram_tensor("out", [128, CH, SEQ], mybir.dt.float32, kind="ExternalOutput").ap()
    build(nc, A)
    r = run_bass_kernel_spmd(nc, [arrays], core_ids=[0])
    got = r.results[0]["out"]
    return np.ascontiguousarray(got.transpose(2, 1, 0).reshape(1, SEQ, D))
```

```python
import numpy as np

import concourse.bass as bass
import concourse.mybir as mybir

D = 1024
CH = D // 128
CTX, SEQ = 256, 256
TOK = CTX + SEQ
FULL, LAT = slice(0, TOK), slice(CTX, TOK)
DFF = 2816
FCH = DFF // 128
EPS = 1e-6
MASKED = -1e30
GRID_W = 64
THETA = 10000.0
RING = 4
TW = 1024

DA_HEADS, DA_QK = 8, 64
GA_HEADS, GA_KV, GA_DIM = 8, 2, 128
DSA_GROUPS = ((128, 1), (512, 4), (2048, 16))
DSA_HPG = 4
MOBA_HEADS, HEAD64 = 8, 64
LAMBDA_INIT = 0.2

MODS = 9 * CH
ADA_SLOTS = 4
ADA_FIRST = 2 * CH
ADA_FREE = 4

COL = {}
_at = 0
for _name, _n in (("norm_g", 2 * 6 * CH), ("norm2", 4 * CH), ("subln", 1), ("qnorm", 1), ("knorm", 1),
                  ("slopes", 20), ("lambda", 4 * DA_QK), ("ada_b", 2 * MODS)):
    COL[_name] = _at
    _at += _n
NCOL = _at
TAB = {"ident": 0, "rot": 128, "da_cos": 256, "da_sin": 512, "ga_cos": 768, "ga_sin": 1024}
NTAB = 1280
DIST = {("dsa", 0): 0, ("dsa", 1): 384, ("moba", 0): 1152, ("moba", 1): 1280}
NDIST = 1536


def sub_blocks():
    spec = [("ffn", FULL, FULL, 0, 0), ("da", FULL, FULL, 0, 1), ("ffn", FULL, FULL, 0, 2),
            ("ffn", FULL, FULL, 1, 0), ("ga", FULL, LAT, 1, 1), ("ffn", LAT, LAT, 1, 2),
            ("ffn", LAT, LAT, None, 0), ("b2", LAT, LAT, None, 1), ("ffn", LAT, LAT, None, 2)]
    ada, at = {}, ADA_FIRST
    for n, body in ((0, (FCH - ADA_FREE) // 2), (2, (FCH - ADA_FREE) // 2), (3, None)):
        out_steps = 2 if body is not None else 0
        body = body if body is not None else (2 * MODS - at) // 4
        ada[n] = (at, body, out_steps)
        at += 4 * body + 8 * out_steps
    assert at == 2 * MODS
    body_tiles = {"ffn": 2 * FCH, "da": 3 * DA_HEADS, "ga": 2 * GA_KV + GA_HEADS, "b2": 30 + 3 * CH}
    out, t, f = [], 0, 0
    for n, (kind, tok_in, tok_out, layer, part) in enumerate(spec):
        b = {"n": n, "kind": kind, "tok": tok_in, "tok_out": tok_out, "layer": layer, "part": part,
             "t_body": t, "t_out": t + body_tiles[kind], "f": f, "ada": ada.get(n, (0, 0, 0))}
        b["out_tiles"] = 3 * CH if kind == "ffn" else CH
        t = b["t_out"] + b["out_tiles"]
        f += kind == "ffn"
        out.append(b)
    return out, t


def out_parts(kind):
    return [(0, 8), (8, 15), (15, 22)] if kind == "ffn" else [(0, 8)]


def mixer_plan(kind, t0):
    sets, t, idx, U = [], t0, 0, 0

    def item(what, s, g, tok, **more):
        nonlocal t, idx
        it = {"what": what, "s": s, "g": g, "tok": tok, "t": t, "idx": idx, "norm": False, "rope": False, **more}
        t, idx = t + 1, idx + 1
        return it

    if kind == "da":
        for h in range(DA_HEADS):
            items = [item("q", h, 0, FULL, rope=True, par=h % 2), item("k", h, 0, FULL, rope=True, par=h % 2),
                     item("v", h, 0, FULL, par=h % 2)]
            sets.append({"s": h, "items": items, "q": items[:1], "k": items[1:2], "v": items[2:],
                         "units": [{"qt": qt, "keys": keys, "ocol": qt * 128} for qt, keys in
                                   ((2, TOK), (3, TOK), (0, CTX), (1, CTX))]})
    elif kind == "ga":
        kv = None
        for h in range(GA_HEADS):
            g = h // (GA_HEADS // GA_KV)
            items = []
            if h % (GA_HEADS // GA_KV) == 0:
                kv = [item("k", h, 0, FULL, norm=True, rope=True, par=g % 2), item("v", h, 0, FULL, par=g % 2)]
                items += kv
            items.append(item("q", h, 0, LAT, norm=True, rope=True, par=0, place=h % 3))
            sets.append({"s": h, "items": items, "q": items[-1:], "k": kv[:1], "v": kv[1:],
                         "units": [{"qt": qt, "keys": TOK, "ocol": qt * 128} for qt in (2, 3)]})
    else:
        for s in range(6):
            ng = 3 if s < 2 else 1
            items = [item(w, s, g, LAT, par=s % 2) for g in range(ng) for w in "qkv"]
            sets.append({"s": s, "items": items, "q": items[0::3], "k": items[1::3], "v": items[2::3],
                         "units": [{"qt": qt, "j": j, "keys": 128 * (qt + 1), "ocol": (2 * j + qt) * 128}
                                   for qt in (1, 0) for j in (0, 1)]})
    for st in sets:
        st["first_unit"] = U
        for u in st["units"]:
            u.update(U=U, set=st, tiles=u["keys"] // 128)
            U += 1
        st["last_unit"] = U - 1

    order, turns, ropes, norms, clock, pending = [], 0, 0, 0, 0, []

    def add(op, x):
        nonlocal turns, ropes, norms
        entry = [op, x, None]
        if op in ("ss", "rot", "vtr", "T", "oss"):
            entry[2] = turns
            turns += 1
        if op == "rot":
            ropes += 1
            x["rope_n"] = ropes
        if op == "ss":
            norms += 1
            x["norm_n"] = norms
        if op in ("ss", "vtr", "oss"):
            x["turn"] = entry[2]
        order.append(entry)

    def add_T(u):
        u["blocks"] = [(g, kt) for g in range(len(u["set"]["v"])) for kt in range(u["tiles"])]
        for a in range(0, len(u["blocks"]), 4):
            add("T", (u, a, min(a + 4, len(u["blocks"]))))
        u["turn"] = turns - 1

    def add_part(part):
        nonlocal clock
        add("proj", part)
        clock += 1
        it, _, k1 = part
        if k1 == CH:
            if it["norm"] or it["rope"] or it["what"] == "v":
                pending.append(("ss" if it["norm"] else "rot" if it["rope"] else "vtr", it, clock + 1))

    def prepare(n):
        op, it, _ = pending.pop(n)
        add(op, it)
        if op == "ss":
            pending.append(("rot", it, clock + 2))

    def prepare_due():
        for n, (_, _, due) in enumerate(pending):
            if due <= clock:
                prepare(n)
                return

    def prepare_all(of):
        while True:
            n = next((n for n, (_, it, _) in enumerate(pending) if any(it is o for o in of)), None)
            if n is None:
                return
            prepare(n)

    def parts(s):
        return [(it, k, k + 2) for it in sets[s]["items"] for k in range(0, CH, 2)] if s < len(sets) else []

    ahead = 2 if kind == "ga" else 1
    for s in range(ahead):
        for part in parts(s):
            add_part(part)
            prepare_due()
    units = [u for st in sets for u in st["units"]]
    LAG = 2
    for U in range(len(units) + LAG):
        u = units[U] if U < len(units) else None
        old = units[U - LAG] if U >= LAG else None
        mine = []
        if u:
            st = u["set"]
            nxt, n, nu = parts(st["s"] + ahead), U - st["first_unit"], len(st["units"])
            mine = nxt[n * len(nxt) // nu:(n + 1) * len(nxt) // nu]
        third = -(-len(mine) // 3)
        if old:
            add_T(old)
        if 1 <= U <= len(units):
            add("C", units[U - 1])
        for part in mine[:third]:
            add_part(part)
        prepare_due()
        if u:
            if U == st["first_unit"]:
                prepare_all(st["q"] + st["k"])
            add("S", u)
        for part in mine[third:2 * third]:
            add_part(part)
        prepare_due()
        if old:
            if old["U"] == old["set"]["first_unit"]:
                prepare_all(old["set"]["v"])
            add("PV", old)
            if old["U"] == old["set"]["last_unit"]:
                if old["set"]["s"]:
                    prepare_all(sets[old["set"]["s"] - 1:old["set"]["s"]])
                add("O", old["set"])
                if kind == "da":
                    pending.append(("oss", old["set"], clock + 2))
        for part in mine[2 * third:]:
            add_part(part)
            prepare_due()
        prepare_due()
    prepare_all([it for _, it, _ in pending])
    return order, idx


def build(nc, A):
    F32, F32R = mybir.dt.float32, mybir.dt.float32r
    ACT, ALU, AX = mybir.ActivationFunctionType, mybir.AluOpType, mybir.AxisListType
    BLOCKS, N_TILES = sub_blocks()
    EXP_SET, SILU_SET, SIG_SET = "natural_log_exp_and_others", "silu_and_others", "sigmoid_and_others"

    base = (nc.sbuf_base + 63) // 64 * 64
    H0 = base
    U0 = H0 + CH * TOK * 4
    GU0 = U0 + 2 * CH * TOK * 4
    RING0 = GU0 + 2 * FCH * TOK * 4
    MISC0 = RING0 + 3 * RING * TW * 4

    def region(start):
        at = [start]

        def take(name, shape, dt=F32):
            t = nc.alloc_sbuf_tensor_at(name, [128, *shape], dt, offset=at[0])
            at[0] += (int(np.prod(shape)) * 4 + 31) // 32 * 32
            return t
        return take, at

    take, _ = region(H0)
    h = take("h", [CH, TOK])
    take, _ = region(U0)
    u_hi, u_lo = take("u_hi", [CH, TOK], F32R), take("u_lo", [CH, TOK], F32R)
    take, _ = region(U0)
    y = take("y", [CH, TOK])
    take, _ = region(U0)
    final = take("final", [CH, SEQ])
    take, _ = region(GU0)
    gu_hi, gu_lo = take("gu_hi", [FCH, TOK], F32R), take("gu_lo", [FCH, TOK], F32R)
    take, _ = region(U0)
    ada_first = take("ada_first", [ADA_FIRST, D])
    lam_t = take("lam_t", [2, DA_QK])
    take, _ = region(GU0 + (FCH - ADA_FREE) * TOK * 4)
    ada_hi = take("ada_hi", [2, D])
    take, _ = region(GU0 + (2 * FCH - ADA_FREE) * TOK * 4)
    ada_lo = take("ada_lo", [2, D])
    take, _ = region(U0 + CH * TOK * 4)
    ada_out = take("ada_out", [ADA_SLOTS, D])
    take, _ = region(GU0)
    v1 = take("v1", [2, TOK])
    ufull = take("ufull", [2, TOK])
    take, at = region(GU0)
    q_st, k_st = take("q_st", [2, 768]), take("k_st", [2, 768])
    vT = take("vT", [768])
    v_st = take("v_st", [2, 768])
    prob = take("prob", [2, 1024])
    pcomb = take("pcomb", [2, 768])
    probT = take("probT", [2, 768])
    rope_a, rope_b = take("rope_a", [SEQ]), take("rope_b", [SEQ])
    MIX0 = at[0]
    o_hi, o_lo = take("o_hi", [CH, TOK], F32R), take("o_lo", [CH, TOK], F32R)
    o_raw, o_sq, rs = take("o_raw", [TOK]), take("o_sq", [TOK]), take("rs", [TOK])
    n_sq = take("n_sq", [2, TOK])
    assert at[0] <= RING0
    take, at = region(MIX0)
    y_hi, y_lo = take("y_hi", [6, SEQ], F32R), take("y_lo", [6, SEQ], F32R)
    mg_hi, mg_lo = take("mg_hi", [CH, SEQ], F32R), take("mg_lo", [CH, SEQ], F32R)
    dist = take("dist", [NDIST])
    sbias = take("sbias", [2, 768])
    assert at[0] <= RING0
    take, _ = region(MIX0 - (2 * SEQ + 2 * 768 + 2 * 768 + 2048) * 4)
    sig_a, sig_b, mg = take("sig_a", [2, SEQ]), take("sig_b", [2, SEQ]), take("mg", [2, SEQ])
    take, _ = region(RING0)
    w_raw = take("w_raw", [RING, TW])
    w_hi, w_lo = take("w_hi", [RING, TW], F32R), take("w_lo", [RING, TW], F32R)
    take, at = region(MISC0)
    tab = take("tab", [NTAB])
    col = take("col", [NCOL])
    mcol = take("mcol", [2, 2 * MODS])
    a_col, g_col = take("a_col", [12, CH]), take("g_col", [12, CH])
    ones = take("ones", [128])
    rstd = take("rstd", [TOK])
    sqsum = rstd
    sq = take("sq", [2, TOK])
    s_up = sq
    ada_sum = take("ada_sum", [2, 2])
    silu_c = take("silu_c", [2, D])
    stat = take("stat", [4, 8])
    small = take("small", [16])
    assert at[0] <= nc.sbuf_usable_end, at[0] - nc.sbuf_usable_end
    psum = nc.alloc_psum_tensor("psum", [128, 8, 512], F32)
    SHARED, PVB, SSY, SSH = 3, 2, 6, 7

    ident, rot = tab[:, 0:128], tab[:, 128:256]
    eps = small[:, 0:1]
    neg_lam = small[:, 1:2]

    sem = nc.alloc_semaphore
    raw_landed = [sem(f"raw_landed{i}") for i in range(RING)]
    ada_landed = [sem(f"ada_landed{i}") for i in range(ADA_SLOTS)]
    hi_ready, lo_ready, tile_used = sem("hi_ready"), sem("lo_ready"), sem("tile_used")
    cond_in, tables_in, consts_in, h_in, dist_in = sem("cond_in"), sem("tables_in"), sem("consts_in"), sem("h_in"), sem("dist_in")
    set_up = sem("set_up")
    silu_c_ready, ada_dot, m_done, coefs = sem("silu_c_ready"), sem("ada_dot"), sem("m_done"), sem("coefs")
    lam_sum, lam_exp, lam_ready, lam_step = sem("lam_sum"), sem("lam_exp"), sem("lam_ready"), sem("lam_step")
    h_ready, hsq_ready, hsq_used = sem("h_ready"), sem("hsq_ready"), sem("hsq_used")
    ln_done, rstd_h_ready, rstd_y_ready = sem("ln_done"), sem("rstd_h_ready"), sem("rstd_y_ready")
    v1_ready, uhi_ready, u_ready = sem("v1_ready"), sem("uhi_ready"), sem("u_ready")
    silu_ready, g_ready, ghi_ready, gu_ready = sem("silu_ready"), sem("g_ready"), sem("ghi_ready"), sem("gu_ready")
    y_evac, ysq_ready, yacc_ready, yss_ready = sem("y_evac"), sem("ysq_ready"), sem("yacc_ready"), sem("yss_ready")
    sqsum_zero, ymul_ready = sem("sqsum_zero"), sem("ymul_ready")
    out_ready, out_done = sem("out_ready"), sem("out_done")
    MS = {}
    for kind in ("da", "ga", "b2"):
        MS[kind] = {name: sem(f"{kind}_{name}") for name in (
            "proj_evac", "turn_ready", "turn_free", "rs_ready", "normed", "qk_ready", "s_ready", "biased",
            "max_part", "max_ready", "exp_done", "recip", "comb_part", "pc_ready", "pv_ready", "osq_ready",
            "o_evac", "on_ready", "ohi_ready", "olo_ready")}
    sig_ready, gate_part, gate_sum, mhi_ready, merged_ready = (sem("sig_ready"), sem("gate_part"), sem("gate_sum"),
                                                               sem("mhi_ready"), sem("merged_ready"))

    LO0, USED0, PAIR0, ADA0 = RING, RING, 2, 1

    def conds(b):
        if b["layer"] is None:
            return [(b["tok"], None)]
        both = [(slice(0, CTX), 2 * b["layer"] + 1), (LAT, 2 * b["layer"])]
        return both if b["tok"] == FULL else both[1:]

    def width(tok):
        return tok.stop - tok.start

    def ada_tile(phase, slot):
        if phase == "output":
            return ada_out[:, slot, :]
        return (ada_hi if slot < 2 else ada_lo)[:, slot % 2, :]

    plans = {b["kind"]: mixer_plan(b["kind"], b["t_body"]) for b in BLOCKS if b["kind"] != "ffn"}

    def item_stage(it):
        n = width(it["tok"])
        off = it.get("place", it["g"]) * SEQ
        if it["what"] == "v":
            return vT[:, off:off + n]
        return (q_st if it["what"] == "q" else k_st)[:, it["par"], off:off + n]

    def latents(it):
        n = width(it["tok"])
        off = it.get("place", it["g"]) * SEQ + n - SEQ
        return (q_st if it["what"] == "q" else k_st)[:, it["par"], off:off + SEQ]

    def v_tile(it, kt):
        off = it["g"] * SEQ + kt * 128
        return v_st[:, it["par"], off:off + 128]

    def scores_of(kind, u):
        b0 = 4 + 2 * (u["U"] % 2)
        if kind == "da":
            return psum[:, b0:b0 + 2, 0:u["keys"]]
        n = u["keys"] * len(u["set"]["v"])
        return psum[:, b0:b0 + 2, :].rearrange("p a b -> p (a b)")[:, 0:n]

    def pv_bank(kind, s):
        return 5 if kind == "ga" and s % 2 else PVB

    def slope_col(kind, u, g):
        s = u["set"]["s"]
        n = DSA_HPG * g + 2 * s + u["j"] if s < 2 else len(DSA_GROUPS) * DSA_HPG + 2 * (s - 2) + u["j"]
        c = COL["slopes"] + n
        return col[:, c:c + 1]

    def exps_through(kind, U):
        return (2 if kind == "da" else 1) * (U + 1)

    block_cm = nc.Block()
    block = block_cm.__enter__()

    @block.sync
    def _(sp):
        sp.dma_start(silu_c[:, :, :], A["cond"]).then_inc(cond_in, 16)
        sp.dma_start(col[:, :], A["columns"]).then_inc(consts_in, 16)
        per = ADA_FIRST // ADA_SLOTS
        for s in range(ADA_SLOTS):
            sp.dma_start(ada_first[:, s * per:(s + 1) * per, :],
                         A["ada_w"][s * per:(s + 1) * per].rearrange("n p c -> p n c")).then_inc(ada_landed[s], 16)
            if s == 0:
                sp.dma_start(h[:, :, :], A["hT"]).then_inc(h_in, 16)
        sp.dma_start(tab[:, :], A["tables"]).then_inc(tables_in, 16)

        def load_ada(phase, n, slot, i=0, per=0):
            sp.wait_ge(ada_dot, i * (2 * per) + (2 * (n - ADA_SLOTS + 1) + ADA0))
            src = A["ada_w"][bass.ds(i * per + n, 1)].rearrange("o p c -> p (o c)")
            sp.dma_start(ada_tile(phase, slot), src).then_inc(ada_landed[slot], 16)

        def load(src, t, slot, cols):
            sp.wait_ge(lo_ready, t + 1)
            sp.dma_start(w_raw[:, slot, 0:cols], src).then_inc(raw_landed[slot], 16)

        def load_whole(dram, t0, count, ada=None):
            loops = count // RING
            first = 0
            if ada:
                n0, first, _ = ada

                for x in range(2):
                    load(dram[x], t0 + x, (t0 + x) % RING, TW)
                sp.wait_ge(tile_used, t0 + USED0)
                with sp.Fori(0, first) as i:
                    for j in range(2):
                        for x in range(2):
                            load_ada("body", n0 + 2 * j + x, 2 * j + x, i, 4)
                        for x in range(2):
                            n = 2 * j + x + 2
                            src = dram[bass.ds(i * RING + n, 1)].rearrange("o p c -> p (o c)")
                            load(src, i * RING + (t0 + n), (t0 + n) % RING, TW)
                for n in range(first * RING + 2, first * RING + RING):
                    load(dram[n], t0 + n, (t0 + n) % RING, TW)
                first += 1
            with sp.Fori(0, loops - first) as i:
                for j in range(RING):
                    src = dram[bass.ds(i * RING + (first * RING + j), 1)].rearrange("o p c -> p (o c)")
                    load(src, i * RING + (t0 + first * RING + j), (t0 + j) % RING, TW)
            for n in range(loops * RING, count):
                load(dram[n], t0 + n, (t0 + n) % RING, TW)

        for b in BLOCKS:
            if b["kind"] == "ffn":
                n0, body_steps, out_steps = b["ada"]
                load_whole(A[f"ffn_in{b['f']}"], b["t_body"], 2 * FCH, b["ada"] if body_steps else None)
                with sp.Fori(0, 2) as i:
                    for j in range(4):
                        row = A[f"ffn_out{b['f']}"][bass.ds(i * 4 + j, 1)].rearrange("o p c -> p (o c)")
                        for n, (k0, k1) in enumerate(out_parts("ffn")):
                            t = b["t_out"] + 3 * j + n
                            load(row[:, k0 * 128:k1 * 128], i * 12 + t, t % RING, (k1 - k0) * 128)
                        if out_steps:
                            n1 = n0 + 4 * body_steps
                            sp.wait_ge(tile_used, b["t_out"] + USED0)
                            sp.wait_ge(ada_dot, 2 * n1 + ADA0)
                            for x in range(2):
                                load_ada("output", n1 + 2 * j + x, (2 * j + x) % ADA_SLOTS, i, 8)
            elif b["kind"] == "b2":
                load_whole(A["b2_qkv"], b["t_body"], RING)
                sp.wait_ge(tile_used, b["t_body"] + USED0)
                sp.dma_start(dist[:, :], A["dist"]).then_inc(dist_in, 16)
                load_whole(A["b2_qkv"][RING:], b["t_body"] + RING, 30 - RING)
                t0 = b["t_body"] + 30
                with sp.Fori(0, 2) as i:
                    for j in range(4):
                        gates = A["b2_gate"][bass.ds(i * 4 + j, 1)].rearrange("o g p c -> p (o g) c")
                        up = A["b2_up"][bass.ds(i * 4 + j, 1)].rearrange("o p c -> p (o c)")
                        for n, (src, cols) in enumerate(((gates[:, 0, :], TW), (gates[:, 1, :], TW), (up, 6 * 128))):
                            load(src, i * 12 + (t0 + 3 * j + n), (t0 + 3 * j + n) % RING, cols)
                load_whole(A["b2_out"], b["t_out"], CH)
            else:
                load_whole(A[b["kind"] + "_in"], b["t_body"], b["t_out"] - b["t_body"])
                load_whole(A[b["kind"] + "_out"], b["t_out"], CH)
        for half in range(2):
            sp.wait_ge(out_ready, 4 * half + 4)
            c = slice(4 * half, 4 * half + 4)
            sp.dma_start(A["out"][:, c, :], final[:, c, :]).then_inc(out_done, 16)
        sp.wait_ge(out_done, 32)

    @block.gpsimd
    def _(pool):
        def rest(t, slot):
            pool.wait_ge(hi_ready, t + 1)
            pool.wait_ge(tile_used, t + 1)
            pool.tensor_tensor(w_lo[:, slot, :], w_raw[:, slot, :], w_hi[:, slot, :].bitcast(F32),
                               ALU.subtract).then_inc(lo_ready, 1)

        loops = N_TILES // RING
        with pool.Fori(0, loops) as i:
            for j in range(RING):
                rest(i * RING + j, j)
        for t in range(loops * RING, N_TILES):
            rest(t, t % RING)

    @block.scalar
    def _(act):
        logs = [0]
        scalar = nc.scalar

        def head(t, slot, cols=TW, i=0, per=0):
            act.wait_ge(raw_landed[slot], i * (per // RING * 16) + 16 * (t // RING + 1))
            scalar.activation(w_hi[:, slot, 0:cols], w_raw[:, slot, 0:cols], ACT.Copy).then_inc(hi_ready, 1)

        def tile_done(t, i=0, per=0):
            act.wait_ge(tile_used, i * per + (t + 1 + USED0))

        def refill(t, i=0, per=0, last=False):
            if not last:
                head(t + RING, (t + RING) % RING, TW, i, per)

        def rstd_of(out, ss, count, scale, ready, freed=None):
            ln = scalar.activation(out, ss, ACT.Ln, bias=eps, scale=scale)
            if freed is not None:
                ln.then_inc(freed, 1)
                act.wait_ge(freed, count)
            else:
                ln.then_inc(ln_done, 1)
                logs[0] += 1
                act.wait_ge(ln_done, logs[0])
            scalar.activation(out, out, ACT.Exp, scale=-0.5).then_inc(ready, 1)

        act.wait_ge(cond_in, 16)
        scalar.preload_act_table_set(SILU_SET)
        scalar.activation(silu_c[:, :, :], silu_c[:, :, :], ACT.Silu).then_inc(silu_c_ready, 1)
        scalar.preload_act_table_set(EXP_SET)
        act.wait_ge(lam_sum, 2)
        scalar.activation(small[:, 4:6], small[:, 2:4], ACT.Exp).then_inc(lam_exp, 1)

        def pre_norm(b):
            n, tok = b["n"], b["tok"]
            if n == 0:
                act.wait_ge(h_in, 16)
                act.wait_ge(set_up, 2)
            for c in range(CH):
                if n:
                    act.wait_ge(h_ready, CH * (n - 1) + c + 1)
                if c >= 2:
                    act.wait_ge(hsq_used, CH * n + c - 1)
                scalar.activation(sq[:, c % 2, tok], h[:, c, tok], ACT.Square).then_inc(hsq_ready, 1)
            act.wait_ge(hsq_used, CH * n + CH)
            rstd_of(rstd[:, tok], psum[:, SSH, tok], None, 1.0 / D, rstd_h_ready)

        def modulate(b):
            n, tok = b["n"], b["tok"]
            for c in range(CH):
                act.wait_ge(v1_ready, CH * n + c + 1)
                if b["layer"] is None:
                    scalar.activation(u_hi[:, c, tok], v1[:, c % 2, tok], ACT.Copy).then_inc(uhi_ready, 1)
                    continue
                if c >= 2:
                    act.wait_ge(u_ready, CH * n + c - 1)
                for part, m in conds(b):
                    shift = MODS * b["layer"] + 3 * b["part"] * CH + c
                    shift = mcol[:, m % 2, shift:shift + 1]
                    scalar.activation(ufull[:, c % 2, part], v1[:, c % 2, part], ACT.Identity, bias=shift)
                    last = scalar.activation(u_hi[:, c, part], v1[:, c % 2, part], ACT.Identity, bias=shift)
                last.then_inc(uhi_ready, 1)

        def ffn_body(b):
            tok, f, t0 = b["tok"], b["f"], b["t_body"]
            scalar.preload_act_table_set(SILU_SET)
            with act.Fori(0, FCH // 2) as i:
                for j in range(2):
                    gate, up = t0 + 2 * j, t0 + 2 * j + 1
                    tile_done(gate, i, 4)
                    act.wait_ge(gu_ready, i * 2 + (FCH * f + j + 1))
                    scalar.activation(s_up[:, j, tok], psum[:, 2 * j, tok], ACT.Silu).then_inc(silu_ready, 1)
                    refill(gate, i, 4)
                    tile_done(up, i, 4)
                    refill(up, i, 4)
            scalar.preload_act_table_set(EXP_SET)

        def output(b):
            n, tok = b["n"], b["tok_out"]
            gated = b["layer"] is not None
            parts = out_parts(b["kind"])
            per = 4 * len(parts)

            def chunks(i, end):
                for j in range(4):
                    for p in range(len(parts)):
                        t = b["t_out"] + len(parts) * j + p
                        tile_done(t, i, per)
                        if gated and p == len(parts) - 1:
                            act.wait_ge(yacc_ready, i * 4 + (CH * n + j + 1))
                            scalar.activation(sq[:, j % 2, tok], psum[:, 4 + j % 2, tok], ACT.Square)\
                                  .then_inc(ysq_ready, 1)
                        refill(t, i, per, last=end and t + per + RING >= N_TILES)

            if b["t_out"] + b["out_tiles"] == N_TILES:
                chunks(0, False)
                chunks(1, True)
            else:
                with act.Fori(0, 2) as i:
                    chunks(i, False)
            if gated:
                act.wait_ge(yss_ready, n + 1)
                rstd_of(rstd[:, tok], psum[:, SSY, tok], None, 1.0 / D, rstd_y_ready)

        def mixer(b):
            kind = b["kind"]
            S = MS[kind]
            order, _ = plans[kind]
            scale = {"da": DA_QK ** -0.5, "ga": GA_DIM ** -0.5, "b2": 1.0}[kind]
            normed, last_oss = 0, None
            ss_turn = {}
            for op, x, turn in order:
                if op == "proj":
                    x, _, k1 = x
                    if k1 < CH:
                        continue
                    tile_done(x["t"])
                    src = psum[:, x["idx"] % 2, x["tok"]]
                    dst = item_stage(x)
                    if x["norm"]:
                        if x["idx"] - 2 in ss_turn:
                            act.wait_ge(S["turn_ready"], ss_turn[x["idx"] - 2] + 1)
                        ss_turn[x["idx"]] = x["turn"]
                        scalar.activation(dst, src, ACT.Copy)
                        scalar.activation(n_sq[:, x["idx"] % 2, x["tok"]], src, ACT.Square).then_inc(S["proj_evac"], 1)
                    else:
                        s = HEAD64 ** -0.5 if kind == "b2" and x["what"] == "q" else 1.0
                        scalar.activation(dst, src, ACT.Copy, scale=s).then_inc(S["proj_evac"], 1)
                    refill(x["t"])
                elif op == "ss":
                    act.wait_ge(S["turn_ready"], turn + 1)
                    if normed:
                        act.wait_ge(S["normed"], normed)
                    normed += 1
                    rstd_of(rs[:, x["tok"]], psum[:, SHARED, x["tok"]], turn + 1, 1.0 / GA_DIM, S["rs_ready"], S["turn_free"])
                elif op == "S":
                    U = x["U"]
                    act.wait_ge(S["max_ready"], U + 1)
                    if U >= 2:
                        act.wait_ge(S["pc_ready"], U - 1)
                    n = x["keys"] * (len(x["set"]["v"]) if kind == "b2" else 1)
                    for m in range(2 if kind == "da" else 1):
                        if kind == "da":
                            src = scores_of(kind, x)[:, m, :]
                        else:
                            src = scores_of(kind, x) if kind == "ga" else sbias[:, U % 2, 0:n]
                        scalar.activation(prob[:, U % 2, m * 512:m * 512 + n], src, ACT.Exp,
                                          bias=stat[:, U % 4, 2 + m:3 + m], scale=scale,
                                          accum_out=stat[:, U % 4, 4 + m:5 + m]).then_inc(S["exp_done"], 1)
                elif op == "T":
                    u, a, e = x
                    act.wait_ge(S["turn_ready"], turn + 1)
                    scalar.activation(probT[:, u["U"] % 2, a * 128:e * 128], psum[:, SHARED, 0:(e - a) * 128],
                                      ACT.Copy).then_inc(S["turn_free"], 1)
                elif op == "O":
                    act.wait_ge(S["pv_ready"], x["last_unit"] + 1)
                    s = x["s"]
                    if kind == "da":
                        if last_oss is not None:
                            act.wait_ge(S["turn_ready"], last_oss + 1)
                        last_oss = x["turn"]
                        scalar.activation(o_sq[:, :], psum[:, PVB, :], ACT.Square).then_inc(S["osq_ready"], 1)
                    elif kind == "ga":
                        scalar.activation(o_hi[:, s, LAT], psum[:, pv_bank(kind, s), LAT], ACT.Copy).then_inc(S["ohi_ready"], 1)
                    else:
                        for j in range(2):
                            p = slice(64 * j, 64 * j + 64)
                            last = scalar.activation(y_hi[p, s, :], psum[p, PVB, 256 * j:256 * j + 256], ACT.Copy)
                        last.then_inc(S["ohi_ready"], 1)
                elif op == "oss":
                    act.wait_ge(S["turn_ready"], turn + 1)
                    rstd_of(rs[:, :], psum[:, SHARED, :], turn + 1, 1.0 / 128, S["rs_ready"], S["turn_free"])
                    act.wait_ge(S["on_ready"], x["s"] + 1)
                    scalar.activation(o_hi[:, x["s"], :], o_raw[:, :], ACT.Copy).then_inc(S["ohi_ready"], 1)

        def gates(b):
            scalar.preload_act_table_set(SIG_SET)
            t0 = b["t_body"] + 30
            with act.Fori(0, 2) as i:
                for j in range(4):
                    for n, sig in ((0, sig_a), (1, sig_b)):
                        tile_done(t0 + 3 * j + n, i, 12)
                        scalar.activation(sig[:, j % 2, :], psum[:, 4 * (j % 2) + n, 0:SEQ], ACT.Sigmoid)\
                              .then_inc(sig_ready, 1)
                        refill(t0 + 3 * j + n, i, 12)
                    tile_done(t0 + 3 * j + 2, i, 12)
                    refill(t0 + 3 * j + 2, i, 12)
            scalar.preload_act_table_set(EXP_SET)

        for b in BLOCKS:
            pre_norm(b)
            if b["n"] == 0:
                for t in range(RING):
                    head(t, t)
            modulate(b)
            if b["kind"] == "ffn":
                ffn_body(b)
            else:
                mixer(b)
                if b["kind"] == "b2":
                    gates(b)
            output(b)
        pre_norm({"n": len(BLOCKS), "tok": LAT})

    @block.vector
    def _(dve):
        vec = nc.vector
        for s, n in ((ada_dot, ADA0), (lo_ready, LO0), (tile_used, USED0), (g_ready, PAIR0),
                     (gu_ready, PAIR0), (y_evac, PAIR0), (ysq_ready, PAIR0), (yacc_ready, PAIR0), (merged_ready, PAIR0)):
            dve.sem_inc(s, n)
        vec.memset(ones[:, :], 1.0).then_inc(set_up, 1)
        vec.memset(eps, EPS).then_inc(set_up, 1)

        dve.wait_ge(consts_in, 16)
        for m in range(2):
            l0 = COL["lambda"] + 2 * m * DA_QK
            vec.tensor_tensor_reduce(out=lam_t[:, m, :], in0=col[:, l0:l0 + DA_QK], in1=col[:, l0 + DA_QK:l0 + 2 * DA_QK],
                                     scale=1.0, scalar=0.0, op0=ALU.mult, op1=ALU.add,
                                     accum_out=small[:, 2 + m:3 + m]).then_inc(lam_sum, 1)
        dve.wait_ge(lam_exp, 1)
        vec.tensor_tensor(small[:, 6:7], small[:, 5:6], small[:, 4:5], ALU.subtract).then_inc(lam_step, 1)
        dve.wait_ge(lam_step, 1)
        vec.tensor_scalar(neg_lam, small[:, 6:7], -LAMBDA_INIT, None, ALU.add).then_inc(lam_ready, 1)

        def ada(tile, n, junk, i=0, per=0):
            if n >= 2:
                dve.wait_ge(m_done, i * per + (n - 1))
            for c in range(2):
                dve.wait_ge(ada_dot, i * (2 * per) + (2 * n + c + ADA0))
                vec.tensor_tensor_reduce(out=psum[:, junk:junk + 2, :].rearrange("p a b -> p (a b)"), in0=tile,
                                         in1=silu_c[:, c, :], scale=1.0, scalar=0.0, op0=ALU.mult, op1=ALU.add,
                                         accum_out=ada_sum[:, n % 2, c:c + 1]).then_inc(ada_dot, 1)
            dve.wait_ge(ada_dot, i * (2 * per) + (2 * n + 2 + ADA0))
            bias = bass.ds(i * per + (COL["ada_b"] + n), 1)
            vec.tensor_scalar(mcol[:, :, bass.ds(i * per + n, 1)], ada_sum[:, n % 2, :].rearrange("p (c o) -> p c o", o=1), col[:, bias], None, ALU.add)\
               .then_inc(m_done, 1)

        def ada_tile_in(n, slot, i=0, steps=0):
            dve.wait_ge(ada_landed[slot], i * (16 * steps) + 16 * (2 + (n - ADA_FIRST) // ADA_SLOTS))

        n_coefs = [0]

        def ada_finish(n0, n1):
            dve.wait_ge(m_done, n1)
            for layer in range(2):
                for part in range(3):
                    scale, gate = (MODS * layer + (3 * part + w) * CH for w in (1, 2))
                    pre = COL["norm_g"] + (6 * layer + 2 * part) * CH
                    post = pre + CH
                    for c in range(2):
                        n = 3 * (2 * layer + c) + part
                        if n0 < scale + CH <= n1:
                            vec.scalar_tensor_tensor(out=a_col[:, n, :], in0=mcol[:, c, scale:scale + CH], scalar=1.0,
                                                     in1=col[:, pre:pre + CH], op0=ALU.add, op1=ALU.mult).then_inc(coefs, 1)
                            n_coefs[0] += 1
                        if n0 < gate + CH <= n1:
                            vec.scalar_tensor_tensor(out=g_col[:, n, :], in0=mcol[:, c, gate:gate + CH],
                                                     scalar=1.0 if part == 1 else 0.5, in1=col[:, post:post + CH],
                                                     op0=ALU.mult, op1=ALU.mult).then_inc(coefs, 1)
                            n_coefs[0] += 1
            if n_coefs[0]:
                dve.wait_ge(coefs, n_coefs[0])

        dve.wait_ge(silu_c_ready, 1)
        for n in range(ADA_FIRST):
            if n % (ADA_FIRST // ADA_SLOTS) == 0:
                dve.wait_ge(ada_landed[n // (ADA_FIRST // ADA_SLOTS)], 16)
            ada(ada_first[:, n, :], n, 0)
        ada_finish(0, ADA_FIRST)

        def norm_gain(b, m, c):
            if m is None:
                g = COL["norm2"] + b["part"] * CH + c
                return col[:, g:g + 1]
            return a_col[:, 3 * m + b["part"], c:c + 1]

        def modulate(b):
            n, tok = b["n"], b["tok"]
            if n == 0:
                dve.wait_ge(h_in, 16)
            dve.wait_ge(rstd_h_ready, n + 1)

            def rest(c):
                dve.wait_ge(uhi_ready, CH * n + c + 1)
                full = v1 if b["layer"] is None else ufull
                vec.tensor_tensor(u_lo[:, c, tok], full[:, c % 2, tok], u_hi[:, c, tok].bitcast(F32), ALU.subtract)\
                   .then_inc(u_ready, 1)

            for c in range(CH):
                if c >= 2:
                    dve.wait_ge(u_ready, CH * n + c - 1)
                for part, m in conds(b):
                    last = vec.scalar_tensor_tensor(out=v1[:, c % 2, part], in0=h[:, c, part], scalar=norm_gain(b, m, c),
                                                    in1=rstd[:, part], op0=ALU.mult, op1=ALU.mult)
                last.then_inc(v1_ready, 1)
                if c:
                    rest(c - 1)
            rest(CH - 1)

        def ffn_body(b):
            tok, f = b["tok"], b["f"]
            n0, first, _ = b["ada"]

            def steps(i, skip):
                for j in range(2):
                    if not skip and first:
                        for x in range(2):
                            n = n0 + 2 * j + x
                            ada_tile_in(n, 2 * j + x, i, 1)
                            ada(ada_tile("body", 2 * j + x), n, 6, i, 4)
                    m0 = FCH * f + j + 2 * skip
                    t0 = b["t_body"] + 4 * skip
                    dve.wait_ge(silu_ready, i * 2 + (m0 + 1))
                    dve.wait_ge(tile_used, i * 4 + (t0 + 2 * j + 2 + USED0))
                    vec.tensor_tensor(s_up[:, j, tok], s_up[:, j, tok], psum[:, 2 * j + 1, tok], ALU.mult)\
                       .then_inc(g_ready, 1)
                    dve.wait_ge(g_ready, i * 2 + (m0 + 1 + PAIR0))
                    hi = gu_hi[:, bass.ds(i * 2 + (j + 2 * skip), 1), tok].rearrange("p o t -> p (o t)")
                    lo = gu_lo[:, bass.ds(i * 2 + (j + 2 * skip), 1), tok].rearrange("p o t -> p (o t)")
                    vec.tensor_copy(hi, s_up[:, j, tok]).then_inc(ghi_ready, 1)
                    dve.wait_ge(ghi_ready, i * 2 + (m0 + 1))
                    vec.tensor_tensor(lo, s_up[:, j, tok], hi.bitcast(F32), ALU.subtract).then_inc(gu_ready, 1)

            if first:
                with dve.Fori(0, first) as i:
                    steps(i, 0)
                ada_finish(n0, n0 + 4 * first)
            with dve.Fori(0, FCH // 2 - first) as i:
                steps(i, first)

        def output(b):
            n, tok = b["n"], b["tok_out"]
            parts = len(out_parts(b["kind"]))
            if b["layer"] is None:
                weight = 1.0 if b["part"] == 1 else 0.5
                with dve.Fori(0, 2) as i:
                    for j in range(4):
                        dve.wait_ge(tile_used, i * (4 * parts) + (b["t_out"] + parts * (j + 1) + USED0))
                        hc = h[:, bass.ds(i * 4 + j, 1), tok].rearrange("p o t -> p (o t)")
                        vec.scalar_tensor_tensor(out=hc, in0=psum[:, 4 + j % 2, tok], scalar=weight, in1=hc,
                                                 op0=ALU.mult, op1=ALU.add).then_inc(h_ready, 1)
                return
            vec.memset(sqsum[:, tok], 0.0).then_inc(sqsum_zero, 1)
            dve.wait_ge(sqsum_zero, n + 1)
            n1 = b["ada"][0] + 4 * b["ada"][1]
            with dve.Fori(0, 2) as i:
                for j in range(4):
                    if b["ada"][2]:
                        for x in range(2):
                            m, slot = n1 + 2 * j + x, (2 * j + x) % ADA_SLOTS
                            ada_tile_in(m, slot, i, 2)
                            ada(ada_tile("output", slot), m, 0, i, 8)
                    dve.wait_ge(tile_used, i * (4 * parts) + (b["t_out"] + parts * (j + 1) + USED0))
                    dve.wait_ge(ysq_ready, i * 4 + (CH * n + j + 1 + PAIR0))
                    for part, m in conds({**b, "tok": tok}):
                        gate = g_col[:, 3 * m + b["part"], bass.ds(i * 4 + j, 1)]
                        yc = y[:, bass.ds(i * 4 + j, 1), part].rearrange("p o t -> p (o t)")
                        last = vec.tensor_scalar(yc, psum[:, 4 + j % 2, part], gate, None, ALU.mult)
                    last.then_inc(y_evac, 1)
                    dve.wait_ge(yacc_ready, i * 4 + (CH * n + j + PAIR0))
                    vec.tensor_tensor(sqsum[:, tok], sqsum[:, tok], sq[:, j % 2, tok], ALU.add).then_inc(yacc_ready, 1)
            if b["ada"][2]:
                ada_finish(n1, n1 + 8 * b["ada"][2])
            dve.wait_ge(rstd_y_ready, n + 1)

            def add(c):
                dve.wait_ge(ymul_ready, CH * n + c + 1)
                vec.tensor_tensor(h[:, c, tok], h[:, c, tok], y[:, c, tok], ALU.add).then_inc(h_ready, 1)

            dve.wait_ge(y_evac, CH * n + CH + PAIR0)
            for c in range(CH):
                vec.tensor_tensor(y[:, c, tok], y[:, c, tok], rstd[:, tok], ALU.mult).then_inc(ymul_ready, 1)
                if c:
                    add(c - 1)
            add(CH - 1)

        def mixer(b):
            kind = b["kind"]
            S = MS[kind]
            order, _ = plans[kind]
            scale = {"da": DA_QK ** -0.5, "ga": GA_DIM ** -0.5, "b2": 1.0}[kind]
            cos, sin = (tab[:, TAB[f"{kind}_{w}"]:TAB[f"{kind}_{w}"] + SEQ] if kind != "b2" else None for w in ("cos", "sin"))
            t_turn = {}
            n_rs = 0
            biased = 0

            def combine(u):
                U = u["U"]
                n = u["keys"] * (len(u["set"]["v"]) if kind == "b2" else 1)
                maps = 2 if kind == "da" else 1
                dve.wait_ge(S["exp_done"], exps_through(kind, U))
                vec.reciprocal(stat[:, U % 4, 6:6 + maps], stat[:, U % 4, 4:4 + maps]).then_inc(S["recip"], 1)
                dve.wait_ge(S["recip"], U + 1)
                if U >= 2:
                    dve.wait_ge(S["turn_ready"], t_turn[U - 2] + 1)
                out = pcomb[:, U % 2, 0:n]
                if kind != "da":
                    vec.tensor_scalar(out, prob[:, U % 2, 0:n], stat[:, U % 4, 6:7], None, ALU.mult).then_inc(S["pc_ready"], 1)
                    return
                vec.tensor_tensor(stat[:, U % 4, 7:8], stat[:, U % 4, 7:8], neg_lam, ALU.mult)
                vec.tensor_scalar(prob[:, U % 2, 0:n], prob[:, U % 2, 0:n], stat[:, U % 4, 6:7], None, ALU.mult)\
                   .then_inc(S["comb_part"], 1)
                dve.wait_ge(S["comb_part"], U + 1)
                vec.scalar_tensor_tensor(out=out, in0=prob[:, U % 2, 512:512 + n], scalar=stat[:, U % 4, 7:8],
                                         in1=prob[:, U % 2, 0:n], op0=ALU.mult, op1=ALU.add).then_inc(S["pc_ready"], 1)

            dve.wait_ge(tables_in, 16)
            if kind == "da":
                dve.wait_ge(lam_ready, 1)
            if kind == "b2":
                dve.wait_ge(dist_in, 16)
            for op, x, turn in order:
                if op == "ss":
                    n_rs += 1
                    dve.wait_ge(S["rs_ready"], n_rs)
                    gain = col[:, COL["qnorm" if x["what"] == "q" else "knorm"]:][:, 0:1]
                    vec.scalar_tensor_tensor(out=item_stage(x), in0=item_stage(x), scalar=gain, in1=rs[:, x["tok"]],
                                             op0=ALU.mult, op1=ALU.mult).then_inc(S["normed"], 1)
                elif op == "rot":
                    if x["norm"]:
                        dve.wait_ge(S["normed"], x["norm_n"])
                    dve.wait_ge(S["turn_ready"], turn + 1)
                    if x["rope_n"] > 1:
                        dve.wait_ge(S["qk_ready"], x["rope_n"] - 1)
                    vec.tensor_tensor(rope_a[:, :], latents(x), cos, ALU.mult)
                    vec.tensor_tensor(rope_b[:, :], psum[:, SHARED, 0:SEQ], sin, ALU.mult).then_inc(S["turn_free"], 1)
                    dve.wait_ge(S["turn_free"], turn + 1)
                    vec.tensor_tensor(latents(x), rope_a[:, :], rope_b[:, :], ALU.add).then_inc(S["qk_ready"], 1)
                elif op == "vtr":
                    dve.wait_ge(S["turn_ready"], turn + 1)
                    n = width(x["tok"])
                    vec.tensor_copy(v_st[:, x["par"], x["g"] * SEQ:x["g"] * SEQ + n], psum[:, SHARED, 0:n])\
                       .then_inc(S["turn_free"], 1)
                elif op == "C":
                    combine(x)
                elif op == "S":
                    U = x["U"]
                    dve.wait_ge(S["s_ready"], U + 1)
                    maps = 2 if kind == "da" else 1
                    if kind == "b2":
                        if U >= 2:
                            dve.wait_ge(S["exp_done"], U - 1)
                        n, ng = x["keys"], len(x["set"]["v"])
                        d0 = DIST["dsa" if ng > 1 else "moba", x["qt"]]
                        for g in range(ng):
                            vec.scalar_tensor_tensor(out=sbias[:, U % 2, g * n:g * n + n], in0=dist[:, d0 + g * n:d0 + g * n + n],
                                                     scalar=slope_col(kind, x, g), in1=scores_of(kind, x)[:, g * n:g * n + n],
                                                     op0=ALU.mult, op1=ALU.add).then_inc(S["biased"], 1)
                        biased += ng
                        x["biased"] = biased
                        dve.wait_ge(S["biased"], biased)
                        src = sbias[:, U % 2, 0:ng * n]
                    else:
                        src = scores_of(kind, x)
                    vec.tensor_reduce(stat[:, U % 4, 0:maps], src, AX.X, ALU.max, negate=True).then_inc(S["max_part"], 1)
                    dve.wait_ge(S["max_part"], U + 1)
                    vec.tensor_scalar(stat[:, U % 4, 2:2 + maps], stat[:, U % 4, 0:maps], scale, None, ALU.mult)\
                       .then_inc(S["max_ready"], 1)
                elif op == "T":
                    u, _, _ = x
                    t_turn[u["U"]] = u["turn"]
                elif op == "O":
                    dve.wait_ge(S["pv_ready"], x["last_unit"] + 1)
                    s = x["s"]
                    if kind == "da":
                        dve.wait_ge(S["osq_ready"], s + 1)
                        if s:
                            dve.wait_ge(S["olo_ready"], s)
                        vec.tensor_scalar(o_raw[:, :], psum[:, PVB, :], col[:, COL["subln"]:COL["subln"] + 1],
                                          1.0 - LAMBDA_INIT, ALU.mult, ALU.mult).then_inc(S["o_evac"], 1)
                        continue
                    dve.wait_ge(S["ohi_ready"], s + 1)
                    if kind == "ga":
                        vec.tensor_tensor(o_lo[:, s, LAT], psum[:, pv_bank(kind, s), LAT], o_hi[:, s, LAT].bitcast(F32), ALU.subtract)\
                           .then_inc(S["olo_ready"], 1)
                    else:
                        for j in range(2):
                            p = slice(64 * j, 64 * j + 64)
                            last = vec.tensor_tensor(y_lo[p, s, :], psum[p, PVB, 256 * j:256 * j + 256],
                                                     y_hi[p, s, :].bitcast(F32), ALU.subtract)
                        last.then_inc(S["olo_ready"], 1)
                elif op == "oss":
                    s = x["s"]
                    dve.wait_ge(S["rs_ready"], s + 1)
                    dve.wait_ge(S["o_evac"], s + 1)
                    vec.tensor_tensor(o_raw[:, :], o_raw[:, :], rs[:, :], ALU.mult).then_inc(S["on_ready"], 1)
                    dve.wait_ge(S["ohi_ready"], s + 1)
                    vec.tensor_tensor(o_lo[:, s, :], o_raw[:, :], o_hi[:, s, :].bitcast(F32), ALU.subtract)\
                       .then_inc(S["olo_ready"], 1)

        def gates(b):
            t0 = b["t_body"] + 30
            with dve.Fori(0, 2) as i:
                for j in range(4):
                    bank = 4 * (j % 2)
                    dve.wait_ge(sig_ready, i * 8 + (2 * j + 2))
                    dve.wait_ge(tile_used, i * 12 + (t0 + 3 * j + 3 + USED0))
                    vec.tensor_tensor(sig_a[:, j % 2, :], sig_a[:, j % 2, :], psum[:, bank + 2, 0:SEQ], ALU.mult)
                    vec.tensor_tensor(sig_b[:, j % 2, :], sig_b[:, j % 2, :], psum[:, bank + 3, 0:SEQ], ALU.mult)\
                       .then_inc(gate_part, 1)
                    dve.wait_ge(gate_part, i * 4 + (j + 1))
                    vec.tensor_tensor(mg[:, j % 2, :], sig_a[:, j % 2, :], sig_b[:, j % 2, :], ALU.add).then_inc(gate_sum, 1)
                    dve.wait_ge(gate_sum, i * 4 + (j + 1))
                    hi = mg_hi[:, bass.ds(i * 4 + j, 1), :].rearrange("p o t -> p (o t)")
                    lo = mg_lo[:, bass.ds(i * 4 + j, 1), :].rearrange("p o t -> p (o t)")
                    vec.tensor_copy(hi, mg[:, j % 2, :]).then_inc(mhi_ready, 1)
                    dve.wait_ge(mhi_ready, i * 4 + (j + 1))
                    vec.tensor_tensor(lo, mg[:, j % 2, :], hi.bitcast(F32), ALU.subtract).then_inc(merged_ready, 1)

        for b in BLOCKS:
            modulate(b)
            if b["kind"] == "ffn":
                ffn_body(b)
            else:
                mixer(b)
                if b["kind"] == "b2":
                    gates(b)
            output(b)
        dve.wait_ge(rstd_h_ready, len(BLOCKS) + 1)
        for c in range(CH):
            g = COL["norm2"] + 3 * CH + c
            vec.scalar_tensor_tensor(out=final[:, c, :], in0=h[:, c, LAT], scalar=col[:, g:g + 1], in1=rstd[:, LAT],
                                     op0=ALU.mult, op1=ALU.mult).then_inc(out_ready, 1)

    @block.tensor
    def _(pe):
        mm = nc.tensor.matmul

        pe.wait_ge(set_up, 2)

        def blocks(slot, out, moving, ks, first=0, start=True, stop=True, ready=None):
            for n, k in enumerate(ks):
                if ready is not None:
                    pe.wait_ge(u_ready, ready + k + 1)
                w = slice((first + n) * 128, (first + n + 1) * 128)
                x_hi, x_lo = moving(k)
                mm(out, w_hi[:, slot, w], x_hi, start=start and n == 0, stop=False)
                mm(out, w_hi[:, slot, w], x_lo, start=False, stop=False)
                last = mm(out, w_lo[:, slot, w], x_hi, start=False, stop=stop and n == len(ks) - 1)
            return last

        def split(t, i=0, per=0):
            pe.wait_ge(lo_ready, i * per + (t + 1 + LO0))
            return t % RING

        def pre_norm(b):
            n, tok = b["n"], b["tok"]
            for c in range(CH):
                pe.wait_ge(hsq_ready, CH * n + c + 1)
                mm(psum[:, SSH, tok], ones[:, :], sq[:, c % 2, tok], start=c == 0, stop=c == CH - 1).then_inc(hsq_used, 1)

        def normed(tok):
            return lambda k: (u_hi[:, k, tok], u_lo[:, k, tok])

        def ffn_body(b):
            tok, t0 = b["tok"], b["t_body"]
            with pe.Fori(0, FCH // 2) as i:
                for j in range(2):
                    pe.wait_ge(g_ready, i * 2 + (FCH * b["f"] + j + 1))
                    for n in range(2):
                        t = t0 + 2 * j + n
                        blocks(split(t, i, 4), psum[:, 2 * j + n, tok], normed(tok), range(CH),
                               ready=CH * b["n"] if j + n == 0 else None).then_inc(tile_used, 1)

        def output(b):
            n, tok = b["n"], b["tok_out"]
            parts = out_parts(b["kind"])
            if b["kind"] == "ffn":
                pe.wait_ge(gu_ready, FCH * (b["f"] + 1) + PAIR0)
                moving = lambda k: (gu_hi[:, k, tok], gu_lo[:, k, tok])
            elif b["kind"] == "b2":
                pe.wait_ge(merged_ready, CH + PAIR0)
                moving = lambda k: (mg_hi[:, k, :], mg_lo[:, k, :])
            else:
                pe.wait_ge(MS[b["kind"]]["olo_ready"], 8)
                moving = lambda k: (o_hi[:, k, tok], o_lo[:, k, tok])
            with pe.Fori(0, 2) as i:
                for j in range(4):
                    if b["layer"] is None:
                        pe.wait_ge(h_ready, i * 4 + (CH * n + j - 1))
                    else:
                        pe.wait_ge(y_evac, i * 4 + (CH * n + j + 1))
                        pe.wait_ge(ysq_ready, i * 4 + (CH * n + j + 1))
                    for p, (k0, k1) in enumerate(parts):
                        t = b["t_out"] + len(parts) * j + p
                        blocks(split(t, i, 4 * len(parts)), psum[:, 4 + j % 2, tok], moving, range(k0, k1),
                               start=p == 0, stop=p == len(parts) - 1).then_inc(tile_used, 1)
            if b["layer"] is not None:
                pe.wait_ge(yacc_ready, CH * n + CH + PAIR0)
                mm(psum[:, SSY, tok], ones[:, :], sqsum[:, tok], start=True, stop=True).then_inc(yss_ready, 1)

        def mixer(b):
            kind = b["kind"]
            S = MS[kind]
            order, _ = plans[kind]
            biased = 0
            pe.wait_ge(tables_in, 16)
            freed = {}

            def item_ready(it):
                if it["rope"]:
                    pe.wait_ge(S["qk_ready"], it["rope_n"])
                else:
                    pe.wait_ge(S["proj_evac"], it["idx"] + 1)

            def turn_wait(turn):
                if turn:
                    pe.wait_ge(S["turn_free"], turn)

            for op, x, turn in order:
                if op == "proj":
                    x, k0, k1 = x
                    if x["idx"] >= 2 and not k0:
                        pe.wait_ge(S["proj_evac"], x["idx"] - 1)
                    slot = x["t"] % RING if k0 else split(x["t"])
                    last = blocks(slot, psum[:, x["idx"] % 2, x["tok"]], normed(x["tok"]), range(k0, k1), first=k0,
                                  start=k0 == 0, stop=k1 == CH, ready=CH * b["n"] if x["idx"] == 0 else None)
                    if k1 == CH:
                        last.then_inc(tile_used, 1)
                elif op == "ss":
                    pe.wait_ge(S["proj_evac"], x["idx"] + 1)
                    turn_wait(turn)
                    mm(psum[:, SHARED, x["tok"]], ones[:, :], n_sq[:, x["idx"] % 2, x["tok"]], start=True, stop=True)\
                        .then_inc(S["turn_ready"], 1)
                elif op == "rot":
                    if x["norm"]:
                        pe.wait_ge(S["normed"], x["norm_n"])
                    else:
                        pe.wait_ge(S["proj_evac"], x["idx"] + 1)
                    turn_wait(turn)
                    mm(psum[:, SHARED, 0:SEQ], rot, latents(x), start=True, stop=True).then_inc(S["turn_ready"], 1)
                elif op == "vtr":
                    pe.wait_ge(S["proj_evac"], x["idx"] + 1)
                    turn_wait(turn)
                    src = item_stage(x)
                    for kt in range(width(x["tok"]) // 128):
                        last = nc.tensor.transpose(psum[:, SHARED, kt * 128:(kt + 1) * 128],
                                                   src[:, kt * 128:(kt + 1) * 128], ident)
                    last.then_inc(S["turn_ready"], 1)
                elif op == "S":
                    U, st, n = x["U"], x["set"], x["keys"]
                    for it in st["q"] + st["k"]:
                        if U == st["first_unit"]:
                            item_ready(it)
                    if kind == "b2":
                        if U >= 2:
                            pe.wait_ge(S["biased"], freed[U - 2])
                        biased += len(st["v"])
                        freed[U] = biased
                    elif U >= 2:
                        pe.wait_ge(S["exp_done"], exps_through(kind, U - 2))
                    out = scores_of(kind, x)
                    if kind == "ga":
                        q = latents(st["q"][0])[:, x["qt"] * 128 - CTX:x["qt"] * 128 - CTX + 128]
                        last = mm(out, q, k_st[:, st["k"][0]["par"], 0:n], start=True, stop=True)
                    elif kind == "da":
                        for m in range(2):
                            rows = slice(64 * m, 64 * m + 64)
                            q = q_st[rows, st["q"][0]["par"], x["qt"] * 128:x["qt"] * 128 + 128]
                            last = mm(out[:, m, :], q, k_st[rows, st["k"][0]["par"], 0:n], start=True, stop=True)
                    else:
                        rows = slice(64 * x["j"], 64 * x["j"] + 64)
                        for g in range(len(st["v"])):
                            q0 = g * SEQ + x["qt"] * 128
                            last = mm(out[:, g * n:g * n + n], q_st[rows, st["q"][g]["par"], q0:q0 + 128],
                                      k_st[rows, st["k"][g]["par"], g * SEQ:g * SEQ + n], start=True, stop=True)
                    last.then_inc(S["s_ready"], 1)
                elif op == "T":
                    u, a, e = x
                    pe.wait_ge(S["pc_ready"], u["U"] + 1)
                    turn_wait(turn)
                    for n in range(a, e):
                        last = nc.tensor.transpose(psum[:, SHARED, (n - a) * 128:(n - a + 1) * 128],
                                                   pcomb[:, u["U"] % 2, n * 128:(n + 1) * 128], ident)
                    last.then_inc(S["turn_ready"], 1)
                elif op == "PV":
                    st, U = x["set"], x["U"]
                    pe.wait_ge(S["turn_free"], max([x["turn"]] + [it["turn"] for it in st["v"]]) + 1)
                    if U == st["first_unit"] and st["s"]:
                        if kind == "ga":
                            if st["s"] > 1:
                                pe.wait_ge(S["olo_ready"], st["s"] - 1)
                        elif kind == "da":
                            pe.wait_ge(S["o_evac"], st["s"])
                            pe.wait_ge(S["osq_ready"], st["s"])
                        else:
                            pe.wait_ge(S["olo_ready"], st["s"])
                    for n, (g, kt) in enumerate(x["blocks"]):
                        last = mm(psum[:, pv_bank(kind, st["s"]), x["ocol"]:x["ocol"] + 128], v_tile(st["v"][g], kt),
                                  probT[:, U % 2, n * 128:(n + 1) * 128], start=n == 0, stop=n == len(x["blocks"]) - 1)
                    last.then_inc(S["pv_ready"], 1)
                elif op == "oss":
                    pe.wait_ge(S["osq_ready"], x["s"] + 1)
                    turn_wait(turn)
                    mm(psum[:, SHARED, :], ones[:, :], o_sq[:, :], start=True, stop=True).then_inc(S["turn_ready"], 1)

        def gates(b):
            t0 = b["t_body"] + 30
            pe.wait_ge(MS["b2"]["olo_ready"], 6)
            branch = lambda k: (y_hi[:, k, :], y_lo[:, k, :])
            with pe.Fori(0, 2) as i:
                for j in range(4):
                    bank = 4 * (j % 2)
                    pe.wait_ge(merged_ready, i * 4 + (j + 1))
                    for n in range(2):
                        t = t0 + 3 * j + n
                        blocks(split(t, i, 12), psum[:, bank + n, 0:SEQ], normed(LAT), range(CH)).then_inc(tile_used, 1)
                    slot = split(t0 + 3 * j + 2, i, 12)
                    blocks(slot, psum[:, bank + 2, 0:SEQ], branch, range(0, 2))
                    blocks(slot, psum[:, bank + 3, 0:SEQ], branch, range(2, 6), first=2).then_inc(tile_used, 1)

        for b in BLOCKS:
            pre_norm(b)
            if b["kind"] == "ffn":
                ffn_body(b)
            else:
                mixer(b)
                if b["kind"] == "b2":
                    gates(b)
            output(b)
        pre_norm({"n": len(BLOCKS), "tok": LAT})

    block_cm.__exit__(None, None, None)


def _tiles(w):
    k, m = w.shape
    return np.ascontiguousarray(w.reshape(k // 128, 128, m // 128, 128).transpose(2, 1, 0, 3).reshape(m // 128, 128, k))


def _columns(v):
    return v.reshape(-1, CH, 128).transpose(2, 0, 1).reshape(128, -1)


def _tables():
    f32 = np.float32
    ident = np.eye(128, dtype=f32)
    rot = np.zeros((128, 128), f32)
    for j in range(64):
        rot[2 * j + 1, 2 * j] = -1.0
        rot[2 * j, 2 * j + 1] = 1.0

    def rope(dim):
        n = dim // 4
        pos = np.arange(SEQ)
        freqs = (f32(THETA) ** (-np.arange(n, dtype=f32) / f32(n))).astype(f32)
        ang = np.concatenate([(pos // GRID_W).astype(f32)[:, None] * freqs, (pos % GRID_W).astype(f32)[:, None] * freqs], 1)
        ang = np.repeat(ang, 2, axis=1)
        ang = np.tile(ang, (1, 128 // dim)).T
        return [np.cos(ang).astype(f32), np.sin(ang).astype(f32)]

    tables = np.concatenate([ident, rot, *rope(DA_QK), *rope(GA_DIM)], axis=1)
    qp, kp = np.arange(SEQ)[:, None], np.arange(SEQ)[None, :]
    delta = qp - kp

    def table(ok):
        return np.where(ok, -delta, f32(MASKED) * 1e3).astype(f32)

    dsa = [table((delta >= 0) & (delta <= w) & (delta % dil == 0)) for w, dil in DSA_GROUPS]
    moba = table(delta >= 0)
    parts = []
    for qt in range(2):
        parts += [d[qt * 128:qt * 128 + 128, 0:128 * (qt + 1)] for d in dsa]
    for qt in range(2):
        parts.append(moba[qt * 128:qt * 128 + 128, 0:128 * (qt + 1)])
    dist = np.concatenate(parts, axis=1)

    def slopes(n):
        return (f32(2.0) ** (f32(-8.0) * np.arange(1, n + 1, dtype=f32) / f32(n))).astype(f32)
    sl = np.concatenate([slopes(len(DSA_GROUPS) * DSA_HPG), slopes(MOBA_HEADS)])
    return np.ascontiguousarray(tables), np.ascontiguousarray(dist), np.broadcast_to(sl, (128, 20))


def kernel(**inputs):
    import concourse.bacc as bacc
    from concourse.bass_utils import run_bass_kernel_spmd

    I = {k: np.asarray(v) for k, v in inputs.items()}
    tables, dist, slopes = _tables()
    col = np.concatenate([
        _columns(I["norm_g"]),
        _columns(np.stack([I["norm_ffn1_2"][0], I["norm_mix_2"][0], I["norm_ffn2_2"][0], I["norm_final_2"]])),
        I["da_subln"].reshape(128, 1), I["ga_q_norm"].reshape(128, 1), I["ga_k_norm"].reshape(128, 1), slopes,
        np.broadcast_to(I["da_lambda"].reshape(1, -1), (128, 4 * DA_QK)),
        I["ada_b"].reshape(2 * MODS, 128).T], axis=1)
    X = {"columns": col, "tables": tables, "dist": dist}
    X["hT"] = np.concatenate([I["ctx"][0], I["x"][0]]).reshape(TOK, CH, 128).transpose(2, 1, 0)
    X["cond"] = np.broadcast_to(np.stack([I["c"][0], I["c_ctx"]]), (128, 2, D))
    X["ada_w"] = I["ada_w"].reshape(2, D, MODS, 128).transpose(0, 2, 3, 1).reshape(2 * MODS, 128, D)
    win = [I["ffn_w_in"][l, p] for l in range(2) for p in range(2)]
    win += [np.concatenate([I[f"ffn{n}_gate_2"][0], I[f"ffn{n}_up_2"][0]], axis=1) for n in (1, 2)]
    wout = [I["ffn_w_out"][l, p] for l in range(2) for p in range(2)] + [I["ffn1_down_2"][0], I["ffn2_down_2"][0]]
    for f in range(6):
        X[f"ffn_in{f}"] = _tiles(win[f]).reshape(2, FCH, 128, TW).transpose(1, 0, 2, 3).reshape(2 * FCH, 128, TW)
        X[f"ffn_out{f}"] = _tiles(wout[f])
    X["da_in"] = _tiles(I["da_w_in"][0]).reshape(3, DA_HEADS, 128, TW).transpose(1, 0, 2, 3).reshape(3 * DA_HEADS, 128, TW)
    X["da_out"] = _tiles(I["da_w_out"][0])
    ga = _tiles(I["ga_w_in"][0])
    per = GA_HEADS // GA_KV
    X["ga_in"] = ga[[n for g in range(GA_KV) for n in (GA_HEADS + g, GA_HEADS + GA_KV + g, *range(per * g, per * g + per))]]
    X["ga_out"] = _tiles(I["ga_w_out"][0])
    w2 = _tiles(I["w_in_2"][0])
    X["b2_qkv"] = w2[[6 * w + 2 * g + s for s in range(2) for g in range(3) for w in range(3)]
                     + [18 + 4 * w + c for c in range(4) for w in range(3)]]
    X["b2_gate"] = w2[30:46].reshape(2, CH, 128, TW).transpose(1, 0, 2, 3)
    X["b2_up"] = np.concatenate([_tiles(I["w_up_a_2"][0]), _tiles(I["w_up_b_2"][0])], axis=2)
    X["b2_out"] = _tiles(I["w_out_2"][0])

    nc = bacc.Bacc("TRN2", target_bir_lowering=False, num_devices=1)
    arrays, A = {}, {}
    for name, a in X.items():
        arrays[f"in_{name}"] = np.ascontiguousarray(a)
        A[name] = nc.dram_tensor(f"in_{name}", list(a.shape), mybir.dt.float32, kind="ExternalInput").ap()
    A["out"] = nc.dram_tensor("out", [128, CH, SEQ], mybir.dt.float32, kind="ExternalOutput").ap()
    build(nc, A)
    r = run_bass_kernel_spmd(nc, [arrays], core_ids=[0])
    got = r.results[0]["out"]
    return np.ascontiguousarray(got.transpose(2, 1, 0).reshape(1, SEQ, D))
```

```python
import numpy as np

import concourse.bass as bass
import concourse.mybir as mybir

D = 1024
CH = D // 128
CTX, SEQ = 256, 256
TOK = CTX + SEQ
FULL, LAT = slice(0, TOK), slice(CTX, TOK)
DFF = 2816
FCH = DFF // 128
EPS = 1e-6
MASKED = -1e30
GRID_W = 64
THETA = 10000.0
RING = 4
TW = 1024

DA_HEADS, DA_QK = 8, 64
GA_HEADS, GA_KV, GA_DIM = 8, 2, 128
DSA_GROUPS = ((128, 1), (512, 4), (2048, 16))
DSA_HPG = 4
MOBA_HEADS, HEAD64 = 8, 64
LAMBDA_INIT = 0.2

MODS = 9 * CH
ADA_SLOTS = 4
ADA_FIRST = 2 * CH
ADA_GROUPS = (2, 4, 5, 5)
ADA_POOL = (1, 4, 7, 10, 13)
ADA_FREE = 4

COL = {}
_at = 0
for _name, _n in (("norm_g", 2 * 6 * CH), ("norm2", 4 * CH), ("subln", 1), ("qnorm", 1), ("knorm", 1),
                  ("slopes", 20), ("lambda", 4 * DA_QK), ("ada_b", 2 * MODS)):
    COL[_name] = _at
    _at += _n
NCOL = _at
TAB = {"ident": 0, "rot": 128, "da_cos": 256, "da_sin": 512, "ga_cos": 768, "ga_sin": 1024}
NTAB = 1280
DIST = {("dsa", 0): 0, ("dsa", 1): 384, ("moba", 0): 1152, ("moba", 1): 1280}
NDIST = 1536


def sub_blocks():
    spec = [("ffn", FULL, FULL, 0, 0), ("da", FULL, FULL, 0, 1), ("ffn", FULL, FULL, 0, 2),
            ("ffn", FULL, FULL, 1, 0), ("ga", FULL, LAT, 1, 1), ("ffn", LAT, LAT, 1, 2),
            ("ffn", LAT, LAT, None, 0), ("b2", LAT, LAT, None, 1), ("ffn", LAT, LAT, None, 2)]
    ada, at = {}, ADA_FIRST
    for n, body in ((0, (FCH - ADA_FREE) // 2), (2, (FCH - ADA_FREE) // 2), (3, None)):
        out_steps = 2 if body is not None else 0
        body = body if body is not None else (2 * MODS - at) // 4
        ada[n] = (at, body, out_steps)
        at += 4 * body + 8 * out_steps
    assert at == 2 * MODS
    body_tiles = {"ffn": 2 * FCH, "da": 3 * DA_HEADS, "ga": 2 * GA_KV + GA_HEADS, "b2": 30 + 3 * CH}
    out, t, f = [], 0, 0
    for n, (kind, tok_in, tok_out, layer, part) in enumerate(spec):
        b = {"n": n, "kind": kind, "tok": tok_in, "tok_out": tok_out, "layer": layer, "part": part,
             "t_body": t, "t_out": t + body_tiles[kind], "f": f, "ada": ada.get(n, (0, 0, 0))}
        b["out_tiles"] = 3 * CH if kind == "ffn" else CH
        t = b["t_out"] + b["out_tiles"]
        f += kind == "ffn"
        out.append(b)
    return out, t


def out_parts(kind):
    return [(0, 8), (8, 15), (15, 22)] if kind == "ffn" else [(0, 8)]


FILL_UNITS = 3
FILL_KEPT = {"da": 4, "ga": 2, "b2": 0}


def mixer_plan(kind, t0):
    sets, t, idx, U = [], t0, 0, 0

    def item(what, s, g, tok, **more):
        nonlocal t, idx
        it = {"what": what, "s": s, "g": g, "tok": tok, "t": t, "idx": idx, "norm": False, "rope": False, **more}
        t, idx = t + 1, idx + 1
        return it

    if kind == "da":
        for h in range(DA_HEADS):
            items = [item("q", h, 0, FULL, rope=True, par=h % 2), item("k", h, 0, FULL, rope=True, par=h % 2),
                     item("v", h, 0, FULL, par=h % 2)]
            sets.append({"s": h, "items": items, "q": items[:1], "k": items[1:2], "v": items[2:],
                         "units": [{"qt": qt, "keys": keys, "ocol": qt * 128} for qt, keys in
                                   ((2, TOK), (0, CTX), (3, TOK), (1, CTX))]})
    elif kind == "ga":
        kv = None
        for h in range(GA_HEADS):
            g = h // (GA_HEADS // GA_KV)
            items = []
            if h % (GA_HEADS // GA_KV) == 0:
                kv = [item("k", h, 0, FULL, norm=True, rope=True, par=g % 2), item("v", h, 0, FULL, par=g % 2)]
                items += kv
            items.append(item("q", h, 0, LAT, norm=True, rope=True, par=0, place=h % 3))
            sets.append({"s": h, "items": items, "q": items[-1:], "k": kv[:1], "v": kv[1:],
                         "units": [{"qt": qt, "keys": TOK, "ocol": qt * 128} for qt in (2, 3)]})
    else:
        for s in range(6):
            ng = 3 if s < 2 else 1
            items = [item(w, s, g, LAT, par=s % 2) for g in range(ng) for w in "qkv"]
            sets.append({"s": s, "items": items, "q": items[0::3], "k": items[1::3], "v": items[2::3],
                         "units": [{"qt": qt, "j": j, "keys": 128 * (qt + 1), "ocol": (2 * j + qt) * 128}
                                   for j in (0, 1) for qt in (1, 0)]})
    for st in sets:
        st["first_unit"] = U
        for u in st["units"]:
            u.update(U=U, set=st, tiles=u["keys"] // 128)
            U += 1
        st["last_unit"] = U - 1

    order, turns, ropes, norms, clock, pending = [], 0, 0, 0, 0, []
    heads = done = 0

    def add(op, x):
        nonlocal turns, ropes, norms, heads
        entry = [op, x, None]
        if op in ("ss", "rot", "vtr", "T", "oss"):
            entry[2] = turns
            turns += 1
        if op == "rot":
            ropes += 1
            x["rope_n"] = ropes
        if op == "ss":
            norms += 1
            x["norm_n"] = norms
        if op in ("ss", "vtr", "oss"):
            x["turn"] = entry[2]
        if op == "oss":
            heads += 1
        order.append(entry)

    def add_T(u):
        u["blocks"] = [(g, kt) for g in range(len(u["set"]["v"])) for kt in range(u["tiles"])]
        u["turns"] = []
        for a in range(0, len(u["blocks"]), 4):
            u["turns"].append(turns)
            add("T", (u, a, min(a + 4, len(u["blocks"]))))
        u["turn"] = turns - 1

    def add_part(part):
        nonlocal clock
        add("proj", part)
        clock += 1
        it, _, k1 = part
        if k1 == CH:
            if it["norm"] or it["rope"] or it["what"] == "v":
                pending.append(("ss" if it["norm"] else "rot" if it["rope"] else "vtr", it, clock + 2))

    def prepare(n):
        op, it, _ = pending.pop(n)
        add(op, it)
        if op == "ss":
            pending.append(("rot", it, clock + 2))

    def prepare_due():
        for n, (_, _, due) in enumerate(pending):
            if due <= clock:
                prepare(n)
                return

    def prepare_all(of):
        while True:
            n = next((n for n, (_, it, _) in enumerate(pending) if any(it is o for o in of)), None)
            if n is None:
                return
            prepare(n)

    def parts(s):
        return [(it, k, k + 2) for it in sets[s]["items"] for k in range(0, CH, 2)] if s < len(sets) else []

    ahead = 2 if kind == "ga" else 1
    for s in range(ahead):
        ps = parts(s)
        if s == 0:
            ps[:CH] = [ps[n // 2 + n % 2 * (CH // 2)] for n in range(CH)]
        for part in ps:
            add_part(part)
            prepare_due()
    units = [u for st in sets for u in st["units"]]
    if kind == "b2":
        filler = [(n, k, k + 2, 0) for n in range(2) for k in range(0, CH, 2)]
    else:
        last = sets[-1]["s"]
        filler = [(d, k, min(k + 2, last), min(k + 2, last)) for k in range(0, last, 2) for d in range(2)]
    kept = FILL_KEPT[kind]

    def fill(count):
        nonlocal clock
        while count and len(filler) > kept and filler[0][3] <= done:
            add("early", filler.pop(0)[:3])
            clock += 1
            count -= 1

    LAG = 2
    for U in range(len(units) + LAG):
        done = heads
        u = units[U] if U < len(units) else None
        old = units[U - LAG] if U >= LAG else None
        mine = []
        if u:
            st = u["set"]
            nxt, n, nu = parts(st["s"] + ahead), U - st["first_unit"], len(st["units"])
            mine = nxt[n * len(nxt) // nu:(n + 1) * len(nxt) // nu]
        fills = 1 if not mine and U >= len(units) - FILL_UNITS else 0
        third = -(-len(mine) // 3)
        if old:
            add_T(old)
        if 1 <= U <= len(units):
            add("C", units[U - 1])
        for part in mine[:third]:
            add_part(part)
        fill(fills)
        prepare_due()
        if u:
            if U == st["first_unit"]:
                prepare_all(st["q"] + st["k"])
            add("S", u)
        for part in mine[third:2 * third]:
            add_part(part)
        fill(fills)
        prepare_due()
        if old:
            if old["U"] == old["set"]["first_unit"]:
                prepare_all(old["set"]["v"])
            add("PV", old)
            if old["U"] == old["set"]["last_unit"]:
                if old["set"]["s"]:
                    prepare_all(sets[old["set"]["s"] - 1:old["set"]["s"]])
                add("O", old["set"])
                if kind == "da":
                    pending.append(("oss", old["set"], clock + 2))
                else:
                    heads += 1
        for part in mine[2 * third:]:
            add_part(part)
            prepare_due()
        fill(fills)
        prepare_due()
    done = len(sets)
    fill(len(filler))
    prepare_all([it for _, it, _ in pending])
    kept = 0
    fill(len(filler))
    prepare_all([it for _, it, _ in pending])
    return order, idx


def build(nc, A):
    F32, F32R = mybir.dt.float32, mybir.dt.float32r
    ACT, ALU, AX = mybir.ActivationFunctionType, mybir.AluOpType, mybir.AxisListType
    BLOCKS, N_TILES = sub_blocks()
    EXP_SET, SILU_SET, SIG_SET = "natural_log_exp_and_others", "silu_and_others", "sigmoid_and_others"

    base = (nc.sbuf_base + 63) // 64 * 64
    H0 = base
    U0 = H0 + CH * TOK * 4
    GU0 = U0 + 2 * CH * TOK * 4
    RING0 = GU0 + 2 * FCH * TOK * 4
    MISC0 = RING0 + 3 * RING * TW * 4

    def region(start):
        at = [start]

        def take(name, shape, dt=F32):
            t = nc.alloc_sbuf_tensor_at(name, [128, *shape], dt, offset=at[0])
            at[0] += (int(np.prod(shape)) * 4 + 31) // 32 * 32
            return t
        return take, at

    take, _ = region(H0)
    h = take("h", [CH, TOK])
    take, _ = region(U0)
    u_hi, u_lo = take("u_hi", [CH, TOK], F32R), take("u_lo", [CH, TOK], F32R)
    take, _ = region(U0)
    y = take("y", [CH, TOK])
    take, _ = region(U0)
    final = take("final", [CH, SEQ])
    take, _ = region(GU0)
    gu_hi, gu_lo = take("gu_hi", [FCH, TOK], F32R), take("gu_lo", [FCH, TOK], F32R)
    take, _ = region(U0)
    ada_first = take("ada_first", [ADA_FIRST, D])
    lam_t = take("lam_t", [2, DA_QK])
    take, _ = region(GU0 + FCH * TOK * 4)
    ada_prod = take("ada_prod", [6, D])
    take, _ = region(GU0 + (FCH - ADA_FREE) * TOK * 4)
    ada_hi = take("ada_hi", [2, D])
    take, _ = region(GU0 + (2 * FCH - ADA_FREE) * TOK * 4)
    ada_lo = take("ada_lo", [2, D])
    take, _ = region(U0 + CH * TOK * 4)
    ada_out = take("ada_out", [ADA_SLOTS, D])
    take, _ = region(GU0)
    v1 = take("v1", [4, TOK])
    ufull = take("ufull", [2, TOK])
    take, at = region(GU0)
    q_st, k_st = take("q_st", [2, 768]), take("k_st", [2, 768])
    vT = take("vT", [768])
    v_st = take("v_st", [2, 768])
    prob = take("prob", [2, 1024])
    pcomb = take("pcomb", [2, 768])
    probT = take("probT", [2, 768])
    rope_a, rope_b = take("rope_a", [SEQ]), take("rope_b", [SEQ])
    MIX0 = at[0]
    o_hi, o_lo = take("o_hi", [CH, TOK], F32R), take("o_lo", [CH, TOK], F32R)
    o_raw, o_sq, rs = take("o_raw", [TOK]), take("o_sq", [TOK]), take("rs", [TOK])
    n_sq = take("n_sq", [2, TOK])
    assert at[0] <= RING0
    take, at = region(MIX0)
    y_hi, y_lo = take("y_hi", [6, SEQ], F32R), take("y_lo", [6, SEQ], F32R)
    mg_hi, mg_lo = take("mg_hi", [CH, SEQ], F32R), take("mg_lo", [CH, SEQ], F32R)
    dist = take("dist", [NDIST])
    sbias = take("sbias", [2, 768])
    assert at[0] <= RING0
    take, _ = region(MIX0 - (2 * SEQ + 2 * 768 + 2 * 768 + 2048) * 4)
    sig_a, sig_b, mg = take("sig_a", [2, SEQ]), take("sig_b", [2, SEQ]), take("mg", [2, SEQ])
    take, _ = region(RING0)
    w_raw = take("w_raw", [RING, TW])
    w_hi, w_lo = take("w_hi", [RING, TW], F32R), take("w_lo", [RING, TW], F32R)
    take, at = region(MISC0)
    tab = take("tab", [NTAB])
    col = take("col", [NCOL])
    mcol = take("mcol", [2, 2 * MODS])
    a_col, g_col = take("a_col", [12, CH]), take("g_col", [12, CH])
    ones = take("ones", [128])
    rstd = take("rstd", [TOK])
    sqsum = rstd
    sq = take("sq", [2, TOK])
    s_up = sq
    ada_sum = take("ada_sum", [2, 2])
    silu_c = take("silu_c", [2, D])
    stat = take("stat", [4, 8])
    small = take("small", [16])
    assert at[0] <= nc.sbuf_usable_end, at[0] - nc.sbuf_usable_end
    psum = nc.alloc_psum_tensor("psum", [128, 8, 512], F32)
    PVB, SSY, SSH = 2, 6, 7
    TURN = (3, 7)

    ident, rot = tab[:, 0:128], tab[:, 128:256]
    eps = small[:, 0:1]
    neg_lam = small[:, 1:2]

    sem = nc.alloc_semaphore
    raw_landed = [sem(f"raw_landed{i}") for i in range(RING)]
    ada_landed = [sem(f"ada_landed{i}") for i in range(ADA_SLOTS)]
    hi_ready, lo_ready, tile_used = sem("hi_ready"), sem("lo_ready"), sem("tile_used")
    cond_in, tables_in, consts_in, h_in, dist_in = sem("cond_in"), sem("tables_in"), sem("consts_in"), sem("h_in"), sem("dist_in")
    set_up = sem("set_up")
    silu_c_ready, ada_dot, m_done, coefs = sem("silu_c_ready"), sem("ada_dot"), sem("m_done"), sem("coefs")
    ada_prod_ready, ada_prod_sum = sem("ada_prod_ready"), sem("ada_prod_sum")
    lam_sum, lam_exp, lam_ready, lam_step = sem("lam_sum"), sem("lam_exp"), sem("lam_ready"), sem("lam_step")
    h_ready, hsq_ready, hsq_used = sem("h_ready"), sem("hsq_ready"), sem("hsq_used")
    ln_done, rstd_h_ready, rstd_y_ready = sem("ln_done"), sem("rstd_h_ready"), sem("rstd_y_ready")
    v1_ready, uhi_ready = sem("v1_ready"), sem("uhi_ready")
    u_ready = [sem("u_even_ready"), sem("u_odd_ready")]
    silu_ready, g_ready, ghi_ready, gu_ready = sem("silu_ready"), sem("g_ready"), sem("ghi_ready"), sem("gu_ready")
    y_evac, ysq_ready, yacc_ready, yss_ready = sem("y_evac"), sem("ysq_ready"), sem("yacc_ready"), sem("yss_ready")
    sqsum_zero, ymul_ready, ymul_pool = sem("sqsum_zero"), sem("ymul_ready"), sem("ymul_pool")
    out_ready, out_done = sem("out_ready"), sem("out_done")
    MS = {}
    for kind in ("da", "ga", "b2"):
        MS[kind] = {name: sem(f"{kind}_{name}") for name in (
            "proj_evac", "turn_ready", "turn_free0", "turn_free1", "rs_ready", "normed", "qk_ready", "s_ready", "biased",
            "max_part", "max_ready", "exp_done", "recip", "comb_part", "pc_ready", "pv_ready", "osq_ready",
            "o_evac", "on_ready", "ohi_ready", "olo_ready")}
    sig_ready, gate_part, gate_sum, mhi_ready, merged_ready = (sem("sig_ready"), sem("gate_part"), sem("gate_sum"),
                                                               sem("mhi_ready"), sem("merged_ready"))

    LO0, USED0, PAIR0, ADA0 = RING, RING, 2, 2

    def conds(b):
        if b["layer"] is None:
            return [(b["tok"], None)]
        both = [(slice(0, CTX), 2 * b["layer"] + 1), (LAT, 2 * b["layer"])]
        return both if b["tok"] == FULL else both[1:]

    def width(tok):
        return tok.stop - tok.start

    def ada_tile(phase, slot):
        if phase == "output":
            return ada_out[:, slot, :]
        return (ada_hi if slot < 2 else ada_lo)[:, slot % 2, :]

    def first_group(n):
        return next(g for g in range(ADA_SLOTS) if n < sum(ADA_GROUPS[:g + 1]))

    FIRST_PRODUCTS = [(n, c) for n in ADA_POOL for c in range(2)]

    POOL_MUL = (1, 2, 4, 5, 7)

    def shift_of(b, m, c):
        n = MODS * b["layer"] + 3 * b["part"] * CH + c
        return mcol[:, m % 2, n:n + 1]

    plans = {b["kind"]: mixer_plan(b["kind"], b["t_body"]) for b in BLOCKS if b["kind"] != "ffn"}

    def item_stage(it):
        n = width(it["tok"])
        off = it.get("place", it["g"]) * SEQ
        if it["what"] == "v":
            return vT[:, off:off + n]
        return (q_st if it["what"] == "q" else k_st)[:, it["par"], off:off + n]

    def latents(it):
        n = width(it["tok"])
        off = it.get("place", it["g"]) * SEQ + n - SEQ
        return (q_st if it["what"] == "q" else k_st)[:, it["par"], off:off + SEQ]

    def v_tile(it, kt):
        off = it["g"] * SEQ + kt * 128
        return v_st[:, it["par"], off:off + 128]

    def scores_of(kind, u):
        b0 = 4 + 2 * (u["U"] % 2)
        if kind == "da":
            return psum[:, 4:6, 0:u["keys"]]
        n = u["keys"] * len(u["set"]["v"])
        return psum[:, b0:b0 + 2, :].rearrange("p a b -> p (a b)")[:, 0:n]

    def out_bank(b, j):
        if b["kind"] in ("da", "ga"):
            return (0, 1, 4, 5)[j % 4]
        return (4 if b["kind"] == "ffn" else 0) + j % 2

    def pv_bank(kind, s):
        return 5 if kind == "ga" and s % 2 else PVB

    def turn_freed(S, turn):
        return S[f"turn_free{turn % 2}"], turn // 2 + 1

    def slope_col(kind, u, g):
        s = u["set"]["s"]
        n = DSA_HPG * g + 2 * s + u["j"] if s < 2 else len(DSA_GROUPS) * DSA_HPG + 2 * (s - 2) + u["j"]
        c = COL["slopes"] + n
        return col[:, c:c + 1]

    def lag_of(kind):
        return 1 if kind == "da" else 2

    def exps_through(kind, U):
        return (2 if kind == "da" else 1) * (U + 1)

    block_cm = nc.Block()
    block = block_cm.__enter__()

    @block.sync
    def _(sp):
        sp.dma_start(silu_c[:, :, :], A["cond"]).then_inc(cond_in, 16)
        sp.dma_start(col[:, :], A["columns"]).then_inc(consts_in, 16)
        at = 0
        for s, count in enumerate(ADA_GROUPS):
            sp.dma_start(ada_first[:, at:at + count, :],
                         A["ada_w"][at:at + count].rearrange("n p c -> p n c")).then_inc(ada_landed[s], 16)
            at += count
            if s == 1:
                sp.dma_start(h[:, :, :], A["hT"]).then_inc(h_in, 16)
        sp.dma_start(tab[:, :], A["tables"]).then_inc(tables_in, 16)

        def load_ada(phase, n, slot, i=0, per=0):
            sp.wait_ge(m_done, i * per + (n - ADA_SLOTS + 1))
            src = A["ada_w"][bass.ds(i * per + n, 1)].rearrange("o p c -> p (o c)")
            sp.dma_start(ada_tile(phase, slot), src).then_inc(ada_landed[slot], 16)

        def load(src, t, slot, cols):
            sp.wait_ge(lo_ready, t + 1)
            sp.dma_start(w_raw[:, slot, 0:cols], src).then_inc(raw_landed[slot], 16)

        def load_whole(dram, t0, count, ada=None):
            loops = count // RING
            first = 0
            if ada:
                n0, first, _ = ada

                for x in range(RING):
                    load(dram[x], t0 + x, (t0 + x) % RING, TW)
                sp.wait_ge(tile_used, t0 + USED0)
                with sp.Fori(0, first) as i:
                    for j in range(2):
                        for x in range(2):
                            load_ada("body", n0 + 2 * j + x, 2 * j + x, i, 4)
                        for x in range(2):
                            n = RING + 2 * j + x
                            src = dram[bass.ds(i * RING + n, 1)].rearrange("o p c -> p (o c)")
                            load(src, i * RING + (t0 + n), (t0 + n) % RING, TW)
                first += 1
            with sp.Fori(0, loops - first) as i:
                for j in range(RING):
                    src = dram[bass.ds(i * RING + (first * RING + j), 1)].rearrange("o p c -> p (o c)")
                    load(src, i * RING + (t0 + first * RING + j), (t0 + j) % RING, TW)
            for n in range(loops * RING, count):
                load(dram[n], t0 + n, (t0 + n) % RING, TW)

        for b in BLOCKS:
            if b["kind"] == "ffn":
                n0, body_steps, out_steps = b["ada"]
                load_whole(A[f"ffn_in{b['f']}"], b["t_body"], 2 * FCH, b["ada"] if body_steps else None)
                with sp.Fori(0, 2) as i:
                    for j in range(4):
                        row = A[f"ffn_out{b['f']}"][bass.ds(i * 4 + j, 1)].rearrange("o p c -> p (o c)")
                        for n, (k0, k1) in enumerate(out_parts("ffn")):
                            t = b["t_out"] + 3 * j + n
                            load(row[:, k0 * 128:k1 * 128], i * 12 + t, t % RING, (k1 - k0) * 128)
                        if out_steps:
                            n1 = n0 + 4 * body_steps
                            sp.wait_ge(tile_used, b["t_out"] + USED0)
                            sp.wait_ge(m_done, n1)
                            for x in range(2):
                                load_ada("output", n1 + 2 * j + x, (2 * j + x) % ADA_SLOTS, i, 8)
            elif b["kind"] == "b2":
                load_whole(A["b2_qkv"], b["t_body"], RING)
                sp.wait_ge(tile_used, b["t_body"] + USED0)
                sp.dma_start(dist[:, :], A["dist"]).then_inc(dist_in, 16)
                load_whole(A["b2_qkv"][RING:], b["t_body"] + RING, 30 - RING)
                t0 = b["t_body"] + 30
                with sp.Fori(0, 2) as i:
                    for j in range(4):
                        gates = A["b2_gate"][bass.ds(i * 4 + j, 1)].rearrange("o g p c -> p (o g) c")
                        up = A["b2_up"][bass.ds(i * 4 + j, 1)].rearrange("o p c -> p (o c)")
                        for n, (src, cols) in enumerate(((gates[:, 0, :], TW), (gates[:, 1, :], TW), (up, 6 * 128))):
                            load(src, i * 12 + (t0 + 3 * j + n), (t0 + 3 * j + n) % RING, cols)
                load_whole(A["b2_out"], b["t_out"], CH)
            else:
                load_whole(A[b["kind"] + "_in"], b["t_body"], b["t_out"] - b["t_body"])
                load_whole(A[b["kind"] + "_out"], b["t_out"], CH)
        for half in range(2):
            sp.wait_ge(out_ready, 4 * half + 4)
            c = slice(4 * half, 4 * half + 4)
            sp.dma_start(A["out"][:, c, :], final[:, c, :]).then_inc(out_done, 16)
        sp.wait_ge(out_done, 32)

    @block.gpsimd
    def _(pool):
        def rest(t, cols=TW, i=0, per=0):
            slot = t % RING
            pool.wait_ge(hi_ready, i * per + (t + 1))
            pool.wait_ge(tile_used, i * per + (t + 1))
            pool.tensor_tensor(w_lo[:, slot, 0:cols], w_raw[:, slot, 0:cols], w_hi[:, slot, 0:cols].bitcast(F32),
                               ALU.subtract).then_inc(lo_ready, 1)

        def rests(t, end, cols=(TW,) * RING):
            steps = (end - t) // len(cols)
            if steps:
                with pool.Fori(0, steps) as i:
                    for j, c in enumerate(cols):
                        rest(t + j, c, i, len(cols))
            for n in range(t + steps * len(cols), end):
                rest(n)

        def residual(b):
            n, tok = b["n"], b["tok_out"]
            pool.wait_ge(rstd_y_ready, n + 1)
            pool.wait_ge(y_evac, CH * n + CH + PAIR0)
            for c in POOL_MUL:
                pool.tensor_tensor(y[:, c, tok], y[:, c, tok], rstd[:, tok], ALU.mult).then_inc(ymul_pool, 1)

        out_cols = [128 * (k1 - k0) for k0, k1 in out_parts("ffn")] * 4
        pool.wait_ge(silu_c_ready, 1)
        for k, (n, c) in enumerate(FIRST_PRODUCTS):
            pool.wait_ge(ada_landed[first_group(n)], 16)
            if k >= 6:
                pool.wait_ge(ada_prod_sum, k - 5)
            pool.tensor_tensor(ada_prod[:, k % 6, :], ada_first[:, n, :], silu_c[:, c, :], ALU.mult).then_inc(ada_prod_ready, 1)
        rests(0, 2)
        for b in BLOCKS:
            for c in range(1, CH, 2):
                pool.wait_ge(uhi_ready, CH * b["n"] + c + 1)
                full = v1[:, c % 4, b["tok"]] if b["layer"] is None else ufull[:, c // 2 % 2, b["tok"]]
                pool.tensor_tensor(u_lo[:, c, b["tok"]], full, u_hi[:, c, b["tok"]].bitcast(F32), ALU.subtract)\
                    .then_inc(u_ready[1], 1)
            if b["n"] == 0:
                rests(2, RING)
            t = b["t_body"] + RING
            if b["kind"] == "ffn":
                rests(t, b["t_out"])
                rests(b["t_out"], b["t_out"] + b["out_tiles"], out_cols)
            else:
                rests(t, b["t_out"] + b["out_tiles"])
            if b["n"] + 1 < len(BLOCKS):
                t = b["t_out"] + b["out_tiles"]
                for n in range(t, t + RING):
                    rest(n)
            if b["layer"] is not None:
                residual(b)

    @block.scalar
    def _(act):
        logs = [0]
        scalar = nc.scalar

        def head(t, slot, cols=TW, i=0, per=0):
            act.wait_ge(raw_landed[slot], i * (per // RING * 16) + 16 * (t // RING + 1))
            scalar.activation(w_hi[:, slot, 0:cols], w_raw[:, slot, 0:cols], ACT.Copy).then_inc(hi_ready, 1)

        def tile_done(t, i=0, per=0):
            act.wait_ge(tile_used, i * per + (t + 1 + USED0))

        def refill(t, i=0, per=0, last=False):
            if not last:
                head(t + RING, (t + RING) % RING, TW, i, per)

        def rstd_of(out, ss, scale, ready, freed=None):
            ln = scalar.activation(out, ss, ACT.Ln, bias=eps, scale=scale)
            if freed is not None:
                ln.then_inc(*freed[:1], 1)
                act.wait_ge(*freed)
            else:
                ln.then_inc(ln_done, 1)
                logs[0] += 1
                act.wait_ge(ln_done, logs[0])
            scalar.activation(out, out, ACT.Exp, scale=-0.5).then_inc(ready, 1)

        act.wait_ge(cond_in, 16)
        scalar.preload_act_table_set(SILU_SET)
        scalar.activation(silu_c[:, :, :], silu_c[:, :, :], ACT.Silu).then_inc(silu_c_ready, 1)
        scalar.preload_act_table_set(EXP_SET)
        act.wait_ge(lam_sum, 2)
        scalar.activation(small[:, 4:6], small[:, 2:4], ACT.Exp).then_inc(lam_exp, 1)

        def pre_norm(b):
            n, tok = b["n"], b["tok"]
            if n == 0:
                act.wait_ge(h_in, 16)
                act.wait_ge(set_up, 2)
            for c in range(CH):
                if n:
                    act.wait_ge(h_ready, CH * (n - 1) + c + 1)
                if c >= 2:
                    act.wait_ge(hsq_used, CH * n + c - 1)
                scalar.activation(sq[:, c % 2, tok], h[:, c, tok], ACT.Square).then_inc(hsq_ready, 1)
            act.wait_ge(hsq_used, CH * n + CH)
            rstd_of(rstd[:, tok], psum[:, SSH, tok], 1.0 / D, rstd_h_ready)

        def modulate(b):
            n, tok = b["n"], b["tok"]
            for c in range(CH):
                act.wait_ge(v1_ready, CH * n + c + 1)
                if b["layer"] is None:
                    last = scalar.activation(u_hi[:, c, tok], v1[:, c % 4, tok], ACT.Copy)
                else:
                    if c % 2 and c >= 5:
                        act.wait_ge(u_ready[1], CH // 2 * n + c // 2 - 1)
                    for part, m in conds(b):
                        last = scalar.activation(u_hi[:, c, part], v1[:, c % 4, part], ACT.Identity, bias=shift_of(b, m, c))
                        if c % 2:
                            last = scalar.activation(ufull[:, c // 2 % 2, part], v1[:, c % 4, part], ACT.Identity,
                                                     bias=shift_of(b, m, c))
                last.then_inc(uhi_ready, 1)

        def ffn_body(b):
            tok, f, t0 = b["tok"], b["f"], b["t_body"]
            scalar.preload_act_table_set(SILU_SET)
            with act.Fori(0, FCH // 2) as i:
                for j in range(2):
                    gate, up = t0 + 2 * j, t0 + 2 * j + 1
                    tile_done(gate, i, 4)
                    act.wait_ge(gu_ready, i * 2 + (FCH * f + j + 1))
                    scalar.activation(s_up[:, j, tok], psum[:, 2 * j, tok], ACT.Silu).then_inc(silu_ready, 1)
                    refill(gate, i, 4)
                    tile_done(up, i, 4)
                    refill(up, i, 4)
            scalar.preload_act_table_set(EXP_SET)

        def output(b):
            n, tok = b["n"], b["tok_out"]
            gated = b["layer"] is not None
            parts = out_parts(b["kind"])
            per = 4 * len(parts)

            def chunks(i, end):
                for j in range(4):
                    for p in range(len(parts)):
                        t = b["t_out"] + len(parts) * j + p
                        tile_done(t, i, per)
                        if gated and p == len(parts) - 1:
                            act.wait_ge(yacc_ready, i * 4 + (CH * n + j + 1))
                            scalar.activation(sq[:, j % 2, tok], psum[:, out_bank(b, j), tok], ACT.Square)\
                                  .then_inc(ysq_ready, 1)
                        refill(t, i, per, last=end and t + per + RING >= N_TILES)

            if b["t_out"] + b["out_tiles"] == N_TILES:
                chunks(0, False)
                chunks(1, True)
            else:
                with act.Fori(0, 2) as i:
                    chunks(i, False)
            if gated:
                act.wait_ge(yss_ready, n + 1)
                rstd_of(rstd[:, tok], psum[:, SSY, tok], 1.0 / D, rstd_y_ready)

        def mixer(b):
            kind = b["kind"]
            S = MS[kind]
            order, _ = plans[kind]
            scale = {"da": DA_QK ** -0.5, "ga": GA_DIM ** -0.5, "b2": 1.0}[kind]
            normed, last_oss = 0, None
            ss_turn = {}
            for op, x, turn in order:
                if op == "proj":
                    x, _, k1 = x
                    if k1 < CH:
                        continue
                    tile_done(x["t"])
                    src = psum[:, x["idx"] % 2, x["tok"]]
                    dst = item_stage(x)
                    if x["norm"]:
                        if x["idx"] - 2 in ss_turn:
                            act.wait_ge(S["turn_ready"], ss_turn[x["idx"] - 2] + 1)
                        ss_turn[x["idx"]] = x["turn"]
                        scalar.activation(dst, src, ACT.Copy)
                        scalar.activation(n_sq[:, x["idx"] % 2, x["tok"]], src, ACT.Square).then_inc(S["proj_evac"], 1)
                    else:
                        s = HEAD64 ** -0.5 if kind == "b2" and x["what"] == "q" else 1.0
                        scalar.activation(dst, src, ACT.Copy, scale=s).then_inc(S["proj_evac"], 1)
                    refill(x["t"])
                elif op == "ss":
                    act.wait_ge(S["turn_ready"], turn + 1)
                    if normed:
                        act.wait_ge(S["normed"], normed)
                    normed += 1
                    rstd_of(rs[:, x["tok"]], psum[:, TURN[turn % 2], x["tok"]], 1.0 / GA_DIM, S["rs_ready"], turn_freed(S, turn))
                elif op == "S":
                    U = x["U"]
                    act.wait_ge(S["max_ready"], U + 1)
                    if U >= 2:
                        act.wait_ge(S["pc_ready"], U - 1)
                    n = x["keys"] * (len(x["set"]["v"]) if kind == "b2" else 1)
                    for m in range(2 if kind == "da" else 1):
                        if kind == "da":
                            src = scores_of(kind, x)[:, m, :]
                        else:
                            src = scores_of(kind, x) if kind == "ga" else sbias[:, U % 2, 0:n]
                        scalar.activation(prob[:, U % 2, m * 512:m * 512 + n], src, ACT.Exp,
                                          bias=stat[:, U % 4, 2 + m:3 + m], scale=scale,
                                          accum_out=stat[:, U % 4, 4 + m:5 + m]).then_inc(S["exp_done"], 1)
                elif op == "T":
                    u, a, e = x
                    act.wait_ge(S["turn_ready"], turn + 1)
                    scalar.activation(probT[:, u["U"] % 2, a * 128:e * 128], psum[:, TURN[turn % 2], 0:(e - a) * 128],
                                      ACT.Copy).then_inc(turn_freed(S, turn)[0], 1)
                elif op == "O":
                    act.wait_ge(S["pv_ready"], x["last_unit"] + 1)
                    s = x["s"]
                    if kind == "da":
                        if last_oss is not None:
                            act.wait_ge(S["turn_ready"], last_oss + 1)
                        last_oss = x["turn"]
                        scalar.activation(o_sq[:, :], psum[:, PVB, :], ACT.Square).then_inc(S["osq_ready"], 1)
                    elif kind == "ga":
                        scalar.activation(o_hi[:, s, LAT], psum[:, pv_bank(kind, s), LAT], ACT.Copy).then_inc(S["ohi_ready"], 1)
                    else:
                        for j in range(2):
                            p = slice(64 * j, 64 * j + 64)
                            last = scalar.activation(y_hi[p, s, :], psum[p, PVB, 256 * j:256 * j + 256], ACT.Copy)
                        last.then_inc(S["ohi_ready"], 1)
                elif op == "oss":
                    act.wait_ge(S["turn_ready"], turn + 1)
                    rstd_of(rs[:, :], psum[:, TURN[turn % 2], :], 1.0 / 128, S["rs_ready"], turn_freed(S, turn))
                    act.wait_ge(S["on_ready"], x["s"] + 1)
                    scalar.activation(o_hi[:, x["s"], :], o_raw[:, :], ACT.Copy).then_inc(S["ohi_ready"], 1)

        def gates(b):
            scalar.preload_act_table_set(SIG_SET)
            t0 = b["t_body"] + 30
            with act.Fori(0, 2) as i:
                for j in range(4):
                    for n, sig in ((0, sig_a), (1, sig_b)):
                        tile_done(t0 + 3 * j + n, i, 12)
                        scalar.activation(sig[:, j % 2, :], psum[:, 4 * (j % 2) + n, 0:SEQ], ACT.Sigmoid)\
                              .then_inc(sig_ready, 1)
                        refill(t0 + 3 * j + n, i, 12)
                    tile_done(t0 + 3 * j + 2, i, 12)
                    refill(t0 + 3 * j + 2, i, 12)
            scalar.preload_act_table_set(EXP_SET)

        for b in BLOCKS:
            pre_norm(b)
            if b["n"] == 0:
                for k, (n, c) in enumerate(FIRST_PRODUCTS):
                    act.wait_ge(ada_prod_ready, k + 1)
                    scalar.activation(ada_prod[:, k % 6, :], ada_prod[:, k % 6, :], ACT.Copy, accum_out=mcol[:, c, n:n + 1])\
                          .then_inc(ada_prod_sum, 1)
                for t in range(RING):
                    head(t, t)
            modulate(b)
            if b["kind"] == "ffn":
                ffn_body(b)
            else:
                mixer(b)
                if b["kind"] == "b2":
                    gates(b)
            output(b)
        pre_norm({"n": len(BLOCKS), "tok": LAT})

    @block.vector
    def _(dve):
        vec = nc.vector
        for s, n in ((ada_dot, ADA0), (lo_ready, LO0), (tile_used, USED0), (g_ready, PAIR0),
                     (gu_ready, PAIR0), (y_evac, PAIR0), (ysq_ready, PAIR0), (yacc_ready, PAIR0), (merged_ready, PAIR0)):
            dve.sem_inc(s, n)
        vec.memset(ones[:, :], 1.0).then_inc(set_up, 1)
        vec.memset(eps, EPS).then_inc(set_up, 1)

        dve.wait_ge(consts_in, 16)
        for m in range(2):
            l0 = COL["lambda"] + 2 * m * DA_QK
            vec.tensor_tensor_reduce(out=lam_t[:, m, :], in0=col[:, l0:l0 + DA_QK], in1=col[:, l0 + DA_QK:l0 + 2 * DA_QK],
                                     scale=1.0, scalar=0.0, op0=ALU.mult, op1=ALU.add,
                                     accum_out=small[:, 2 + m:3 + m]).then_inc(lam_sum, 1)
        dve.wait_ge(lam_exp, 1)
        vec.tensor_tensor(small[:, 6:7], small[:, 5:6], small[:, 4:5], ALU.subtract).then_inc(lam_step, 1)
        dve.wait_ge(lam_step, 1)
        vec.tensor_scalar(neg_lam, small[:, 6:7], -LAMBDA_INIT, None, ALU.add).then_inc(lam_ready, 1)

        def dot(tile, c, q, junk, out, i=0, per=0):
            dve.wait_ge(ada_dot, i * per + (q - 1 + ADA0))
            vec.tensor_tensor_reduce(out=psum[:, junk:junk + 2, :].rearrange("p a b -> p (a b)"), in0=tile,
                                     in1=silu_c[:, c, :], scale=1.0, scalar=0.0, op0=ALU.mult, op1=ALU.add,
                                     accum_out=out).then_inc(ada_dot, 1)

        FIRST_DOTS = 2 * (ADA_FIRST - len(ADA_POOL))

        def dots_before(n):
            return FIRST_DOTS + 2 * (n - ADA_FIRST)

        def ada(tile, n, junk, i, per):
            dve.wait_ge(m_done, i * per + (n - 1))
            for c in range(2):
                dot(tile, c, dots_before(n) + c, junk + 2 * c, ada_sum[:, n % 2, c:c + 1], i, 2 * per)
            dve.wait_ge(ada_dot, i * (2 * per) + (dots_before(n + 1) + ADA0))
            bias = bass.ds(i * per + (COL["ada_b"] + n), 1)
            vec.tensor_scalar(mcol[:, :, bass.ds(i * per + n, 1)], ada_sum[:, n % 2, :].rearrange("p (c o) -> p c o", o=1),
                              col[:, bias], None, ALU.add).then_inc(m_done, 1)

        def ada_tile_in(n, slot, i=0, steps=0):
            dve.wait_ge(ada_landed[slot], i * (16 * steps) + 16 * (2 + (n - ADA_FIRST) // ADA_SLOTS))

        n_coefs = [0]

        def ada_finish(n0, n1):
            dve.wait_ge(m_done, n1)
            for layer in range(2):
                for part in range(3):
                    scale, gate = (MODS * layer + (3 * part + w) * CH for w in (1, 2))
                    pre = COL["norm_g"] + (6 * layer + 2 * part) * CH
                    post = pre + CH
                    for c in range(2):
                        n = 3 * (2 * layer + c) + part
                        if n0 < scale + CH <= n1:
                            vec.scalar_tensor_tensor(out=a_col[:, n, :], in0=mcol[:, c, scale:scale + CH], scalar=1.0,
                                                     in1=col[:, pre:pre + CH], op0=ALU.add, op1=ALU.mult).then_inc(coefs, 1)
                            n_coefs[0] += 1
                        if n0 < gate + CH <= n1:
                            vec.scalar_tensor_tensor(out=g_col[:, n, :], in0=mcol[:, c, gate:gate + CH],
                                                     scalar=1.0 if part == 1 else 0.5, in1=col[:, post:post + CH],
                                                     op0=ALU.mult, op1=ALU.mult).then_inc(coefs, 1)
                            n_coefs[0] += 1
            if n_coefs[0]:
                dve.wait_ge(coefs, n_coefs[0])

        dve.wait_ge(silu_c_ready, 1)
        q = 0
        for n in range(ADA_FIRST):
            if n in ADA_POOL:
                continue
            dve.wait_ge(ada_landed[first_group(n)], 16)
            for c in range(2):
                dot(ada_first[:, n, :], c, q, 2 * c, mcol[:, c, n:n + 1])
                q += 1
        dve.wait_ge(ada_dot, FIRST_DOTS + ADA0)
        dve.wait_ge(ada_prod_sum, len(FIRST_PRODUCTS))
        for c in range(2):
            vec.tensor_tensor(mcol[:, c, 0:ADA_FIRST], mcol[:, c, 0:ADA_FIRST], col[:, COL["ada_b"]:COL["ada_b"] + ADA_FIRST],
                              ALU.add).then_inc(m_done, ADA_FIRST // 2)
        ada_finish(0, ADA_FIRST)

        def norm_gain(b, m, c):
            if m is None:
                g = COL["norm2"] + b["part"] * CH + c
                return col[:, g:g + 1]
            return a_col[:, 3 * m + b["part"], c:c + 1]

        def modulate(b):
            n, tok = b["n"], b["tok"]
            if n == 0:
                dve.wait_ge(h_in, 16)
            dve.wait_ge(rstd_h_ready, n + 1)

            def rest(c):
                dve.wait_ge(uhi_ready, CH * n + c + 1)
                if b["layer"] is None:
                    last = vec.tensor_tensor(u_lo[:, c, tok], v1[:, c % 4, tok], u_hi[:, c, tok].bitcast(F32), ALU.subtract)
                else:
                    for part, m in conds(b):
                        last = vec.scalar_tensor_tensor(out=u_lo[:, c, part], in0=v1[:, c % 4, part], scalar=shift_of(b, m, c),
                                                        in1=u_hi[:, c, part].bitcast(F32), op0=ALU.add, op1=ALU.subtract)
                last.then_inc(u_ready[0], 1)

            for c in range(CH):
                if c >= 4:
                    dve.wait_ge(u_ready[c % 2], CH // 2 * n + c // 2 - 1)
                for part, m in conds(b):
                    last = vec.scalar_tensor_tensor(out=v1[:, c % 4, part], in0=h[:, c, part], scalar=norm_gain(b, m, c),
                                                    in1=rstd[:, part], op0=ALU.mult, op1=ALU.mult)
                last.then_inc(v1_ready, 1)
                if c % 2:
                    rest(c - 1)
            dve.wait_ge(u_ready[1], CH // 2 * (n + 1))

        def ffn_body(b):
            tok, f = b["tok"], b["f"]
            n0, first, _ = b["ada"]

            def steps(i, skip):
                for j in range(2):
                    if not skip and first:
                        for x in range(2):
                            n = n0 + 2 * j + x
                            ada_tile_in(n, 2 * j + x, i, 1)
                            ada(ada_tile("body", 2 * j + x), n, 4, i, 4)
                    m0 = FCH * f + j + 2 * skip
                    t0 = b["t_body"] + 4 * skip
                    dve.wait_ge(silu_ready, i * 2 + (m0 + 1))
                    dve.wait_ge(tile_used, i * 4 + (t0 + 2 * j + 2 + USED0))
                    vec.tensor_tensor(s_up[:, j, tok], s_up[:, j, tok], psum[:, 2 * j + 1, tok], ALU.mult)\
                       .then_inc(g_ready, 1)
                    dve.wait_ge(g_ready, i * 2 + (m0 + 1 + PAIR0))
                    hi = gu_hi[:, bass.ds(i * 2 + (j + 2 * skip), 1), tok].rearrange("p o t -> p (o t)")
                    lo = gu_lo[:, bass.ds(i * 2 + (j + 2 * skip), 1), tok].rearrange("p o t -> p (o t)")
                    vec.tensor_copy(hi, s_up[:, j, tok]).then_inc(ghi_ready, 1)
                    dve.wait_ge(ghi_ready, i * 2 + (m0 + 1))
                    vec.tensor_tensor(lo, s_up[:, j, tok], hi.bitcast(F32), ALU.subtract).then_inc(gu_ready, 1)

            if first:
                with dve.Fori(0, first) as i:
                    steps(i, 0)
                ada_finish(n0, n0 + 4 * first)
            with dve.Fori(0, FCH // 2 - first) as i:
                steps(i, first)

        def output(b):
            n, tok = b["n"], b["tok_out"]
            parts = len(out_parts(b["kind"]))
            if b["layer"] is None:
                weight = 1.0 if b["part"] == 1 else 0.5
                with dve.Fori(0, 2) as i:
                    for j in range(4):
                        dve.wait_ge(tile_used, i * (4 * parts) + (b["t_out"] + parts * (j + 1) + USED0))
                        hc = h[:, bass.ds(i * 4 + j, 1), tok].rearrange("p o t -> p (o t)")
                        vec.scalar_tensor_tensor(out=hc, in0=psum[:, out_bank(b, j), tok], scalar=weight, in1=hc,
                                                 op0=ALU.mult, op1=ALU.add).then_inc(h_ready, 1)
                return
            vec.memset(sqsum[:, tok], 0.0).then_inc(sqsum_zero, 1)
            dve.wait_ge(sqsum_zero, n + 1)
            n1 = b["ada"][0] + 4 * b["ada"][1]
            with dve.Fori(0, 2) as i:
                for j in range(4):
                    if b["ada"][2]:
                        for x in range(2):
                            m, slot = n1 + 2 * j + x, (2 * j + x) % ADA_SLOTS
                            ada_tile_in(m, slot, i, 2)
                            ada(ada_tile("output", slot), m, 0, i, 8)
                    dve.wait_ge(tile_used, i * (4 * parts) + (b["t_out"] + parts * (j + 1) + USED0))
                    dve.wait_ge(ysq_ready, i * 4 + (CH * n + j + 1 + PAIR0))
                    dve.wait_ge(yacc_ready, i * 4 + (CH * n + j + PAIR0))
                    vec.tensor_tensor(sqsum[:, tok], sqsum[:, tok], sq[:, j % 2, tok], ALU.add).then_inc(yacc_ready, 1)
                    for part, m in conds({**b, "tok": tok}):
                        gate = g_col[:, 3 * m + b["part"], bass.ds(i * 4 + j, 1)]
                        yc = y[:, bass.ds(i * 4 + j, 1), part].rearrange("p o t -> p (o t)")
                        last = vec.tensor_scalar(yc, psum[:, out_bank(b, j), part], gate, None, ALU.mult)
                    last.then_inc(y_evac, 1)
            if b["ada"][2]:
                ada_finish(n1, n1 + 8 * b["ada"][2])
            dve.wait_ge(rstd_y_ready, n + 1)

            own = [c for c in range(CH) if c not in POOL_MUL]

            def add(c):
                if c in POOL_MUL:
                    dve.wait_ge(ymul_pool, len(POOL_MUL) * n + POOL_MUL.index(c) + 1)
                else:
                    dve.wait_ge(ymul_ready, len(own) * n + own.index(c) + 1)
                vec.tensor_tensor(h[:, c, tok], h[:, c, tok], y[:, c, tok], ALU.add).then_inc(h_ready, 1)

            dve.wait_ge(y_evac, CH * n + CH + PAIR0)
            added = 0
            for c in own:
                vec.tensor_tensor(y[:, c, tok], y[:, c, tok], rstd[:, tok], ALU.mult).then_inc(ymul_ready, 1)
                while added < max(c, 2) and added < CH:
                    if added == c:
                        break
                    add(added)
                    added += 1
            while added < CH:
                add(added)
                added += 1

        def mixer(b):
            kind = b["kind"]
            S = MS[kind]
            order, _ = plans[kind]
            scale = {"da": DA_QK ** -0.5, "ga": GA_DIM ** -0.5, "b2": 1.0}[kind]
            cos, sin = (tab[:, TAB[f"{kind}_{w}"]:TAB[f"{kind}_{w}"] + SEQ] if kind != "b2" else None for w in ("cos", "sin"))
            t_turn = {}
            n_rs = 0
            biased = 0

            def combine(u):
                U = u["U"]
                n = u["keys"] * (len(u["set"]["v"]) if kind == "b2" else 1)
                maps = 2 if kind == "da" else 1
                dve.wait_ge(S["exp_done"], exps_through(kind, U))
                vec.reciprocal(stat[:, U % 4, 6:6 + maps], stat[:, U % 4, 4:4 + maps]).then_inc(S["recip"], 1)
                dve.wait_ge(S["recip"], U + 1)
                if U >= 2:
                    dve.wait_ge(S["turn_ready"], t_turn[U - 2] + 1)
                out = pcomb[:, U % 2, 0:n]
                if kind != "da":
                    vec.tensor_scalar(out, prob[:, U % 2, 0:n], stat[:, U % 4, 6:7], None, ALU.mult).then_inc(S["pc_ready"], 1)
                    return
                vec.tensor_tensor(stat[:, U % 4, 7:8], stat[:, U % 4, 7:8], neg_lam, ALU.mult)
                vec.tensor_scalar(prob[:, U % 2, 0:n], prob[:, U % 2, 0:n], stat[:, U % 4, 6:7], None, ALU.mult)\
                   .then_inc(S["comb_part"], 1)
                dve.wait_ge(S["comb_part"], U + 1)
                vec.scalar_tensor_tensor(out=out, in0=prob[:, U % 2, 512:512 + n], scalar=stat[:, U % 4, 7:8],
                                         in1=prob[:, U % 2, 0:n], op0=ALU.mult, op1=ALU.add).then_inc(S["pc_ready"], 1)

            dve.wait_ge(tables_in, 16)
            if kind == "da":
                dve.wait_ge(lam_ready, 1)
            if kind == "b2":
                dve.wait_ge(dist_in, 16)
            for op, x, turn in order:
                if op == "ss":
                    n_rs += 1
                    dve.wait_ge(S["rs_ready"], n_rs)
                    gain = col[:, COL["qnorm" if x["what"] == "q" else "knorm"]:][:, 0:1]
                    vec.scalar_tensor_tensor(out=item_stage(x), in0=item_stage(x), scalar=gain, in1=rs[:, x["tok"]],
                                             op0=ALU.mult, op1=ALU.mult).then_inc(S["normed"], 1)
                elif op == "rot":
                    if x["norm"]:
                        dve.wait_ge(S["normed"], x["norm_n"])
                    dve.wait_ge(S["turn_ready"], turn + 1)
                    if x["rope_n"] > 1:
                        dve.wait_ge(S["qk_ready"], x["rope_n"] - 1)
                    vec.tensor_tensor(rope_a[:, :], latents(x), cos, ALU.mult)
                    vec.tensor_tensor(rope_b[:, :], psum[:, TURN[turn % 2], 0:SEQ], sin, ALU.mult).then_inc(turn_freed(S, turn)[0], 1)
                    dve.wait_ge(*turn_freed(S, turn))
                    vec.tensor_tensor(latents(x), rope_a[:, :], rope_b[:, :], ALU.add).then_inc(S["qk_ready"], 1)
                elif op == "vtr":
                    dve.wait_ge(S["turn_ready"], turn + 1)
                    n = width(x["tok"])
                    vec.tensor_copy(v_st[:, x["par"], x["g"] * SEQ:x["g"] * SEQ + n], psum[:, TURN[turn % 2], 0:n])\
                       .then_inc(turn_freed(S, turn)[0], 1)
                elif op == "C":
                    combine(x)
                elif op == "S":
                    U = x["U"]
                    dve.wait_ge(S["s_ready"], U + 1)
                    maps = 2 if kind == "da" else 1
                    if kind == "b2":
                        if U >= 2:
                            dve.wait_ge(S["exp_done"], U - 1)
                        n, ng = x["keys"], len(x["set"]["v"])
                        d0 = DIST["dsa" if ng > 1 else "moba", x["qt"]]
                        for g in range(ng):
                            vec.scalar_tensor_tensor(out=sbias[:, U % 2, g * n:g * n + n], in0=dist[:, d0 + g * n:d0 + g * n + n],
                                                     scalar=slope_col(kind, x, g), in1=scores_of(kind, x)[:, g * n:g * n + n],
                                                     op0=ALU.mult, op1=ALU.add).then_inc(S["biased"], 1)
                        biased += ng
                        x["biased"] = biased
                        dve.wait_ge(S["biased"], biased)
                        src = sbias[:, U % 2, 0:ng * n]
                    else:
                        src = scores_of(kind, x)
                    vec.tensor_reduce(stat[:, U % 4, 0:maps], src, AX.X, ALU.max, negate=True).then_inc(S["max_part"], 1)
                    dve.wait_ge(S["max_part"], U + 1)
                    vec.tensor_scalar(stat[:, U % 4, 2:2 + maps], stat[:, U % 4, 0:maps], scale, None, ALU.mult)\
                       .then_inc(S["max_ready"], 1)
                elif op == "T":
                    u, _, _ = x
                    t_turn[u["U"]] = u["turn"]
                elif op == "O":
                    dve.wait_ge(S["pv_ready"], x["last_unit"] + 1)
                    s = x["s"]
                    if kind == "da":
                        dve.wait_ge(S["osq_ready"], s + 1)
                        if s:
                            dve.wait_ge(S["olo_ready"], s)
                        vec.tensor_scalar(o_raw[:, :], psum[:, PVB, :], col[:, COL["subln"]:COL["subln"] + 1],
                                          1.0 - LAMBDA_INIT, ALU.mult, ALU.mult).then_inc(S["o_evac"], 1)
                        continue
                    dve.wait_ge(S["ohi_ready"], s + 1)
                    if kind == "ga":
                        vec.tensor_tensor(o_lo[:, s, LAT], psum[:, pv_bank(kind, s), LAT], o_hi[:, s, LAT].bitcast(F32), ALU.subtract)\
                           .then_inc(S["olo_ready"], 1)
                    else:
                        for j in range(2):
                            p = slice(64 * j, 64 * j + 64)
                            last = vec.tensor_tensor(y_lo[p, s, :], psum[p, PVB, 256 * j:256 * j + 256],
                                                     y_hi[p, s, :].bitcast(F32), ALU.subtract)
                        last.then_inc(S["olo_ready"], 1)
                elif op == "oss":
                    s = x["s"]
                    dve.wait_ge(S["rs_ready"], s + 1)
                    dve.wait_ge(S["o_evac"], s + 1)
                    vec.tensor_tensor(o_raw[:, :], o_raw[:, :], rs[:, :], ALU.mult).then_inc(S["on_ready"], 1)
                    dve.wait_ge(S["ohi_ready"], s + 1)
                    vec.tensor_tensor(o_lo[:, s, :], o_raw[:, :], o_hi[:, s, :].bitcast(F32), ALU.subtract)\
                       .then_inc(S["olo_ready"], 1)

        def gates(b):
            t0 = b["t_body"] + 30
            with dve.Fori(0, 2) as i:
                for j in range(4):
                    bank = 4 * (j % 2)
                    dve.wait_ge(sig_ready, i * 8 + (2 * j + 2))
                    dve.wait_ge(tile_used, i * 12 + (t0 + 3 * j + 3 + USED0))
                    vec.tensor_tensor(sig_a[:, j % 2, :], sig_a[:, j % 2, :], psum[:, bank + 2, 0:SEQ], ALU.mult)
                    vec.tensor_tensor(sig_b[:, j % 2, :], sig_b[:, j % 2, :], psum[:, bank + 3, 0:SEQ], ALU.mult)\
                       .then_inc(gate_part, 1)
                    dve.wait_ge(gate_part, i * 4 + (j + 1))
                    vec.tensor_tensor(mg[:, j % 2, :], sig_a[:, j % 2, :], sig_b[:, j % 2, :], ALU.add).then_inc(gate_sum, 1)
                    dve.wait_ge(gate_sum, i * 4 + (j + 1))
                    hi = mg_hi[:, bass.ds(i * 4 + j, 1), :].rearrange("p o t -> p (o t)")
                    lo = mg_lo[:, bass.ds(i * 4 + j, 1), :].rearrange("p o t -> p (o t)")
                    vec.tensor_copy(hi, mg[:, j % 2, :]).then_inc(mhi_ready, 1)
                    dve.wait_ge(mhi_ready, i * 4 + (j + 1))
                    vec.tensor_tensor(lo, mg[:, j % 2, :], hi.bitcast(F32), ALU.subtract).then_inc(merged_ready, 1)

        for b in BLOCKS:
            modulate(b)
            if b["kind"] == "ffn":
                ffn_body(b)
            else:
                mixer(b)
                if b["kind"] == "b2":
                    gates(b)
            output(b)
        dve.wait_ge(rstd_h_ready, len(BLOCKS) + 1)
        for c in range(CH):
            g = COL["norm2"] + 3 * CH + c
            vec.scalar_tensor_tensor(out=final[:, c, :], in0=h[:, c, LAT], scalar=col[:, g:g + 1], in1=rstd[:, LAT],
                                     op0=ALU.mult, op1=ALU.mult).then_inc(out_ready, 1)

    @block.tensor
    def _(pe):
        mm = nc.tensor.matmul

        pe.wait_ge(set_up, 2)

        def blocks(slot, out, moving, ks, first=0, start=True, stop=True, ready=None, rest_ready=None):
            for n, k in enumerate(ks):
                if ready is not None:
                    ready(k)
                w = slice((first + n) * 128, (first + n + 1) * 128)
                x_hi, x_lo = moving(k)
                mm(out, w_hi[:, slot, w], x_hi, start=start and n == 0, stop=False)
                mm(out, w_lo[:, slot, w], x_hi, start=False, stop=False)
                if rest_ready is not None:
                    rest_ready(k)
                last = mm(out, w_hi[:, slot, w], x_lo, start=False, stop=stop and n == len(ks) - 1)
            return last

        def split(t, i=0, per=0):
            pe.wait_ge(lo_ready, i * per + (t + 1 + LO0))
            return t % RING

        def pre_norm(b):
            n, tok = b["n"], b["tok"]
            for c in range(CH):
                pe.wait_ge(hsq_ready, CH * n + c + 1)
                mm(psum[:, SSH, tok], ones[:, :], sq[:, c % 2, tok], start=c == 0, stop=c == CH - 1).then_inc(hsq_used, 1)

        def normed(tok):
            return lambda k: (u_hi[:, k, tok], u_lo[:, k, tok])

        def keep_clock(tok, bank):
            for _ in range(12 if tok == FULL else 8):
                mm(psum[:, bank, 0:128], ones[:, :], ones[:, :], start=True, stop=True)

        def u_chunk(b):
            return {"ready": lambda k: pe.wait_ge(uhi_ready, CH * b["n"] + k + 1),
                    "rest_ready": lambda k: pe.wait_ge(u_ready[k % 2], CH // 2 * b["n"] + k // 2 + 1)}

        def ffn_body(b):
            tok, t0 = b["tok"], b["t_body"]

            def step(m, j, i=0):
                pe.wait_ge(g_ready, i * 2 + (FCH * b["f"] + m + 1))
                for n in range(2):
                    t = t0 + 2 * m + n
                    blocks(split(t, i, 4), psum[:, 2 * j + n, tok], normed(tok), range(CH)).then_inc(tile_used, 1)

            pe.wait_ge(g_ready, FCH * b["f"] + 1)
            slots = split(t0), split(t0 + 1)
            for k in range(CH):
                for n in range(2):
                    last = blocks(slots[n], psum[:, n, tok], normed(tok), [k], first=k, start=k == 0, stop=k == CH - 1,
                                  **u_chunk(b))
                    if k == CH - 1:
                        last.then_inc(tile_used, 1)
            step(1, 1)
            with pe.Fori(0, FCH // 2 - 1) as i:
                for j in range(2):
                    step(2 + j, j, i)

        def output(b):
            n, tok = b["n"], b["tok_out"]
            parts = out_parts(b["kind"])
            if b["kind"] == "ffn":
                ready = lambda k: pe.wait_ge(gu_ready, FCH * b["f"] + k + 1 + PAIR0)
                moving = lambda k: (gu_hi[:, k, tok], gu_lo[:, k, tok])
            elif b["kind"] == "b2":
                ready = lambda k: pe.wait_ge(merged_ready, max(k, CH - 2) + 1 + PAIR0)
                moving = lambda k: (mg_hi[:, k, :], mg_lo[:, k, :])
            else:
                ready = lambda k: pe.wait_ge(MS[b["kind"]]["olo_ready"], k + 1)
                moving = lambda k: (o_hi[:, k, tok], o_lo[:, k, tok])
            def chunk(j, i=0, per=0, early=False):
                if early:
                    t = b["t_out"] + j
                    blocks(t % RING, psum[:, out_bank(b, j), tok], moving, [CH - 1], first=CH - 1, start=False,
                           ready=ready).then_inc(tile_used, 1)
                    return
                if b["layer"] is None:
                    pe.wait_ge(h_ready, i * per + (CH * n + j - 1))
                else:
                    before = CH * n + j + 1 - (2 if b["kind"] != "ffn" else 0)
                    pe.wait_ge(y_evac, i * per + before)
                    pe.wait_ge(ysq_ready, i * per + before)
                for p, (k0, k1) in enumerate(parts):
                    t = b["t_out"] + len(parts) * j + p
                    blocks(split(t, i, per * len(parts)), psum[:, out_bank(b, j), tok], moving, range(k0, k1),
                           start=p == 0, stop=p == len(parts) - 1, ready=None if j else ready).then_inc(tile_used, 1)

            if b["kind"] in ("da", "ga"):
                for j in range(2):
                    chunk(j, early=True)
                for j in range(2, CH):
                    chunk(j)
            else:
                with pe.Fori(0, 2) as i:
                    for j in range(4):
                        chunk(j, i, 4)
            if b["layer"] is not None:
                pe.wait_ge(yacc_ready, CH * n + CH + PAIR0)
                mm(psum[:, SSY, tok], ones[:, :], sqsum[:, tok], start=True, stop=True).then_inc(yss_ready, 1)

        def mixer(b):
            kind = b["kind"]
            S = MS[kind]
            order, n_items = plans[kind]
            biased = 0
            pe.wait_ge(tables_in, 16)
            freed = {}

            def item_ready(it):
                if it["rope"]:
                    pe.wait_ge(S["qk_ready"], it["rope_n"])
                else:
                    pe.wait_ge(S["proj_evac"], it["idx"] + 1)

            def turn_wait(turn):
                if turn >= 2:
                    pe.wait_ge(*turn_freed(S, turn - 2))

            for op, x, turn in order:
                if op == "proj":
                    x, k0, k1 = x
                    if x["idx"] >= 2 and not k0:
                        pe.wait_ge(S["proj_evac"], x["idx"] - 1)
                    slot = x["t"] % RING if k0 else split(x["t"])
                    last = blocks(slot, psum[:, x["idx"] % 2, x["tok"]], normed(x["tok"]), range(k0, k1), first=k0,
                                  start=k0 == 0, stop=k1 == CH, **(u_chunk(b) if x["idx"] == 0 else {}))
                    if k1 == CH:
                        last.then_inc(tile_used, 1)
                elif op == "ss":
                    pe.wait_ge(S["proj_evac"], x["idx"] + 1)
                    turn_wait(turn)
                    mm(psum[:, TURN[turn % 2], x["tok"]], ones[:, :], n_sq[:, x["idx"] % 2, x["tok"]], start=True, stop=True)\
                        .then_inc(S["turn_ready"], 1)
                elif op == "rot":
                    if x["norm"]:
                        pe.wait_ge(S["normed"], x["norm_n"])
                    else:
                        pe.wait_ge(S["proj_evac"], x["idx"] + 1)
                    turn_wait(turn)
                    mm(psum[:, TURN[turn % 2], 0:SEQ], rot, latents(x), start=True, stop=True).then_inc(S["turn_ready"], 1)
                elif op == "vtr":
                    pe.wait_ge(S["proj_evac"], x["idx"] + 1)
                    turn_wait(turn)
                    src = item_stage(x)
                    for kt in range(width(x["tok"]) // 128):
                        last = nc.tensor.transpose(psum[:, TURN[turn % 2], kt * 128:(kt + 1) * 128],
                                                   src[:, kt * 128:(kt + 1) * 128], ident)
                    last.then_inc(S["turn_ready"], 1)
                elif op == "S":
                    U, st, n = x["U"], x["set"], x["keys"]
                    for it in st["q"] + st["k"]:
                        if U == st["first_unit"]:
                            item_ready(it)
                    if kind == "b2":
                        if U >= 2:
                            pe.wait_ge(S["biased"], freed[U - 2])
                        biased += len(st["v"])
                        freed[U] = biased
                    elif U >= lag_of(kind):
                        pe.wait_ge(S["exp_done"], exps_through(kind, U - lag_of(kind)))
                    out = scores_of(kind, x)
                    if kind == "ga":
                        q = latents(st["q"][0])[:, x["qt"] * 128 - CTX:x["qt"] * 128 - CTX + 128]
                        last = mm(out, q, k_st[:, st["k"][0]["par"], 0:n], start=True, stop=True)
                    elif kind == "da":
                        for m in range(2):
                            rows = slice(64 * m, 64 * m + 64)
                            q = q_st[rows, st["q"][0]["par"], x["qt"] * 128:x["qt"] * 128 + 128]
                            last = mm(out[:, m, :], q, k_st[rows, st["k"][0]["par"], 0:n], start=True, stop=True)
                    else:
                        rows = slice(64 * x["j"], 64 * x["j"] + 64)
                        for g in range(len(st["v"])):
                            q0 = g * SEQ + x["qt"] * 128
                            last = mm(out[:, g * n:g * n + n], q_st[rows, st["q"][g]["par"], q0:q0 + 128],
                                      k_st[rows, st["k"][g]["par"], g * SEQ:g * SEQ + n], start=True, stop=True)
                    last.then_inc(S["s_ready"], 1)
                elif op == "T":
                    u, a, e = x
                    pe.wait_ge(S["pc_ready"], u["U"] + 1)
                    turn_wait(turn)
                    for n in range(a, e):
                        last = nc.tensor.transpose(psum[:, TURN[turn % 2], (n - a) * 128:(n - a + 1) * 128],
                                                   pcomb[:, u["U"] % 2, n * 128:(n + 1) * 128], ident)
                    last.then_inc(S["turn_ready"], 1)
                elif op == "PV":
                    st, U = x["set"], x["U"]
                    done = x["turns"] + [it["turn"] for it in st["v"]]
                    for bank in range(2):
                        if any(n % 2 == bank for n in done):
                            pe.wait_ge(*turn_freed(S, max(n for n in done if n % 2 == bank)))
                    if U == st["first_unit"] and st["s"]:
                        if kind == "ga":
                            if st["s"] > 1:
                                pe.wait_ge(S["olo_ready"], st["s"] - 1)
                        elif kind == "da":
                            pe.wait_ge(S["o_evac"], st["s"])
                            pe.wait_ge(S["osq_ready"], st["s"])
                        else:
                            pe.wait_ge(S["olo_ready"], st["s"])
                    for n, (g, kt) in enumerate(x["blocks"]):
                        last = mm(psum[:, pv_bank(kind, st["s"]), x["ocol"]:x["ocol"] + 128], v_tile(st["v"][g], kt),
                                  probT[:, U % 2, n * 128:(n + 1) * 128], start=n == 0, stop=n == len(x["blocks"]) - 1)
                    last.then_inc(S["pv_ready"], 1)
                elif op == "early":
                    d, k0, k1 = x
                    if d + k0 == 0:
                        pe.wait_ge(S["proj_evac"], n_items)
                    if kind == "b2":
                        t = b["t_body"] + 30 + d
                        last = blocks(t % RING if k0 else split(t), psum[:, d, 0:SEQ], normed(LAT), range(k0, k1), first=k0,
                                      start=k0 == 0, stop=k1 == CH)
                        if k1 == CH:
                            last.then_inc(tile_used, 1)
                    else:
                        t = b["t_out"] + d
                        pe.wait_ge(S["olo_ready"], k1)
                        tok = b["tok_out"]
                        blocks(t % RING if k0 else split(t), psum[:, out_bank(b, d), tok],
                               lambda k: (o_hi[:, k, tok], o_lo[:, k, tok]), range(k0, k1), first=k0, start=k0 == 0, stop=False)
                elif op == "oss":
                    pe.wait_ge(S["osq_ready"], x["s"] + 1)
                    turn_wait(turn)
                    mm(psum[:, TURN[turn % 2], :], ones[:, :], o_sq[:, :], start=True, stop=True).then_inc(S["turn_ready"], 1)

        def gates(b):
            t0 = b["t_body"] + 30
            branch = lambda k: (y_hi[:, k, :], y_lo[:, k, :])
            def chunk(j, i=0, early=False):
                bank = 4 * (j % 2)
                if not early:
                    pe.wait_ge(merged_ready, i * 4 + (j + 1))
                    for n in range(2):
                        t = t0 + 3 * j + n
                        blocks(split(t, i, 12), psum[:, bank + n, 0:SEQ], normed(LAT), range(CH)).then_inc(tile_used, 1)
                slot = split(t0 + 3 * j + 2, i, 12)
                if early:
                    pe.wait_ge(MS["b2"]["olo_ready"], 6)
                blocks(slot, psum[:, bank + 2, 0:SEQ], branch, range(0, 2))
                blocks(slot, psum[:, bank + 3, 0:SEQ], branch, range(2, 6), first=2).then_inc(tile_used, 1)

            for j in range(4):
                chunk(j, early=j == 0)
            for j in range(4):
                chunk(4 + j)

        for b in BLOCKS:
            pre_norm(b)
            if b["n"]:
                keep_clock(b["tok"], 2)
            if b["kind"] == "ffn":
                ffn_body(b)
            else:
                mixer(b)
                if b["kind"] == "b2":
                    gates(b)
            output(b)
            if b["layer"] is not None:
                keep_clock(b["tok_out"], 2)
        pre_norm({"n": len(BLOCKS), "tok": LAT})

    block_cm.__exit__(None, None, None)


def _tiles(w):
    k, m = w.shape
    return np.ascontiguousarray(w.reshape(k // 128, 128, m // 128, 128).transpose(2, 1, 0, 3).reshape(m // 128, 128, k))


def _columns(v):
    return v.reshape(-1, CH, 128).transpose(2, 0, 1).reshape(128, -1)


def _tables():
    f32 = np.float32
    ident = np.eye(128, dtype=f32)
    rot = np.zeros((128, 128), f32)
    for j in range(64):
        rot[2 * j + 1, 2 * j] = -1.0
        rot[2 * j, 2 * j + 1] = 1.0

    def rope(dim):
        n = dim // 4
        pos = np.arange(SEQ)
        freqs = (f32(THETA) ** (-np.arange(n, dtype=f32) / f32(n))).astype(f32)
        ang = np.concatenate([(pos // GRID_W).astype(f32)[:, None] * freqs, (pos % GRID_W).astype(f32)[:, None] * freqs], 1)
        ang = np.repeat(ang, 2, axis=1)
        ang = np.tile(ang, (1, 128 // dim)).T
        return [np.cos(ang).astype(f32), np.sin(ang).astype(f32)]

    tables = np.concatenate([ident, rot, *rope(DA_QK), *rope(GA_DIM)], axis=1)
    qp, kp = np.arange(SEQ)[:, None], np.arange(SEQ)[None, :]
    delta = qp - kp

    def table(ok):
        return np.where(ok, -delta, f32(MASKED) * 1e3).astype(f32)

    dsa = [table((delta >= 0) & (delta <= w) & (delta % dil == 0)) for w, dil in DSA_GROUPS]
    moba = table(delta >= 0)
    parts = []
    for qt in range(2):
        parts += [d[qt * 128:qt * 128 + 128, 0:128 * (qt + 1)] for d in dsa]
    for qt in range(2):
        parts.append(moba[qt * 128:qt * 128 + 128, 0:128 * (qt + 1)])
    dist = np.concatenate(parts, axis=1)

    def slopes(n):
        return (f32(2.0) ** (f32(-8.0) * np.arange(1, n + 1, dtype=f32) / f32(n))).astype(f32)
    sl = np.concatenate([slopes(len(DSA_GROUPS) * DSA_HPG), slopes(MOBA_HEADS)])
    return np.ascontiguousarray(tables), np.ascontiguousarray(dist), np.broadcast_to(sl, (128, 20))


def kernel(**inputs):
    import concourse.bacc as bacc
    from concourse.bass_utils import run_bass_kernel_spmd

    I = {k: np.asarray(v) for k, v in inputs.items()}
    tables, dist, slopes = _tables()
    col = np.concatenate([
        _columns(I["norm_g"]),
        _columns(np.stack([I["norm_ffn1_2"][0], I["norm_mix_2"][0], I["norm_ffn2_2"][0], I["norm_final_2"]])),
        I["da_subln"].reshape(128, 1), I["ga_q_norm"].reshape(128, 1), I["ga_k_norm"].reshape(128, 1), slopes,
        np.broadcast_to(I["da_lambda"].reshape(1, -1), (128, 4 * DA_QK)),
        I["ada_b"].reshape(2 * MODS, 128).T], axis=1)
    X = {"columns": col, "tables": tables, "dist": dist}
    X["hT"] = np.concatenate([I["ctx"][0], I["x"][0]]).reshape(TOK, CH, 128).transpose(2, 1, 0)
    X["cond"] = np.broadcast_to(np.stack([I["c"][0], I["c_ctx"]]), (128, 2, D))
    X["ada_w"] = I["ada_w"].reshape(2, D, MODS, 128).transpose(0, 2, 3, 1).reshape(2 * MODS, 128, D)
    win = [I["ffn_w_in"][l, p] for l in range(2) for p in range(2)]
    win += [np.concatenate([I[f"ffn{n}_gate_2"][0], I[f"ffn{n}_up_2"][0]], axis=1) for n in (1, 2)]
    wout = [I["ffn_w_out"][l, p] for l in range(2) for p in range(2)] + [I["ffn1_down_2"][0], I["ffn2_down_2"][0]]
    for f in range(6):
        X[f"ffn_in{f}"] = _tiles(win[f]).reshape(2, FCH, 128, TW).transpose(1, 0, 2, 3).reshape(2 * FCH, 128, TW)
        X[f"ffn_out{f}"] = _tiles(wout[f])
    X["da_in"] = _tiles(I["da_w_in"][0]).reshape(3, DA_HEADS, 128, TW).transpose(1, 0, 2, 3).reshape(3 * DA_HEADS, 128, TW)
    X["da_out"] = _tiles(I["da_w_out"][0])
    ga = _tiles(I["ga_w_in"][0])
    per = GA_HEADS // GA_KV
    X["ga_in"] = ga[[n for g in range(GA_KV) for n in (GA_HEADS + g, GA_HEADS + GA_KV + g, *range(per * g, per * g + per))]]
    X["ga_out"] = _tiles(I["ga_w_out"][0])
    w2 = _tiles(I["w_in_2"][0])
    X["b2_qkv"] = w2[[6 * w + 2 * g + s for s in range(2) for g in range(3) for w in range(3)]
                     + [18 + 4 * w + c for c in range(4) for w in range(3)]]
    X["b2_gate"] = w2[30:46].reshape(2, CH, 128, TW).transpose(1, 0, 2, 3)
    X["b2_up"] = np.concatenate([_tiles(I["w_up_a_2"][0]), _tiles(I["w_up_b_2"][0])], axis=2)
    X["b2_out"] = _tiles(I["w_out_2"][0])

    nc = bacc.Bacc("TRN2", target_bir_lowering=False, num_devices=1)
    arrays, A = {}, {}
    for name, a in X.items():
        arrays[f"in_{name}"] = np.ascontiguousarray(a)
        A[name] = nc.dram_tensor(f"in_{name}", list(a.shape), mybir.dt.float32, kind="ExternalInput").ap()
    A["out"] = nc.dram_tensor("out", [128, CH, SEQ], mybir.dt.float32, kind="ExternalOutput").ap()
    build(nc, A)
    r = run_bass_kernel_spmd(nc, [arrays], core_ids=[0])
    got = r.results[0]["out"]
    return np.ascontiguousarray(got.transpose(2, 1, 0).reshape(1, SEQ, D))
```
